# Optimizing a Trainium2 kernel written in Bass

```python
import functools
import jax, jax.numpy as jnp
from jax import lax
import numpy as np

D_MODEL = 1024
BATCH = 1
SEQ = 1024
DEPTH = 1
DEC_BATCH = 8
DEC_SEQ = 1
PAST_LEN = 8192
PAGE_SIZE = 128

MIX_WIDTH = D_MODEL
HEAD_DIM = 64
RWKV_WIDTH = MIX_WIDTH // 2
RWKV_HEADS = RWKV_WIDTH // HEAD_DIM
RWKV_DECAY_LORA = 64
RWKV_A_LORA = 64
RWKV_GATE_LORA = 128
RWKV_GN_EPS = 64e-5
SWA_WIDTH = MIX_WIDTH - RWKV_WIDTH
SWA_HEADS = SWA_WIDTH // HEAD_DIM
SWA_KV_HEADS = 2
SWA_GROUP = SWA_HEADS // SWA_KV_HEADS
WINDOW = 128
ROPE_THETA = 10000.0
ATTN_SCALE = HEAD_DIM ** -0.5
D_FF = 2816
CONV_WIDTH = 3
NORM_EPS = 1e-6
MASK_VALUE = -1e30

RWKV_SIZES = (RWKV_WIDTH, RWKV_WIDTH, RWKV_WIDTH, RWKV_DECAY_LORA, RWKV_A_LORA, RWKV_GATE_LORA)
RWKV_COLS = sum(RWKV_SIZES)
SWA_SIZES = (SWA_WIDTH, SWA_KV_HEADS * HEAD_DIM, SWA_KV_HEADS * HEAD_DIM)
PROJ_COLS = RWKV_COLS + sum(SWA_SIZES)

kernel_name = 'hymba_rwkv7_swa_sink_convffn_step'

def _offsets(sizes):
    return [int(s) for s in np.cumsum(sizes)[:-1]]

def _rmsnorm(x, g):
    xf = x.astype(jnp.float32)
    y = xf * lax.rsqrt(jnp.mean(xf * xf, axis=-1, keepdims=True) + NORM_EPS)
    return (y * g.astype(jnp.float32)).astype(x.dtype)

def _rope(x, pos):
    half = HEAD_DIM // 2
    inv = ROPE_THETA ** (-jnp.arange(half, dtype=jnp.float32) / half)
    ang = pos.astype(jnp.float32)[:, None] * inv[None, :]
    cos = jnp.cos(ang)[None, :, None, :]
    sin = jnp.sin(ang)[None, :, None, :]
    x1 = x[..., :half].astype(jnp.float32)
    x2 = x[..., half:].astype(jnp.float32)
    return jnp.concatenate([x1 * cos - x2 * sin, x2 * cos + x1 * sin], axis=-1).astype(x.dtype)

def _wkv_scan(r, w, k, v, kk, a, S0):
    def step(S, inp):
        r_t, w_t, k_t, v_t, kk_t, a_t = inp
        sa = jnp.einsum('bhvk,bhk->bhv', S, -kk_t)
        S = (S * w_t[:, :, None, :] + sa[..., None] * (kk_t * a_t)[:, :, None, :]
             + v_t[..., None] * k_t[:, :, None, :])
        return S, jnp.einsum('bhvk,bhk->bhv', S, r_t)
    xs = tuple(jnp.swapaxes(t, 0, 1) for t in (r, w, k, v, kk, a))
    S_T, o = lax.scan(step, S0, xs)
    return S_T, jnp.swapaxes(o, 0, 1)

def _rwkv7(p, prev_row, S0, P):
    B, T, _ = p.shape
    f32 = jnp.float32
    prev = jnp.concatenate([prev_row[:, None, :].astype(p.dtype), p[:, :-1]], axis=1)
    xm = p + (prev - p) * P['rwkv_mu']
    r, k, v, wd, ad, gd = jnp.split(xm, _offsets(RWKV_SIZES), axis=-1)
    w_log = -jax.nn.softplus(-(P['rwkv_w0'] + jnp.tanh(wd) @ P['rwkv_w_up']).astype(f32)) - 0.5
    decay = jnp.exp(-jnp.exp(w_log))
    a = jax.nn.sigmoid((P['rwkv_a0'] + ad @ P['rwkv_a_up']).astype(f32))
    g = (jax.nn.sigmoid(gd) @ P['rwkv_g_up']).astype(f32)
    heads = lambda t: t.reshape(B, T, RWKV_HEADS, HEAD_DIM)
    kf = k.astype(f32)
    kk = heads(kf * P['rwkv_k_k'].astype(f32))
    kk = kk / jnp.maximum(jnp.sqrt(jnp.sum(kk * kk, axis=-1, keepdims=True)), 1e-12)
    kf = heads(kf * (1.0 + (a - 1.0) * P['rwkv_k_a'].astype(f32)))
    rf, vf, a, decay = heads(r.astype(f32)), heads(v.astype(f32)), heads(a), heads(decay)
    S_T, o = _wkv_scan(rf, decay, kf, vf, kk, a, S0.astype(f32))
    mu = jnp.mean(o, axis=-1, keepdims=True)
    var = jnp.mean(jnp.square(o - mu), axis=-1, keepdims=True)
    o = ((o - mu) * lax.rsqrt(var + RWKV_GN_EPS)).reshape(B, T, RWKV_WIDTH)
    o = o * P['rwkv_ln_w'].astype(f32) + P['rwkv_ln_b'].astype(f32)
    bonus = (jnp.sum(rf * kf * P['rwkv_r_k'].astype(f32), axis=-1, keepdims=True) * vf).reshape(B, T, RWKV_WIDTH)
    out = ((o + bonus) * g).astype(p.dtype)
    return out, S_T.astype(S0.dtype), p[:, -1]

def _sink_attention(q, k, v, qpos, kpos, sinks):
    s = jnp.einsum('...qkgd,...skd->...kgqs', q, k, preferred_element_type=jnp.float32) * ATTN_SCALE
    diff = qpos[..., :, None] - kpos[..., None, :]
    valid = (diff >= 0) & (diff < WINDOW) & (kpos[..., None, :] >= 0)
    s = jnp.where(valid[..., None, None, :, :], s, MASK_VALUE)
    sink = sinks.astype(jnp.float32).reshape(SWA_KV_HEADS, SWA_GROUP)[:, :, None, None]
    m = jnp.maximum(jnp.max(s, axis=-1, keepdims=True), sink)
    e = jnp.exp(s - m)
    prob = e / (jnp.sum(e, axis=-1, keepdims=True) + jnp.exp(sink - m))
    return jnp.einsum('...kgqs,...skd->...qkgd', prob.astype(v.dtype), v)

def _swa_prompt(q, k, v, sinks):
    B, T, _, _ = q.shape
    nb = T // WINDOW
    qb = q.reshape(B, nb, WINDOW, SWA_KV_HEADS, SWA_GROUP, HEAD_DIM)
    kb = k.reshape(B, nb, WINDOW, SWA_KV_HEADS, HEAD_DIM)
    vb = v.reshape(B, nb, WINDOW, SWA_KV_HEADS, HEAD_DIM)
    pad = ((0, 0), (1, 0), (0, 0), (0, 0), (0, 0))
    kc = jnp.concatenate([jnp.pad(kb[:, :-1], pad), kb], axis=2)
    vc = jnp.concatenate([jnp.pad(vb[:, :-1], pad), vb], axis=2)
    qpos = jnp.arange(T, dtype=jnp.int32).reshape(nb, WINDOW)
    kpos = qpos[:, :1] - WINDOW + jnp.arange(2 * WINDOW, dtype=jnp.int32)[None, :]
    o = _sink_attention(qb, kc, vc, qpos, kpos, sinks)
    keep = min(WINDOW, T)
    return o.reshape(B, T, SWA_WIDTH), k[:, -keep:], v[:, -keep:]

def _swa_sample(q, k, v, sinks, cache_k, cache_v):
    B, T, _, _ = q.shape
    L = cache_k.shape[1]
    kc = jnp.concatenate([cache_k.astype(k.dtype), k], axis=1)
    vc = jnp.concatenate([cache_v.astype(v.dtype), v], axis=1)
    kpos = PAST_LEN - L + jnp.arange(L + T, dtype=jnp.int32)
    qpos = PAST_LEN + jnp.arange(T, dtype=jnp.int32)
    o = _sink_attention(q.reshape(B, T, SWA_KV_HEADS, SWA_GROUP, HEAD_DIM), kc, vc, qpos, kpos, sinks)
    return o.reshape(B, T, SWA_WIDTH), kc[:, -L:], vc[:, -L:]

def _conv_ffn(h, conv_prev, P):
    T = h.shape[1]
    u = h @ P['ffn_w_up']
    ext = jnp.concatenate([conv_prev.astype(u.dtype), u], axis=1)
    z = P['ffn_conv_b']
    for j in range(CONV_WIDTH):
        z = z + ext[:, j:j + T] * P['ffn_conv_w'][j]
    za, zb = jnp.split(z, 2, axis=-1)
    return (jax.nn.silu(za) * zb) @ P['ffn_w_down'], ext[:, T:]

def _layer(x, c, pos, wkv0, shift0, conv0, attend, P):
    B, T, _ = x.shape
    mod = jax.nn.silu(c) @ P['w_ada'] + P['b_ada']
    sh1, sc1, g1, sh2, sc2, g2 = jnp.split(mod[:, None, :], 6, axis=-1)
    h = _rmsnorm(x, P['norm_pre_mix']) * (1.0 + sc1) + sh1
    proj = h @ P['w_in']
    p_rwkv, q, k, v = jnp.split(proj, _offsets((RWKV_COLS,) + SWA_SIZES), axis=-1)
    y_rwkv, wkv_T, shift_T = _rwkv7(p_rwkv, shift0, wkv0, P)
    q = _rope(q.reshape(B, T, SWA_HEADS, HEAD_DIM), pos)
    k = _rope(k.reshape(B, T, SWA_KV_HEADS, HEAD_DIM), pos)
    v = v.reshape(B, T, SWA_KV_HEADS, HEAD_DIM)
    y_swa, kbuf, vbuf = attend(q, k, v, P['swa_sinks'])
    mix = jnp.concatenate([y_rwkv, y_swa], axis=-1) @ P['w_out']
    x = x + g1 * _rmsnorm(mix, P['norm_post_mix'])
    h2 = _rmsnorm(x, P['norm_pre_ffn']) * (1.0 + sc2) + sh2
    ff, conv_T = _conv_ffn(h2, conv0, P)
    x = x + g2 * _rmsnorm(ff, P['norm_post_ffn'])
    return x, (wkv_T, shift_T, kbuf, vbuf, conv_T)

def setup_inputs(seed: int = 0) -> dict:
    key = jax.random.key(seed)
    ks = iter(jax.random.split(key, 48))
    L = DEPTH
    win = min(WINDOW, PAST_LEN)

    def nrm(shape, scale=1.0):
        return jax.random.normal(next(ks), shape, jnp.float32) * scale

    def unif(shape, lo, hi):
        return jax.random.uniform(next(ks), shape, jnp.float32, lo, hi)

    return {
        'x_prompt': nrm((BATCH, SEQ, D_MODEL)),
        'x_sample': nrm((DEC_BATCH, DEC_SEQ, D_MODEL)),
        'state_rwkv_wkv': nrm((L, DEC_BATCH, RWKV_HEADS, HEAD_DIM, HEAD_DIM), 0.3),
        'state_rwkv_shift': nrm((L, DEC_BATCH, RWKV_COLS)),
        'cache_swa_k': nrm((L, DEC_BATCH, win, SWA_KV_HEADS, HEAD_DIM)),
        'cache_swa_v': nrm((L, DEC_BATCH, win, SWA_KV_HEADS, HEAD_DIM)),
        'state_ffn_conv': nrm((L, DEC_BATCH, CONV_WIDTH - 1, 2 * D_FF)),
        'c_prompt': nrm((BATCH, D_MODEL)),
        'c_sample': nrm((DEC_BATCH, D_MODEL)),
        'w_ada': nrm((L, D_MODEL, 6 * D_MODEL), 0.5 * D_MODEL ** -0.5),
        'b_ada': nrm((L, 6 * D_MODEL), 0.01),
        'norm_pre_mix': 1.0 + nrm((L, D_MODEL), 0.05),
        'norm_post_mix': 1.0 + nrm((L, D_MODEL), 0.05),
        'norm_pre_ffn': 1.0 + nrm((L, D_MODEL), 0.05),
        'norm_post_ffn': 1.0 + nrm((L, D_MODEL), 0.05),
        'w_in': nrm((L, D_MODEL, PROJ_COLS), D_MODEL ** -0.5),
        'rwkv_mu': unif((L, RWKV_COLS), 0.0, 1.0),
        'rwkv_w0': unif((L, RWKV_WIDTH), -5.0, -1.0),
        'rwkv_w_up': nrm((L, RWKV_DECAY_LORA, RWKV_WIDTH), RWKV_DECAY_LORA ** -0.5),
        'rwkv_a0': nrm((L, RWKV_WIDTH), 0.1),
        'rwkv_a_up': nrm((L, RWKV_A_LORA, RWKV_WIDTH), RWKV_A_LORA ** -0.5),
        'rwkv_g_up': nrm((L, RWKV_GATE_LORA, RWKV_WIDTH), RWKV_GATE_LORA ** -0.5),
        'rwkv_k_k': 0.85 + nrm((L, RWKV_WIDTH), 0.05),
        'rwkv_k_a': 1.0 + nrm((L, RWKV_WIDTH), 0.05),
        'rwkv_r_k': nrm((L, RWKV_HEADS, HEAD_DIM), 0.1),
        'rwkv_ln_w': 1.0 + nrm((L, RWKV_WIDTH), 0.05),
        'rwkv_ln_b': nrm((L, RWKV_WIDTH), 0.01),
        'swa_sinks': nrm((L, SWA_HEADS), 0.5),
        'w_out': nrm((L, MIX_WIDTH, D_MODEL), MIX_WIDTH ** -0.5),
        'ffn_w_up': nrm((L, D_MODEL, 2 * D_FF), D_MODEL ** -0.5),
        'ffn_conv_w': nrm((L, CONV_WIDTH, 2 * D_FF), CONV_WIDTH ** -0.5),
        'ffn_conv_b': nrm((L, 2 * D_FF), 0.01),
        'ffn_w_down': nrm((L, D_FF, D_MODEL), D_FF ** -0.5),
    }

def reference(x_prompt, x_sample, state_rwkv_wkv, state_rwkv_shift, cache_swa_k, cache_swa_v,
              state_ffn_conv, c_prompt, c_sample, w_ada, b_ada, norm_pre_mix, norm_post_mix,
              norm_pre_ffn, norm_post_ffn, w_in, rwkv_mu, rwkv_w0, rwkv_w_up, rwkv_a0, rwkv_a_up,
              rwkv_g_up, rwkv_k_k, rwkv_k_a, rwkv_r_k, rwkv_ln_w, rwkv_ln_b, swa_sinks, w_out,
              ffn_w_up, ffn_conv_w, ffn_conv_b, ffn_w_down):
    B, T = x_prompt.shape[0], x_prompt.shape[1]
    Td = x_sample.shape[1]
    dt = x_prompt.dtype
    pos_p = jnp.arange(T, dtype=jnp.int32)
    pos_s = PAST_LEN + jnp.arange(Td, dtype=jnp.int32)
    yp, ys = x_prompt, x_sample
    new_p, new_s = [], []
    for l in range(DEPTH):
        P = dict(w_ada=w_ada[l], b_ada=b_ada[l], norm_pre_mix=norm_pre_mix[l],
                 norm_post_mix=norm_post_mix[l], norm_pre_ffn=norm_pre_ffn[l],
                 norm_post_ffn=norm_post_ffn[l], w_in=w_in[l], rwkv_mu=rwkv_mu[l],
                 rwkv_w0=rwkv_w0[l], rwkv_w_up=rwkv_w_up[l], rwkv_a0=rwkv_a0[l],
                 rwkv_a_up=rwkv_a_up[l], rwkv_g_up=rwkv_g_up[l], rwkv_k_k=rwkv_k_k[l],
                 rwkv_k_a=rwkv_k_a[l], rwkv_r_k=rwkv_r_k[l], rwkv_ln_w=rwkv_ln_w[l],
                 rwkv_ln_b=rwkv_ln_b[l], swa_sinks=swa_sinks[l], w_out=w_out[l],
                 ffn_w_up=ffn_w_up[l], ffn_conv_w=ffn_conv_w[l], ffn_conv_b=ffn_conv_b[l],
                 ffn_w_down=ffn_w_down[l])
        yp, st_p = _layer(yp, c_prompt, pos_p,
                          jnp.zeros((B, RWKV_HEADS, HEAD_DIM, HEAD_DIM), dt),
                          jnp.zeros((B, RWKV_COLS), dt),
                          jnp.zeros((B, CONV_WIDTH - 1, 2 * D_FF), dt),
                          _swa_prompt, P)
        ys, st_s = _layer(ys, c_sample, pos_s, state_rwkv_wkv[l], state_rwkv_shift[l],
                          state_ffn_conv[l],
                          functools.partial(_swa_sample, cache_k=cache_swa_k[l], cache_v=cache_swa_v[l]),
                          P)
        new_p.append(st_p)
        new_s.append(st_s)
    wkv_p, shift_p, k_p, v_p, conv_p = [jnp.stack(a) for a in zip(*new_p)]
    wkv_s, shift_s, k_s, v_s, conv_s = [jnp.stack(a) for a in zip(*new_s)]
    return (yp, ys, wkv_p, shift_p, k_p, v_p, conv_p, wkv_s, shift_s, k_s, v_s, conv_s)


_drawn_inputs = setup_inputs


def setup_inputs(seed=0):
    import zlib

    import numpy as np

    out = dict(_drawn_inputs(seed))
    spreads = {}
    factors = {'norm_post_mix': 3.951,
     'norm_post_ffn': 3.874,
     'rwkv_ln_w': 4.051,
     'rwkv_ln_b': 27.116,
     'swa_sinks': 8.0,
     'ffn_conv_b': 8.0}
    for name, (base, spread) in spreads.items():
        noise = np.random.default_rng([zlib.crc32(name.encode()), seed]).standard_normal(out[name].shape)
        drawn = base * np.exp(spread * noise) if base else spread * noise
        out[name] = __import__('jax').numpy.asarray(drawn.astype(out[name].dtype))
    for name, factor in factors.items():
        out[name] = (out[name] * factor).astype(out[name].dtype)
    return out
```

```python
from contextlib import ExitStack

import numpy as np
import concourse.bass as bass
from concourse import mybir

F32 = mybir.dt.float32
F32R = mybir.dt.float32r
U32 = mybir.dt.uint32
ALU = mybir.AluOpType
ACT = mybir.ActivationFunctionType
AX = mybir.AxisListType

P = 128
D = 1024
KD = D // P
T = 1024
NS = 8
N = T + NS
SL = N // 3
HD = 64
RW = 512
NJ = RW // P
RC = 14
PC = 20
FF = 2816
FC = FF // P
CW = 3
C = 64
NCH = T // C
NT = T // P
PW = N + 2
PO = 2
KAPPA = float(np.exp(np.float32(-0.5)))
NORM_EPS = 1e-6
GN_EPS = 64e-5
MASKED = -1e30
SCALE = HD ** -0.5
LEVELS = (2, 4, 8, 16, 32)

CONSTS = [("ident", P), ("swap", P), ("headsum", P), ("ones", P), ("cumsum", 2 * P),
          ("after", C), ("upto", C), ("eye", C), ("window", 2 * P)]
PARAMS = [("b_ada", 48), ("norm_pre_mix", 8), ("norm_post_mix", 8), ("norm_pre_ffn", 8),
          ("norm_post_ffn", 8), ("rwkv_mu", RC), ("rwkv_w0", 4), ("rwkv_a0", 4), ("rwkv_k_k", 4),
          ("rwkv_k_a", 4), ("rwkv_r_k", 4), ("rwkv_ln_w", 4), ("rwkv_ln_b", 4),
          ("ffn_conv_w", CW * 2 * FC), ("ffn_conv_b", 2 * FC), ("sinks", 8), ("sink_rows", 1)]


def columns(table):
    at, n = {}, 0
    for name, width in table:
        at[name] = (n, n + width)
        n += width
    return at, n


CONST_AT, CONST_N = columns(CONSTS)
PARAM_AT, PARAM_N = columns(PARAMS)


def build_program(nc, io):
    ctx = ExitStack()
    with ctx:
        base = (nc.sbuf_base + 63) // 64 * 64
        end = nc.sbuf_base + nc.sbuf_bytes_remaining

        def sb(name, shape, dt, off):
            size = int(np.prod(shape[1:])) * 4
            assert base + off + size <= end, (name, off, size, end - base)
            return nc.alloc_sbuf_tensor_at(name, shape, dt, offset=base + off)

        def place(names, at):
            out = []
            for name, shape, dt in names:
                out.append(sb(name, shape, dt, at))
                at += (int(np.prod(shape[1:])) * 4 + 31) // 32 * 32
            return out, at

        def sem(name):
            return ctx.enter_context(nc.semaphore(name))

        (cst, lvl, par, mod, cT, cTs, shift_st, tail_shift, conv_add, lora, g_up, gs1, gs2, gate, Pc, eps,
         sc_mod), at = place([
            ("cst", [P, CONST_N], F32), ("lvl", [P, 2 * (len(LEVELS) + 1), C], U32), ("par", [P, PARAM_N], F32),
            ("mod", [P, 48, 9], F32), ("cT", [P, KD, 9], F32), ("cTs", [P, KD, 9], F32),
            ("shift_st", [P, RC, NS], F32), ("tail_shift", [P, RC, NS + 1], F32),
            ("conv_add", [P, 2 * FC, NS], F32), ("lora", [P, RW], F32), ("g_up", [P, RW], F32),
            ("gs1", [P, KD, 9], F32), ("gs2", [P, KD, 9], F32), ("gate", [P, 2, KD, 9], F32),
            ("Pc", [P, NCH], F32), ("eps", [P, 4], F32),
            ("sc_mod", [P, 4], F32)], 0)
        PT0 = (at + 63) // 64 * 64
        (PT,), REM = place([("PT", [P, PC, PW], F32)], PT0)
        (xT,), _ = place([("xT", [P, KD, N], F32)], PT0 + 12 * PW * 4)
        (XS,), RING = place([("XS", [P, KD, 2, N], F32R)], REM)
        (raw, spl), TMP = place([("raw", [P, 4, D], F32), ("spl", [P, 2, 2, D], F32R)], RING)
        (rs, tmpA), _ = place([("rs", [P, N], F32), ("tmpA", [P, N], F32)], TMP)

        (rope, S4, PR, VA, Kf, Vf, KTs, kvrow, sS, sP, sPT, mx, nm, sk, den, rd), at = place([
            ("rope", [P, 2, N], F32), ("S4", [P, 2, 4, 2 * P], F32), ("PR", [P, 2, 4, 2, P], F32),
            ("VA", [P, NT, P], F32), ("Kf", [P, NS, P], F32), ("Vf", [P, NS, P], F32), ("KTs", [P, NS, P], F32),
            ("kvrow", [NS, 2, P], F32), ("sS", [P, 64], F32), ("sP", [64, P], F32), ("sPT", [P, 64], F32),
            ("mx", [P, 2, 4], F32), ("nm", [P, 2, 4], F32), ("sk", [P, 2, 4], F32), ("den", [P, 2, 4], F32),
            ("rd", [P, 2, 4], F32)], REM)
        assert at <= RING, (at, RING)
        (dif,), _ = place([("dif", [P, 2, N], F32)], TMP)
        UN = [P, 2 * NT, C]
        (Aff, Ein, St, TT, MT, MkT, NbT, NkT, T0), at = place([
            ("Aff", [P, NJ, NCH, C], F32), ("Ein", [P, NJ, NCH, C], F32), ("St", [P, 4, NJ, C], F32),
            ("TT", UN, F32), ("MT", UN, F32), ("MkT", UN, F32), ("NbT", UN, F32), ("NkT", UN, F32),
            ("T0", UN, F32)], REM)
        FB = at
        (aTm, bTm, kTm, vTm, F0, F1, F2, F3, F4, F5, F6, SMP), at = place([
            ("aTm", [P, NT, P], F32), ("bTm", [P, NT, P], F32), ("kTm", [P, NT, P], F32), ("vTm", [P, NT, P], F32),
            ("F0", [P, N], F32), ("F1", [P, N], F32), ("F2", [P, N], F32), ("F3", [P, N], F32), ("F4", [P, N], F32),
            ("F5", [P, N], F32), ("F6", [P, N], F32), ("SMP", [P, NJ, 6, NS], F32)], at)
        (sWKV, sTmp, V6, V32, Osm, sa, SM48, OR), at2 = place([
            ("sWKV", [P, 32, HD], F32), ("sTmp", [P, 32, HD], F32), ("V6", [P, 6, HD], F32), ("V32", [P, 32], F32),
            ("Osm", [P, 32], F32), ("sa", [P, 32], F32), ("SM48", [48, RW], F32), ("OR", [NS, RW], F32)], FB)
        assert at2 <= at - NJ * 6 * NS * 4
        (MO, X2, sqs, sq2, rsC), at2 = place([
            ("MO", [P, KD, N], F32), ("X2", [P, KD, N], F32), ("sqs", [P, N], F32), ("sq2", [P, 2, N], F32),
            ("rsC", [P, N], F32)], PT0)
        assert at2 <= REM
        (acc, U, Z, G, act2, ftail, conv_st, sqF), at2 = place([
            ("acc", [P, KD, N], F32), ("U", [P, 2, N], F32), ("Z", [P, 2, N], F32), ("G", [P, N], F32),
            ("act2", [P, 2, 2, N], F32R), ("ftail", [P, 2 * FC, NS + 2], F32), ("conv_st", [P, 2, 2 * FC, NS], F32),
            ("sqF", [P, N], F32)], PT0)
        assert at2 <= REM
        (raw3, spl3), at2 = place([("raw3", [P, 3, D], F32), ("spl3", [P, 3, 2, D], F32R)], RING)
        (X1,), _ = place([("X1", [P, KD, N], F32)], REM)
        x1_dram = nc.dram_tensor("x1_dram", [P, KD, N], F32).ap()
        scr_a = nc.dram_tensor("scr_a", [6, NS, RW], F32).ap()
        scr_o = nc.dram_tensor("scr_o", [NS, 8, 2, 32], F32).ap()

        def chunk_at(c):
            return c % 2 * NT + c // 2

        def unit(f):
            return f[:, 0:T].rearrange("p (u c) -> p u c", c=C)

        Tm, W1, Gm, Hm, Ym = T0, unit(F0), unit(F2), unit(F5), unit(F6)
        SGt = T0[:].rearrange("p u c -> p (u c)").rearrange("p (n c) -> p n c", c=P)

        ps = ctx.enter_context(nc.psum_tensor("ps", [P, 8, 512], F32))

        def const(name):
            a, b = CONST_AT[name]
            return cst[:, a:b]

        def param(name, n):
            return par[:, PARAM_AT[name][0] + n:PARAM_AT[name][0] + n + 1]

        def params(name):
            return par[:, PARAM_AT[name][0]:PARAM_AT[name][1]]

        def slices(ap):
            return ap.rearrange("p (s t) -> p s t", s=3)

        def three(bank_set):
            return ps[:, 3 * bank_set:3 * bank_set + 3, 0:SL]

        def col(first, n):
            return par[:, bass.ds(n + first, 1)]

        def at_chunk(t, n):
            return t[:, bass.ds(n, 1), :].rearrange("p o c -> p (o c)")

        def one(ap, index):
            return ap[bass.ds(index, 1)].rearrange("o p n -> (o p) n")

        sqA = [PT[:, 0, 0:N], PT[:, 1, 0:N]]
        hA = [PT[:, 2, 0:N], PT[:, 3, 0:N]]

        ones, ident, bones = const("ones"), const("ident"), const("headsum")

        dve_step, act_step = sem("dve_step"), sem("act_step")
        consts_in, x_in, small_out = sem("consts_in"), sem("x_in"), sem("small_out")
        raw_in = [sem(f"raw_in{i}") for i in range(4)]
        zeros_set, silu_c, ada_used, mod_ready = sem("zeros_set"), sem("silu_c"), sem("ada_used"), sem("mod_ready")
        sq_ready, sumsq_ready, std_ready = sem("sq_ready"), sem("sumsq_ready"), sem("std_ready")
        sq_used = sem("sq_used")
        h_ready, h_hi, h_lo = sem("h_ready"), sem("h_hi"), sem("h_lo")
        w_hi, w_lo = sem("w_hi"), sem("w_lo")
        proj_ready, proj_out = sem("proj_ready"), sem("proj_out")
        S = {}
        STEPS = ["M", "MT", "MkT", "NbT", "NkT"]
        for n in range(len(LEVELS)):
            STEPS += [f"Y{n}"] + ([f"Z{n}"] if n < len(LEVELS) - 1 else []) + [f"ZT{n}"]
        STEPS += ["W1", "G", "H", "E", "A", "RG", "O"]
        ON_ACT = {f"Y{n}" for n in range(len(LEVELS))} | {"W1", "G", "E", "O", "H"}
        dve_steps = [x for x in STEPS if x not in ON_ACT]
        act_steps = [x for x in STEPS if x in ON_ACT]

        def evacuated(name, pair, half):
            order = act_steps if name in ON_ACT else dve_steps
            return s("unit_act" if name in ON_ACT else "unit_dve"), (pair * len(order) + order.index(name)) * 2 + half + 1

        def computed(name, pair, half):
            return s("unit_mm"), (pair * len(STEPS) + STEPS.index(name)) * 2 + half + 1

        def s(name):
            if name not in S:
                S[name] = sem(name)
            return S[name]

        JOBS = 2 * FC + KD * (FC // 2)
        block = ctx.enter_context(nc.Block())
        ADA_A, ADA_B = 16, 32

        @block.sync
        def _(sp):
            def dma(dst, src, signal):
                return nc.sync.dma_start(dst, src).then_inc(signal, 16)

            dma(cT[:], io["cT"], s("c_in"))
            for n in range(4):
                dma(raw[:, n], io["ada"][n], raw_in[n])
            for i, (dst, src) in enumerate([(cst, "consts"), (lvl, "levels"), (par, "params"), (shift_st, "shift_st"),
                                            (lora, "lora"), (g_up, "g_up")]):
                dma(dst[:], io[src], consts_in)
            dma(xT[:], io["xT"], x_in)

            def load(tile, slot, used, count):
                sp.wait_ge(used, count)
                dma(raw[:, slot], tile, raw_in[slot])

            def tiles(name, first, count, used):
                with sp.Fori(0, (count - first) // 4) as i:
                    for j in range(4):
                        load(one(io[name], i * 4 + (first + j)), j, used, i * 4 + (first - 3 + j))

            tiles("ada", 4, ADA_A, ada_used)
            for n in range(4):
                load(io["w_in"][n], n, ada_used, ADA_A - 3 + n)
            tiles("w_in", 4, PC, w_lo)
            for n in range(4):
                load(io["ada"][ADA_A + n], n, w_lo, PC - 3 + n)
            with sp.Fori(0, (ADA_B - 4) // 4) as i:
                for j in range(4):
                    load(one(io["ada"], i * 4 + (ADA_A + 4 + j)), j, ada_used, i * 4 + (ADA_A + 1 + j))

            sp.wait_ge(s("shift_saved"), 1)
            dma(io["o_shift"], tail_shift[:], small_out)
            dma(io["o_ks"][:, 0:P - 1, :], io["cache_k"][:, 1:P, :], s("cache_out"))
            dma(io["o_vs"][:, 0:P - 1, :], io["cache_v"][:, 1:P, :], s("cache_out"))
            sp.wait_ge(s("kvrow_ready"), 1)
            dma(io["o_ks"][:, P - 1, :], kvrow[:, 0, :], s("cache_out"))
            dma(io["o_vs"][:, P - 1, :], kvrow[:, 1, :], s("cache_out"))
            dma(io["o_kvp"], PT[:, 18:20, PW - NS - P:PW - NS], small_out)
            sp.wait_ge(s("cache_out"), 64)
            dma(Kf[:], io["o_ks"].rearrange("b s d -> s b d"), s("cache_in"))
            dma(Vf[:], io["o_vs"].rearrange("b s d -> s b d"), s("cache_in"))
            sp.wait_ge(s("sm48_ready"), 1)
            dma(sWKV[:], io["wkv"].rearrange("p (v k) -> p v k", k=HD), s("wkv_in"))
            dma(scr_a.rearrange("q b c -> (q b) c"), SM48[:], s("scr_out"))
            sp.wait_ge(s("scr_out"), 16)
            for vh in range(2):
                dma(V6[64 * vh:64 * vh + 64], scr_a.rearrange("q b (h k) -> (b h) q k", k=HD), s("wkv_in"))
                dma(V32[64 * vh:64 * vh + 64], scr_a[5].rearrange("b (h u v) -> (b h) u v", u=2, v=32)[:, vh], s("wkv_in"))
            sp.wait_ge(s("sample_o"), 1)
            dma(io["o_wkvs"], sWKV[:], s("states_out"))
            for vh in range(2):
                dma(scr_o.rearrange("b h u v -> (b h) u v")[:, vh], Osm[64 * vh:64 * vh + 64], s("scro_out"))
            sp.wait_ge(s("scro_out"), 32)
            dma(OR[:], scr_o.rearrange("b h u v -> b (h u v)"), s("or_in"))
            sp.wait_ge(s("state_ready"), NCH)
            dma(io["o_wkvp"], St[:, NCH % 4], s("states_out"))
            sp.wait_ge(s("o_sample"), 1)
            sp.wait_ge(s("states_out"), 32)
            for n in range(4):
                dma(raw[:, n], io["w_out"][n], raw_in[n])
            for n in range(4, KD):
                sp.wait_ge(w_lo, PC + n - 3)
                dma(raw[:, n % 4], io["w_out"][n], raw_in[n % 4])
            sp.wait_ge(s("mix_ready"), 8)
            dma(X2[:], io["xT"], s("x2_in"))
            for k in range(KD):
                sp.wait_ge(s("x1_ready"), k + 1)
                dma(x1_dram[:, k], X2[:, k], s("x1_out"))
            sp.wait_ge(w_lo, PC + KD)
            sp.wait_ge(s("out_ready"), KD)

            def tile(src, slot, count):
                if count is not None:
                    sp.wait_ge(s("w3_lo"), count)
                dma(raw3[:, slot], src, s(f"raw3_in{slot}"))

            for m, c in enumerate((0, FC, 1, FC + 1)):
                tile(io["up"][c], m % 3, None if m < 3 else m - 2)
            sp.wait_ge(s("h2_lo"), KD)
            dma(conv_st[:], io["conv_st"], s("conv_in"))
            with sp.Fori(1, FC // 2) as i:
                for x, (name, off) in enumerate((("up", 0), ("down", -2), ("down", -1), ("up", FC), ("up", 1),
                                                 ("up", FC + 1))):
                    tile(one(io[name], i * 2 + off), (1 + x) % 3, i * 6 + (x - 4))
            for x in range(2):
                tile(io["down"][FC - 2 + x], (1 + x) % 3, 3 * FC + x - 4)
            sp.wait_ge(s("x1_out"), 16 * KD)
            sp.wait_ge(s("ffn_mm"), JOBS - KD)
            dma(X1[:], x1_dram, s("x1_in"))
            sp.wait_ge(s("conv_done"), 2 * FC)
            dma(io["o_tail"], ftail[:], small_out)
            dma(io["o_prev"], conv_st[:, 1], small_out)
            for k in range(KD):
                sp.wait_ge(s("y_ready"), k + 1)
                dma(io["o_y"][:, k], acc[:, k], s("y_out"))
            sp.wait_ge(s("y_out"), 16 * KD)
            sp.wait_ge(small_out, 16 * 4)


        XB = (12, 18)

        @block.tensor
        def _(pe):
            def sum_squares(square_of, ready, used):
                for k in range(KD):
                    pe.wait_ge(ready, k + 1)
                    for t in range(3):
                        mm = nc.tensor.matmul(ps[:, 3 + t, 0:SL], ones, square_of(k)[:, t * SL:(t + 1) * SL],
                                              start=(k == 0), stop=(k == KD - 1))
                    mm.then_inc(used, 1)

            def ada(first, count, slot_count):
                with pe.Fori(0, count // 4) as i:
                    for j in range(4):
                        pe.wait_ge(raw_in[j], (i + slot_count + 1) * 16)
                        for k in range(KD):
                            mm = nc.tensor.matmul(ps[:, 7, bass.ds((i * 4 + (first + j)) * 9, 9)],
                                                  raw[:, j, k * P:(k + 1) * P], cTs[:, k, :],
                                                  start=(k == 0), stop=(k == KD - 1), skip_group_check=True)
                        mm.then_inc(ada_used, 1)

            def product(bank_set, w, x):
                for k in range(KD):
                    for n, (a, b) in enumerate(((0, 0), (0, 1), (1, 0))):
                        for t in range(3):
                            mm = nc.tensor.matmul(ps[:, 3 * bank_set + t, 0:SL], w[:, a, k * P:(k + 1) * P],
                                                  x[:, k, b, t * SL:(t + 1) * SL],
                                                  start=(k == 0 and n == 0), stop=(k == KD - 1 and n == 2))
                return mm

            pe.wait_ge(silu_c, 1)
            ada(0, ADA_A, 0)
            pe.wait_ge(consts_in, 16 * 6)
            sum_squares(lambda k: sqA[k % 2], sq_ready, sq_used)
            def proj(n, j):
                if n is not None:
                    pe.wait_ge(w_lo, n + 1)
                return None
            for n in range(4):
                pe.wait_ge(w_lo, n + 1)
                pe.wait_ge(h_lo, KD)
                if n >= 2:
                    pe.wait_ge(proj_out, n - 1)
                product(n % 2, spl[:, n % 2], XS[:]).then_inc(proj_ready, 1)
            with pe.Fori(0, (PC - 4) // 2) as i:
                for j in range(2):
                    pe.wait_ge(w_lo, i * 2 + (5 + j))
                    pe.wait_ge(proj_out, i * 2 + (3 + j))
                    product(j, spl[:, j], XS[:]).then_inc(proj_ready, 1)
            pe.wait_ge(mod_ready, 1)
            ada(ADA_A, ADA_B, (ADA_A + PC) // 4)

            pe.wait_ge(proj_out, PC)
            for n, c in enumerate((18, 14, 15, 16, 17)):
                if n >= 2:
                    pe.wait_ge(s("rotated"), n - 1)
                for t in range(3):
                    mm = nc.tensor.matmul(ps[:, 3 * (n % 2) + t, 0:SL], const("swap"),
                                          PT[:, c, PO + t * SL:PO + (t + 1) * SL], start=True, stop=True)
                mm.then_inc(s("swapped"), 1)
                if n in (0, 1):
                    if n == 1:
                        pe.wait_ge(s("v_turned"), 1)
                    for i in range(4):
                        mm = nc.tensor.transpose(ps[:, 6, i * P:(i + 1) * P],
                                                 PT[:, 19, PO + (4 * n + i) * P:PO + (4 * n + i + 1) * P], ident)
                    mm.then_inc(s("v_turns"), 1)
            pe.wait_ge(s("v_turned"), 2)
            pe.wait_ge(s("rotated"), 1)
            for i, c in enumerate((18, 19)):
                mm = nc.tensor.transpose(ps[0:NS, 6, i * P:(i + 1) * P], PT[:, c, PO + T:PW], ident)
            mm.then_inc(s("kvrow_turned"), 1)

            def scores(u):
                i, kv = u // 2, u % 2
                lo = P if i == 0 else 0
                h = slice(HD * kv, HD * kv + HD)
                if u >= 2:
                    pe.wait_ge(s("masked"), u - 1)
                for j in range(4):
                    mm = nc.tensor.matmul(ps[:, 2 * (u % 2) + j // 2, (j % 2) * 2 * P + lo:(j % 2 + 1) * 2 * P],
                                          PT[h, 14 + j, PO + i * P:PO + (i + 1) * P],
                                          PT[h, 18, PO + (i - 1) * P + lo:PO + (i + 1) * P], start=True, stop=True)
                mm.then_inc(s("scored"), 1)

            def turn_probs(u):
                i = u // 2
                pe.wait_ge(s("probs"), u + 1)
                if u >= 1:
                    pe.wait_ge(s("probs_turned"), u)
                for j in range(4):
                    for kt in range(2):
                        if i == 0 and kt == 0:
                            continue
                        mm = nc.tensor.transpose(ps[:, 4 + j // 2, ((j % 2) * 2 + kt) * P:((j % 2) * 2 + kt + 1) * P],
                                                 S4[:, u % 2, j, kt * P:(kt + 1) * P], ident)
                mm.then_inc(s("probs_turns"), 1)

            def values(u):
                i, kv = u // 2, u % 2
                pe.wait_ge(s("probs_turned"), u + 1)
                if u >= 1:
                    pe.wait_ge(s("mixed"), u)
                else:
                    pe.wait_ge(s("kvrow_ready"), 1)
                kts = (1,) if i == 0 else (0, 1)
                for j in range(4):
                    for kt in kts:
                        mm = nc.tensor.matmul(ps[HD * kv:HD * kv + HD, 6, j * P:(j + 1) * P],
                                              VA[:, i - 1 + kt, HD * kv:HD * kv + HD], PR[:, u % 2, j, kt, :],
                                              start=(kt == kts[0]), stop=(kt == 1))
                mm.then_inc(s("valued"), 1)

            pe.wait_ge(s("rotated"), 5)
            scores(0)
            for u in range(2 * NT):
                if u + 1 < 2 * NT:
                    scores(u + 1)
                turn_probs(u)
                values(u)
            pe.wait_ge(s("cache_in"), 32)
            pe.wait_ge(s("masked"), 2 * NT)
            for b in range(NS):
                mm = nc.tensor.transpose(ps[:, b // 4, (b % 4) * P:(b % 4 + 1) * P], Kf[:, b, :], ident)
            mm.then_inc(s("sk_turns"), 1)
            pe.wait_ge(s("sk_turned"), 1)
            for b in range(NS):
                for kv in range(2):
                    h = slice(HD * kv, HD * kv + HD)
                    mm = nc.tensor.matmul(ps[:, 2 + kv, b * 4:b * 4 + 4], KTs[h, b, :],
                                          PT[h, 14:18, PO + T + b], start=True, stop=True)
            mm.then_inc(s("s_scored"), 1)
            pe.wait_ge(s("s_copied"), 1)
            nc.tensor.transpose(ps[0:64, 0, 0:P], sS[:], ident).then_inc(s("s_turns"), 1)
            pe.wait_ge(s("s_probs"), 1)
            nc.tensor.transpose(ps[:, 2, 0:64], sP[:], ident[0:64, 0:64]).then_inc(s("s_turns"), 1)
            pe.wait_ge(s("s_turned"), 1)
            pe.wait_ge(s("mixed"), 2 * NT)
            for b in range(NS):
                for kv in range(2):
                    mm = nc.tensor.matmul(ps[HD * kv:HD * kv + HD, 6, b * 4:b * 4 + 4],
                                          Vf[:, b, HD * kv:HD * kv + HD], sPT[:, b * 8 + kv * 4:b * 8 + kv * 4 + 4],
                                          start=True, stop=True)
            mm.then_inc(s("s_valued"), 1)
            pe.wait_ge(s("s_mixed"), 1)

            def by_head_sum(bank_set, src):
                for t in range(3):
                    mm = nc.tensor.matmul(ps[:, 3 * bank_set + t, 0:SL], bones, src[:, t * SL:(t + 1) * SL],
                                          start=True, stop=True)
                return mm

            def to_tokens(bank, src):
                for i in range(NT):
                    mm = nc.tensor.transpose(ps[:, bank + i // 4, (i % 4) * P:(i % 4 + 1) * P],
                                             src[:, i * P:(i + 1) * P], ident)
                return mm

            def prepare(j):
                cols = slice(j * P, (j + 1) * P)
                if j == 0:
                    pe.wait_ge(s("tanh_w"), 1)
                else:
                    pe.wait_ge(*evacuated("O", j - 1, 1))
                    pe.wait_ge(*evacuated("RG", j - 1, 1))
                for t in range(3):
                    mm = nc.tensor.matmul(ps[:, t, 0:SL], lora[0:64, cols],
                                          PT[0:64, 12, PO + t * SL:PO + (t + 1) * SL], start=True, stop=True)
                mm.then_inc(s("p_decay"), 1)
                for t in range(3):
                    mm = nc.tensor.matmul(ps[:, 3 + t, 0:SL], lora[64:P, cols],
                                          PT[64:P, 12, PO + t * SL:PO + (t + 1) * SL], start=True, stop=True)
                mm.then_inc(s("p_rate"), 1)
                pe.wait_ge(s("sig_decay"), j + 1)
                to_tokens(6, F0).then_inc(s("p_sgt"), 1)
                pe.wait_ge(s("k_square"), j + 1)
                by_head_sum(0, F2).then_inc(s("p_norm"), 1)
                pe.wait_ge(s("sgt_copied"), j + 1)
                pe.wait_ge(s("k_norm"), j + 1)
                for i in range(NT):
                    mm = nc.tensor.matmul(ps[:, i // 2, (i % 2) * 2 * P:(i % 2 + 1) * 2 * P], SGt[:, i],
                                          const("cumsum"), start=True, stop=True)
                mm.then_inc(s("p_cum"), 1)
                pe.wait_ge(s("decays"), 4 * (j + 1))
                pe.wait_ge(s("rkk"), j + 1)
                by_head_sum(1, F0).then_inc(s("p_bonus"), 1)
                pe.wait_ge(s("factors"), 4 * j + 1)
                to_tokens(6, F3).then_inc(s("p_turn"), 1)
                pe.wait_ge(s("factors"), 4 * j + 3)
                to_tokens(0, F5).then_inc(s("p_turn"), 1)
                pe.wait_ge(s("turned_a"), 2 * j + 1)
                pe.wait_ge(s("factors"), 4 * j + 4)
                to_tokens(6, F6).then_inc(s("p_turn"), 1)
                pe.wait_ge(s("turned_d"), 2 * j + 1)
                to_tokens(0, PT[:, 8 + j, PO:PO + T]).then_inc(s("p_turn"), 1)

            def units(half, by_chunk):
                for cp in range(NT):
                    for n in range(2):
                        yield (cp, n, half) if by_chunk else (cp, half, n)

            def fm(src, cp, hh, q):
                return src[HD * hh:HD * hh + HD, (2 * cp + q) * C:(2 * cp + q + 1) * C]

            def um(src, cp, hh, q):
                return src[HD * q:HD * q + HD, NT * hh + cp, :]

            def tm(src, cp, hh, q):
                return src[HD * q:HD * q + HD, cp, HD * hh:HD * hh + HD]

            def chunks(j):
                r = PT[:, j, PO:PO + T]
                count = [0]

                def step(name, half, terms, by_chunk=False):
                    g = (j * len(STEPS) + STEPS.index(name)) * 2 + half
                    assert count[0] + j * len(STEPS) * 2 == g
                    count[0] += 1
                    bank = g % 8
                    if count[0] > 8:
                        before = STEPS[(g - 8) // 2 % len(STEPS)]
                        pe.wait_ge(*evacuated(before, j, half))
                    for cp, hh, q in units(half, by_chunk):
                        h = HD * (hh if by_chunk else q)
                        out = ps[h:h + HD, bank, cp * C:(cp + 1) * C]
                        for i, (fa, a, fb, b) in enumerate(terms):
                            mm = nc.tensor.matmul(out, fa(a, cp, hh, q), fb(b, cp, hh, q), start=(i == 0),
                                                  stop=(i == len(terms) - 1))
                    mm.then_inc(s("unit_mm"), 1)

                pe.wait_ge(s("turned_a"), 2 * j + 2)
                pe.wait_ge(s("turned_d"), 2 * j + 2)
                pe.wait_ge(s("bonus"), j + 1)
                for name, a, b in (("M", F3, F1), ("MT", F1, F3), ("MkT", F4, F3), ("NbT", F1, r), ("NkT", F4, r)):
                    for half in range(2):
                        step(name, half, [(fm, a, fm, b)])
                for n in range(len(LEVELS)):
                    for half in range(2):
                        pe.wait_ge(*evacuated("MT" if n == 0 else f"Z{n - 1}", j, half))
                        step(f"Y{n}", half, [(um, MT, um, Tm)])
                    if n < len(LEVELS) - 1:
                        for half in range(2):
                            pe.wait_ge(*evacuated(f"Y{n}", j, half))
                            if n >= 1:
                                pe.wait_ge(*evacuated(f"ZT{n - 1}", j, half))
                            step(f"Z{n}", half, [(um, TT, um, Ym)])
                    for half in range(2):
                        pe.wait_ge(*evacuated(f"Y{n}", j, half))
                        if n >= 1:
                            pe.wait_ge(*evacuated(f"ZT{n - 1}", j, half))
                        step(f"ZT{n}", half, [(um, Ym, um, TT)])
                last = len(LEVELS) - 1
                for half in range(2):
                    pe.wait_ge(*evacuated("MkT", j, half))
                    step("W1", half, [(um, MkT, tm, vTm)])
                for half in range(2):
                    pe.wait_ge(*evacuated(f"ZT{last}", j, half))
                    step("G", half, [(um, TT, tm, aTm)])
                for half in range(2):
                    pe.wait_ge(*evacuated("W1", j, half))
                    step("H", half, [(um, TT, um, W1)])
                pe.wait_ge(*evacuated("H", j, 1))
                for half in range(2):
                    step("E", half, [(tm, bTm, um, Hm), (tm, kTm, tm, vTm)], True)
                for half in range(2):
                    step("A", half, [(um, Gm, tm, bTm)], True)
                for half in range(2):
                    step("RG", half, [(um, Gm, um, NbT)], True)
                for half in range(2):
                    step("O", half, [(um, Hm, um, NbT), (tm, vTm, um, NkT)], True)

            for j in range(NJ):
                prepare(j)
                chunks(j)

            pe.wait_ge(*evacuated("O", NJ - 1, 1))
            pe.wait_ge(*evacuated("RG", NJ - 1, 1))
            pe.wait_ge(s("smp_ready"), NJ)
            for j in range(NJ):
                mm = nc.tensor.transpose(ps[0:48, 4, j * P:(j + 1) * P], SMP[:, j].rearrange("p q b -> p (q b)"), ident)
            mm.then_inc(s("smp_turns"), 1)
            for c in range(1, NCH):
                pe.wait_ge(s("state_ready"), c)
                for j in range(NJ):
                    for hh in range(2):
                        h = slice(HD * hh, HD * hh + HD)
                        mm = nc.tensor.matmul(ps[h, c % 2, j * C:(j + 1) * C], Aff[h, j, chunk_at(c), :], St[h, c % 4, j, :],
                                              start=True, stop=True)
                mm.then_inc(s("state_mm"), 1)
                if c >= 3:
                    pe.wait_ge(s("o_added"), c - 2)
                for j in range(NJ):
                    for hh in range(2):
                        h = slice(HD * hh, HD * hh + HD)
                        mm = nc.tensor.matmul(ps[h, 2 + c % 2, j * C:(j + 1) * C], St[h, c % 4, j, :],
                                              PT[h, j, PO + c * C:PO + (c + 1) * C], start=True, stop=True)
                mm.then_inc(s("o_mm"), 1)
            pe.wait_ge(s("or_in"), 16)
            for j in range(NJ):
                mm = nc.tensor.transpose(ps[:, 5, j * NS:(j + 1) * NS], OR[:, j * P:(j + 1) * P], ident[0:NS, 0:NS])
            mm.then_inc(s("or_turns"), 1)

            pe.wait_ge(s("o_sample"), 1)
            pe.wait_ge(s("o_added"), NCH - 1)
            pe.wait_ge(s("sig_g"), 1)
            for j in range(NJ):
                if j >= 1:
                    pe.wait_ge(s("gated"), j)
                by_head_sum(0, PT[:, 8 + j, PO:PW]).then_inc(s("gn_mean"), 1)
                pe.wait_ge(s("gn_square"), j + 1)
                by_head_sum(1, PT[:, XB[j % 2], PO:PW]).then_inc(s("gn_var"), 1)
                for t in range(3):
                    mm = nc.tensor.matmul(ps[:, t, 0:SL], g_up[:, j * P:(j + 1) * P],
                                          PT[:, 13, PO + t * SL:PO + (t + 1) * SL], start=True, stop=True)
                mm.then_inc(s("gn_gate"), 1)
            pe.wait_ge(s("mix_ready"), 8)
            pe.wait_ge(s("gated"), NJ)
            for n in range(KD):
                pe.wait_ge(w_lo, PC + n + 1)
                if n >= 2:
                    pe.wait_ge(s("out_out"), n - 1)
                product(n % 2, spl[:, n % 2], XS[:]).then_inc(s("out_ready"), 1)
            for n in range(2):
                pe.wait_ge(s("sq_sum"), n + 1)
                pe.wait_ge(s("out_out"), KD)
                for t in range(3):
                    mm = nc.tensor.matmul(ps[:, 3 * n + t, 0:SL], ones, sqs[:, t * SL:(t + 1) * SL],
                                          start=True, stop=True)
                mm.then_inc(s("sq_total"), 1)
            pe.wait_ge(s("std2"), 2)

            def up(i, x, off, w3, waits):
                pe.wait_ge(s("w3_lo"), w3)
                for name, count in waits:
                    pe.wait_ge(s(name), count)
                product(off % 2, spl3[:, (1 + x) % 3], XS[:]).then_inc(s("ffn_mm"), 1)

            def down(i, w3):
                pe.wait_ge(s("w3_lo"), w3)
                pe.wait_ge(s("g_lo"), i * 2)
                for k in range(KD):
                    y = k + 1
                    if y == 1:
                        pe.wait_ge(s("up_out"), i * 4)
                    elif y == 2:
                        pe.wait_ge(s("up_out"), up2(i))
                    else:
                        pe.wait_ge(s("down_out"), i * 8 + (y - 10))
                    first = down_slot(i)
                    for f in range(2):
                        w = spl3[:, (first + f) % 3]
                        for n, (a, b) in enumerate(((0, 0), (0, 1), (1, 0))):
                            for t in range(3):
                                mm = nc.tensor.matmul(ps[:, 3 * (down_set(i, y)) + t, 0:SL], w[:, a, k * P:(k + 1) * P],
                                                      act2[:, f, b, t * SL:(t + 1) * SL],
                                                      start=(f == 0 and n == 0), stop=(f == 1 and n == 2))
                    mm.then_inc(s("ffn_mm"), 1)

            LAST = FC // 2

            def is_last(i):
                return isinstance(i, int) and i == LAST

            def up2(i):
                return i * 4 if is_last(i) else i * 4 + 1

            def down_slot(i):
                return 1 if is_last(i) else 2

            def down_set(i, y):
                return (y - 1) % 2 if is_last(i) else y % 2

            pe.wait_ge(s("h2_lo"), KD)
            for m in range(4):
                pe.wait_ge(s("w3_lo"), m + 1)
                if m >= 2:
                    pe.wait_ge(s("up_out"), m - 1)
                product(m % 2, spl3[:, m % 3], XS[:]).then_inc(s("ffn_mm"), 1)
            with pe.Fori(1, LAST) as i:
                up(i, 0, 0, i * 6 - 1, [("up_out", i * 4 - 1)])
                down(i, i * 6 + 1)
                up(i, 3, 9, i * 6 + 2, [("down_out", i * 8 - 1)])
                up(i, 4, 10, i * 6 + 3, [("down_out", i * 8)])
                up(i, 5, 11, i * 6 + 4, [("up_out", i * 4 + 2)])
            down(LAST, 3 * FC)
            pe.wait_ge(s("sq_sum"), 3)
            pe.wait_ge(s("down_out"), KD * LAST)
            for t in range(3):
                mm = nc.tensor.matmul(ps[:, t, 0:SL], ones, sqF[:, t * SL:(t + 1) * SL], start=True, stop=True)
            mm.then_inc(s("sq_total"), 1)

        @block.scalar
        def _(act):
            mark = [0]

            def link(ins):
                mark[0] += 1
                ins.then_inc(act_step, 1)
                act.wait_ge(act_step, mark[0])

            act.wait_ge(s("c_in"), 16)
            nc.scalar.activation(cTs[:], cT[:], ACT.Silu).then_inc(silu_c, 1)
            act.wait_ge(x_in, 16)
            for k in range(KD):
                if k >= 2:
                    act.wait_ge(sq_used, k - 1)
                nc.scalar.activation(sqA[k % 2], xT[:, k], ACT.Square).then_inc(sq_ready, 1)
            act.wait_ge(zeros_set, 1)
            act.wait_ge(sq_used, KD)
            nc.scalar.activation(slices(tmpA[:]), three(1), ACT.Sqrt, bias=eps[:, 0:1],
                                 scale=1.0 / D).then_inc(std_ready, 1)
            def whi(slot2, slot4):
                nc.scalar.activation(spl[:, slot2, 0], raw[:, slot4], ACT.Copy).then_inc(w_hi, 1)
            for n in range(2):
                act.wait_ge(raw_in[n], (ADA_A // 4 + 1) * 16)
                whi(n, n)
            for k in range(KD):
                act.wait_ge(h_ready, k + 1)
                nc.scalar.activation(XS[:, k, 0], hA[k % 2], ACT.Copy).then_inc(h_hi, 1)

            def evac(n, bank_set):
                nc.scalar.activation(PT[:, bass.ds(n, 1), PO:PW].rearrange("p o (s t) -> p (o s) t", s=3),
                                     three(bank_set), ACT.Copy).then_inc(proj_out, 1)

            for n in range(2):
                act.wait_ge(proj_ready, n + 1)
                act.wait_ge(raw_in[n + 2], (ADA_A // 4 + 1) * 16)
                whi(n, n + 2)
                evac(n, n)
            with act.Fori(0, (PC - 4) // 4) as i:
                for j in range(4):
                    act.wait_ge(proj_ready, i * 4 + (3 + j))
                    act.wait_ge(raw_in[j], (i + (ADA_A // 4 + 2)) * 16)
                    whi(j % 2, j)
                    evac(i * 4 + (2 + j), j % 2)
            for n in range(PC - 2, PC):
                act.wait_ge(proj_ready, n + 1)
                evac(n, n % 2)

            nc.scalar.dma_start(rope[:], io["rope"]).then_inc(s("rope_in"), 16)
            for n in range(2):
                act.wait_ge(s("v_turns"), n + 1)
                nc.scalar.activation(VA[:, 4 * n:4 * n + 4, :], ps[:, 6, :].rearrange("p (i c) -> p i c", c=P),
                                     ACT.Copy).then_inc(s("v_turned"), 1)
            act.wait_ge(s("kvrow_turned"), 1)
            nc.scalar.activation(kvrow[:], ps[0:NS, 6, 0:2 * P].rearrange("p (i c) -> p i c", c=P),
                                 ACT.Copy).then_inc(s("kvrow_ready"), 1)

            def exps(u):
                i = u // 2
                lo = P if i == 0 else 0
                act.wait_ge(s("maxed"), u + 1)
                for j in range(4):
                    nc.scalar.activation(S4[:, u % 2, j, lo:], S4[:, u % 2, j, lo:], ACT.Exp, bias=nm[:, u % 2, j:j + 1],
                                         accum_out=den[:, u % 2, j:j + 1])
                nc.scalar.activation(sk[:, u % 2, :], sk[:, u % 2, :], ACT.Exp).then_inc(s("exped"), 1)

            def move(u):
                i, kv = u // 2, u % 2
                act.wait_ge(s("probs_turns"), u + 1)
                kt = slice(1, 2) if i == 0 else slice(0, 2)
                nc.scalar.activation(PR[:, u % 2, :, kt, :],
                                     ps[:, 4:6, :].rearrange("p b (j k c) -> p (b j) k c", k=2, c=P)[:, :, kt, :],
                                     ACT.Copy).then_inc(s("probs_turned"), 1)
                act.wait_ge(s("valued"), u + 1)
                nc.scalar.activation(PT[HD * kv:HD * kv + HD, 14:18, PO + i * P:PO + (i + 1) * P],
                                     ps[HD * kv:HD * kv + HD, 6, :].rearrange("p (j c) -> p j c", c=P),
                                     ACT.Copy).then_inc(s("mixed"), 1)

            for u in range(2 * NT):
                exps(u)
                if u >= 1:
                    move(u - 1)
            move(2 * NT - 1)
            act.wait_ge(s("sk_turns"), 1)
            nc.scalar.activation(KTs[:], ps[:, 0:2, :].rearrange("p b (i c) -> p (b i) c", c=P),
                                 ACT.Copy).then_inc(s("sk_turned"), 1)
            act.wait_ge(s("s_scored"), 1)
            nc.scalar.activation(sS[:].rearrange("p (b v g) -> p v b g", v=2, g=4),
                                 ps[:, 2:4, 0:32].rearrange("p v (b g) -> p v b g", g=4), ACT.Copy).then_inc(s("s_copied"), 1)
            act.wait_ge(s("s_maxed"), 1)
            nc.scalar.activation(sP[:], sP[:], ACT.Exp, bias=nm[0:64, 0, 0:1], accum_out=den[0:64, 0, 0:1])
            nc.scalar.activation(sk[0:64, 0, 0:1], sk[0:64, 0, 0:1], ACT.Exp).then_inc(s("s_exped"), 1)
            act.wait_ge(s("s_turns"), 2)
            nc.scalar.activation(sPT[:], ps[:, 2, 0:64], ACT.Copy).then_inc(s("s_turned"), 1)
            act.wait_ge(s("s_valued"), 1)
            nc.scalar.activation(PT[:, 14:18, PO + T:PW], ps[:, 6, 0:32].rearrange("p (b j) -> p j b", j=4),
                                 ACT.Copy).then_inc(s("s_mixed"), 1)

            act.wait_ge(s("shifted"), RC)
            nc.scalar.activation(PT[0:64, 12, PO:PW], PT[0:64, 12, PO:PW], ACT.Tanh).then_inc(s("tanh_w"), 1)
            nc.scalar.activation(PT[:, 13, PO:PW], PT[:, 13, PO:PW], ACT.Sigmoid).then_inc(s("sig_g"), 1)
            for j in range(NJ):
                if j >= 1:
                    act.wait_ge(*computed("O", j - 1, 1))
                act.wait_ge(s("p_decay"), j + 1)
                nc.scalar.activation(slices(F0[:]), three(0), ACT.Sigmoid, bias=param("rwkv_w0", j)).then_inc(s("sig_decay"), 1)
                act.wait_ge(s("p_rate"), j + 1)
                nc.scalar.activation(slices(F1[:]), three(1), ACT.Sigmoid, bias=param("rwkv_a0", j)).then_inc(s("sig_rate"), 1)
                nc.scalar.activation(F2[:], PT[:, 4 + j, PO:PW], ACT.Square, scale=param("rwkv_k_k", j)).then_inc(s("k_square"), 1)
                act.wait_ge(s("p_sgt"), j + 1)
                nc.scalar.activation(SGt, ps[:, 6:8, :].rearrange("p b (i c) -> p (b i) c", c=P),
                                     ACT.Copy).then_inc(s("sgt_copied"), 1)
                act.wait_ge(s("p_norm"), j + 1)
                nc.scalar.activation(slices(F3[:]), three(0), ACT.Sqrt).then_inc(s("k_norm"), 1)
                act.wait_ge(s("p_cum"), j + 1)
                act.wait_ge(s("sig_decay"), j + 1)
                cum = ps[:, 0:4, :].rearrange("p b (i x t) -> p (b i) x t", x=2, t=P)

                def tiled(f):
                    return f[:, 0:T].rearrange("p (i t) -> p i t", t=P)

                nc.scalar.activation(tiled(F5), cum[:, :, 0, :], ACT.Exp, scale=-KAPPA).then_inc(s("decays"), 1)
                nc.scalar.activation(tiled(F6), cum[:, :, 0, :], ACT.Exp, scale=KAPPA).then_inc(s("decays"), 1)
                nc.scalar.activation(tiled(F2), cum[:, :, 1, :], ACT.Exp, scale=-KAPPA).then_inc(s("decays"), 1)
                nc.scalar.activation(SMP[:, j, 1, :], F0[:, T:N], ACT.Exp, scale=-KAPPA).then_inc(s("decays"), 1)
                for n, (bank, dst) in enumerate(((6, aTm), (6, kTm))):
                    act.wait_ge(s("p_turn"), 4 * j + 1 + 2 * n)
                    nc.scalar.activation(dst[:], ps[:, bank:bank + 2, :].rearrange("p b (i c) -> p (b i) c", c=P),
                                         ACT.Copy).then_inc(s("turned_a"), 1)
                dests = {"W1": W1, "G": Gm, "H": Hm}
                for name in act_steps:
                    for half in range(2):
                        act.wait_ge(*computed(name, j, half))
                        bank = (computed(name, j, half)[1] - 1) % 8
                        u = slice(8 * half, 8 * half + 8)
                        if name == "E":
                            dst = Ein[:, j, u, :]
                        elif name == "O":
                            dst = PT[:, 8 + j, PO:PO + T].rearrange("p (u q c) -> p q u c", q=2, c=C)[:, half]
                        else:
                            dst = (Ym if name[0] == "Y" else dests[name])[:, u, :]
                        nc.scalar.activation(dst, ps[:, bank, :].rearrange("p (u c) -> p u c", c=C),
                                             ACT.Copy).then_inc(s("unit_act"), 1)
            act.wait_ge(s("smp_turns"), 1)
            nc.scalar.activation(SM48[:], ps[0:48, 4, :], ACT.Copy).then_inc(s("sm48_ready"), 1)
            act.wait_ge(s("or_turns"), 1)
            nc.scalar.activation(PT[:, 8:12, PO + T:PW], ps[:, 5, 0:4 * NS].rearrange("p (j b) -> p j b", b=NS),
                                 ACT.Copy).then_inc(s("o_sample"), 1)
            for j in range(NJ):
                X = PT[:, XB[j % 2], PO:PW]
                act.wait_ge(s("centred"), j + 1)
                nc.scalar.activation(X, PT[:, j, PO:PW], ACT.Square).then_inc(s("gn_square"), 1)
                act.wait_ge(s("gn_var"), j + 1)
                nc.scalar.activation(slices(X), three(1), ACT.Sqrt, bias=eps[:, 1:2], scale=1.0 / HD).then_inc(s("gn_std"), 1)
                act.wait_ge(s("gated"), j + 1)
                if j == 0:
                    act.wait_ge(s("states_out"), 32)
                nc.scalar.activation(XS[:, j, 0], PT[:, j, PO:PW], ACT.Copy).then_inc(s("mix_hi"), 1)
                nc.scalar.activation(XS[:, 4 + j, 0], PT[:, 14 + j, PO:PW], ACT.Copy).then_inc(s("mix_hi"), 1)
            def whi_out(n):
                act.wait_ge(raw_in[n % 4], ((ADA_A + ADA_B + PC + n) // 4 + 1) * 16)
                whi(n % 2, n % 4)

            whi_out(0)
            whi_out(1)
            for n in range(KD):
                act.wait_ge(s("out_ready"), n + 1)
                if n + 2 < KD:
                    whi_out(n + 2)
                if n >= 2:
                    act.wait_ge(s("sq_added"), n - 1)
                nc.scalar.activation(slices(sq2[:, n % 2]), three(n % 2), ACT.Square).then_inc(s("sq_c"), 1)
                nc.scalar.activation(slices(MO[:, n]), three(n % 2), ACT.Copy).then_inc(s("out_out"), 1)
            act.wait_ge(s("sq_total"), 1)
            nc.scalar.activation(slices(rsC[:]), three(0), ACT.Sqrt, bias=eps[:, 0:1], scale=1.0 / D).then_inc(s("std2"), 1)
            for k in range(KD):
                act.wait_ge(s("x1_ready"), k + 1)
                if k >= 2:
                    act.wait_ge(s("sq_added"), KD + k - 1)
                nc.scalar.activation(sq2[:, k % 2], X2[:, k], ACT.Square).then_inc(s("sq_c"), 1)
            act.wait_ge(s("sq_total"), 2)
            nc.scalar.activation(slices(rsC[:]), three(1), ACT.Sqrt, bias=eps[:, 0:1], scale=1.0 / D).then_inc(s("std2"), 1)

            def w3(m_slot, in_count, used):
                act.wait_ge(s(f"raw3_in{m_slot}"), in_count * 16)
                if used is not None:
                    act.wait_ge(s("ffn_mm"), used)
                nc.scalar.activation(spl3[:, m_slot, 0], raw3[:, m_slot], ACT.Copy).then_inc(s("w3_hi"), 1)

            for m in range(3):
                w3(m, 1, None)
            for k in range(KD):
                act.wait_ge(s("h2_ready"), k + 1)
                nc.scalar.activation(XS[:, k, 0], MO[:, k], ACT.Copy).then_inc(s("h2_hi"), 1)

            def evac_up(c, chunk, job, bank_set, before):
                act.wait_ge(s("ffn_mm"), job)
                act.wait_ge(s("g_done"), before)
                nc.scalar.activation(slices(U[:, c]), three(bank_set), ACT.Copy)
                a = PARAM_AT["ffn_conv_w"][0] + 2 * 2 * FC
                b = PARAM_AT["ffn_conv_b"][0]
                nc.scalar.activation(slices(Z[:, c]), three(bank_set), ACT.Identity, bias=col(b, chunk),
                                     scale=col(a, chunk)).then_inc(s("up_out"), 1)

            def gate_up(pair, slot):
                act.wait_ge(s("conv_done"), pair * 2 + 1)
                nc.scalar.activation(Z[:, 0], Z[:, 0], ACT.Silu).then_inc(s("silu_done"), 1)
                act.wait_ge(s("g_done"), pair + 2)
                nc.scalar.activation(act2[:, slot, 0], G[:], ACT.Copy).then_inc(s("g_hi"), 1)

            act.wait_ge(s("ffn_mm"), 1)
            w3(0, 2, 1)
            evac_up(0, 0, 1, 0, 1)
            evac_up(1, FC, 2, 1, 1)
            gate_up(0, 0)
            w3(1, 2, 2)
            evac_up(0, 1, 3, 0, 2)
            w3(2, 2, 3)
            w3(0, 3, 4)
            evac_up(1, FC + 1, 4, 1, 2)
            gate_up(1, 1)

            def act_body(i, last):
                w3(1, i * 2 + 1, i * 12 - 7)
                evac_up(0, i * 2, i * 12 - 7, 0, i * 2 + 1)
                w3(2, i * 2 + 1, i * 12 + 1)
                w3(0, i * 2 + 2, i * 12 + 1)
                evac_up(1, i * 2 + FC, i * 12 + 2, 1, i * 2 + 1)
                gate_up(i * 2, 0)
                w3(1, i * 2 + 2, i * 12 + 2)
                evac_up(0, i * 2 + 1, i * 12 + 3, 0, i * 2 + 2)
                w3(2, i * 2 + 2, i * 12 + 3)
                if not last:
                    w3(0, i * 2 + 3, i * 12 + 4)
                evac_up(1, i * 2 + (FC + 1), i * 12 + 4, 1, i * 2 + 2)
                gate_up(i * 2 + 1, 1)

            with act.Fori(1, FC // 2 - 1) as i:
                act_body(i, False)
            act_body(FC // 2 - 1, True)
            for k in range(KD):
                act.wait_ge(s("down_out"), KD * (FC // 2 - 1) + k + 1)
                if k >= 2:
                    act.wait_ge(s("sq_added"), 2 * KD + k - 1)
                nc.scalar.activation(Z[:, k % 2], acc[:, k], ACT.Square).then_inc(s("sq_c"), 1)
            act.wait_ge(s("sq_total"), 3)
            nc.scalar.activation(slices(G[:]), three(0), ACT.Sqrt, bias=eps[:, 0:1], scale=1.0 / D).then_inc(s("std2"), 1)

        @block.vector
        def _(dve):
            mark, past = [0], [0]

            def link(ins):
                mark[0] += 1
                ins.then_inc(dve_step, 1)
                dve.wait_ge(dve_step, mark[0] + past[0])

            link(nc.vector.memset(eps[:, 0:1], NORM_EPS))
            link(nc.vector.memset(eps[:, 2:3], 0.0))
            nc.vector.memset(eps[:, 1:2], GN_EPS).then_inc(zeros_set, 1)
            dve.wait_ge(consts_in, 16 * 6)
            dve.wait_ge(std_ready, 1)
            link(nc.vector.reciprocal(rs[:], tmpA[:]))

            def modulation(first, count, ready):
                dve.wait_ge(ada_used, first + count)
                a = PARAM_AT["b_ada"][0] + first
                ins = nc.vector.tensor_tensor(mod[:, first:first + count, :],
                                              ps[:, 7, first * 9:(first + count) * 9].rearrange(
                                                  "p (n c) -> p n c", c=9),
                                              par[:, a:a + count].unsqueeze(2).broadcast_to([P, count, 9]),
                                              ALU.add)
                link(ins)

            def norm_scale(out, name, chunk):
                link(nc.vector.tensor_scalar(out[:], mod[:, chunk:chunk + KD, :], 1.0, None, ALU.add))
                link(nc.vector.tensor_tensor(out[:], out[:], params(name).unsqueeze(2).broadcast_to([P, KD, 9]),
                                             ALU.mult))

            modulation(0, ADA_A, None)
            norm_scale(gs1, "norm_pre_mix", 8)
            def w_low(slot2, slot4):
                return nc.vector.tensor_tensor(spl[:, slot2, 1], raw[:, slot4], spl[:, slot2, 0].bitcast(F32),
                                               ALU.subtract)
            for n in range(2):
                dve.wait_ge(w_hi, n + 1)
                w_low(n, n).then_inc(w_lo, 1)
            def low(k):
                dve.wait_ge(h_hi, k + 1)
                nc.vector.tensor_tensor(XS[:, k, 1], hA[k % 2], XS[:, k, 0].bitcast(F32),
                                        ALU.subtract).then_inc(h_lo, 1)
            for k in range(KD):
                if k >= 2:
                    dve.wait_ge(h_lo, k - 1)
                link(nc.vector.tensor_tensor(xT[:, k], xT[:, k], rs[:], ALU.mult))
                link(nc.vector.tensor_tensor(hA[k % 2][:, T:N], xT[:, k, T:N], gs1[:, k, 1:9], ALU.mult))
                link(nc.vector.tensor_tensor(hA[k % 2][:, T:N], hA[k % 2][:, T:N], mod[:, k, 1:9], ALU.add))
                nc.vector.tensor_scalar(hA[k % 2][:, 0:T], xT[:, k, 0:T], gs1[:, k, 0:1], mod[:, k, 0:1],
                                        ALU.mult, ALU.add).then_inc(h_ready, 1)
                if k >= 1:
                    low(k - 1)
            low(KD - 1)
            for n in range(2):
                dve.wait_ge(w_hi, n + 3)
                w_low(n, n + 2).then_inc(w_lo, 1)
            with dve.Fori(0, (PC - 4) // 4) as i:
                for j in range(4):
                    dve.wait_ge(w_hi, i * 4 + (5 + j))
                    w_low(j % 2, j).then_inc(w_lo, 1)
            nc.vector.memset(PT[:, :, 0:PO], 0.0).then_inc(mod_ready, 1)
            dve.wait_ge(proj_out, PC)
            dve.wait_ge(mod_ready, 1)
            nc.vector.tensor_copy(tail_shift[:], PT[:, 0:RC, PW - NS - 1:PW]).then_inc(s("shift_saved"), 1)
            dve.wait_ge(s("shift_saved"), 1)
            for n, c in enumerate((12, 13) + tuple(range(12))):
                d = dif[:, n % 2]
                if n >= 2:
                    dve.wait_ge(s("shifted"), n - 1)
                link(nc.vector.tensor_tensor(d[:, 0:T], PT[:, c, PO - 1:PO - 1 + T], PT[:, c, PO:PO + T], ALU.subtract))
                link(nc.vector.tensor_tensor(d[:, T:N], shift_st[:, c], PT[:, c, PO + T:PW], ALU.subtract))
                nc.vector.scalar_tensor_tensor(PT[:, c, PO:PW], d, param("rwkv_mu", c), PT[:, c, PO:PW], ALU.mult,
                                               ALU.add).then_inc(s("shifted"), 1)
            dve.wait_ge(s("shifted"), RC)
            modulation(ADA_A, ADA_B, None)
            dve.wait_ge(s("rope_in"), 16)
            for n, c in enumerate((18, 14, 15, 16, 17)):
                if n >= 1:
                    dve.wait_ge(s("rotated"), n)
                link(nc.vector.tensor_tensor(dif[:, 0], PT[:, c, PO:PW], rope[:, 0], ALU.mult))
                dve.wait_ge(s("swapped"), n + 1)
                link(nc.vector.tensor_tensor(slices(dif[:, 1]), three(n % 2), slices(rope[:, 1]), ALU.mult))
                ins = nc.vector.tensor_tensor(PT[:, c, PO:PW], dif[:, 0], dif[:, 1], ALU.add)
                ins.then_inc(s("rotated"), 1)
            dve.wait_ge(s("rotated"), 5)

            def mask_max(u):
                i, kv, v = u // 2, u % 2, u % 2
                lo = P if i == 0 else 0
                dve.wait_ge(s("scored"), u + 1)
                if u >= 2:
                    dve.wait_ge(s("probs_turns"), u - 1)
                win = const("window")[:, lo:].unsqueeze(1).broadcast_to([P, 4, 2 * P - lo])
                sc = ps[:, 2 * v:2 * v + 2, :].rearrange("p b (j k) -> p (b j) k", j=2)[:, :, lo:]
                nc.vector.scalar_tensor_tensor(S4[:, v, :, lo:], sc, SCALE, win, ALU.mult, ALU.add).then_inc(s("masked"), 1)
                dve.wait_ge(s("masked"), u + 1)
                link(nc.vector.tensor_reduce(mx[:, v], S4[:, v, :, lo:], AX.X, ALU.max))
                a = PARAM_AT["sinks"][0] + 4 * kv
                link(nc.vector.tensor_tensor(mx[:, v], mx[:, v], par[:, a:a + 4], ALU.max))
                link(nc.vector.tensor_tensor(sk[:, v], par[:, a:a + 4], mx[:, v], ALU.subtract))
                nc.vector.tensor_scalar(nm[:, v], mx[:, v], -1.0, None, ALU.mult).then_inc(s("maxed"), 1)

            def normalise(u):
                i, v = u // 2, u % 2
                lo = P if i == 0 else 0
                dve.wait_ge(s("exped"), u + 1)
                link(nc.vector.tensor_tensor(den[:, v], den[:, v], sk[:, v], ALU.add))
                link(nc.vector.reciprocal(rd[:, v], den[:, v]))
                nc.vector.tensor_tensor(S4[:, v, :, lo:], S4[:, v, :, lo:],
                                        rd[:, v].unsqueeze(2).broadcast_to([P, 4, 2 * P - lo]),
                                        ALU.mult).then_inc(s("probs"), 1)

            for u in range(2 * NT):
                mask_max(u)
                if u >= 1:
                    normalise(u - 1)
            normalise(2 * NT - 1)
            dve.wait_ge(s("s_turns"), 1)
            link(nc.vector.tensor_scalar(sP[:], ps[0:64, 0, 0:P], SCALE, None, ALU.mult))
            link(nc.vector.tensor_reduce(mx[0:64, 0, 0:1], sP[:], AX.X, ALU.max))
            srow = par[0:64, PARAM_AT["sink_rows"][0]:PARAM_AT["sink_rows"][1]]
            link(nc.vector.tensor_tensor(mx[0:64, 0, 0:1], mx[0:64, 0, 0:1], srow, ALU.max))
            link(nc.vector.tensor_tensor(sk[0:64, 0, 0:1], srow, mx[0:64, 0, 0:1], ALU.subtract))
            nc.vector.tensor_scalar(nm[0:64, 0, 0:1], mx[0:64, 0, 0:1], -1.0, None, ALU.mult).then_inc(s("s_maxed"), 1)
            dve.wait_ge(s("s_exped"), 1)
            link(nc.vector.tensor_tensor(den[0:64, 0, 0:1], den[0:64, 0, 0:1], sk[0:64, 0, 0:1], ALU.add))
            link(nc.vector.reciprocal(rd[0:64, 0, 0:1], den[0:64, 0, 0:1]))
            nc.vector.tensor_scalar(sP[:], sP[:], rd[0:64, 0, 0:1], None, ALU.mult).then_inc(s("s_probs"), 1)
            link(nc.vector.tensor_scalar(sc_mod[:], params("rwkv_k_a"), -1.0, 1.0, ALU.mult, ALU.add))

            dve.wait_ge(s("s_mixed"), 1)
            for j in range(NJ):
                r, k, v = (PT[:, c + j, PO:PW] for c in (0, 4, 8))
                q = slice(0, T)
                dve.wait_ge(s("sig_rate"), j + 1)
                if j >= 1:
                    dve.wait_ge(*computed("O", j - 1, 1))
                link(nc.vector.tensor_scalar(F4[:], F1[:], param("rwkv_k_a", j), sc_mod[:, j:j + 1], ALU.mult, ALU.add))
                link(nc.vector.tensor_tensor(F4[:], F4[:], k, ALU.mult))
                dve.wait_ge(s("k_norm"), j + 1)
                link(nc.vector.tensor_scalar(F3[:], F3[:], 1e-12, None, ALU.max))
                link(nc.vector.reciprocal(F3[:], F3[:]))
                link(nc.vector.scalar_tensor_tensor(F3[:], k, param("rwkv_k_k", j), F3[:], ALU.mult, ALU.mult))
                link(nc.vector.tensor_tensor(F1[:], F1[:], F3[:], ALU.mult))
                dve.wait_ge(s("decays"), 4 * (j + 1))
                for n, src in ((0, F3[:, T:N]), (2, F4[:, T:N]), (3, F1[:, T:N]), (4, r[:, T:N]), (5, v[:, T:N])):
                    ins = nc.vector.tensor_copy(SMP[:, j, n, :], src)
                ins.then_inc(s("smp_ready"), 1)
                nc.vector.scalar_tensor_tensor(F0[:], r, param("rwkv_r_k", j), F4[:], ALU.mult, ALU.mult).then_inc(s("rkk"), 1)
                dve.wait_ge(s("rkk"), j + 1)
                nc.vector.scalar_tensor_tensor(F3[:, q], F3[:, q], -1.0, F2[:, q], ALU.mult, ALU.mult).then_inc(s("factors"), 1)
                link(nc.vector.tensor_tensor(F1[:, q], F1[:, q], F6[:, q], ALU.mult))
                link(nc.vector.tensor_tensor(F4[:, q], F4[:, q], F6[:, q], ALU.mult))
                nc.vector.tensor_tensor(r[:, q], r[:, q], F5[:, q], ALU.mult).then_inc(s("factors"), 1)
                link(nc.vector.tensor_copy(Pc[:], F5[:, C - 1:T:C]))
                dve.wait_ge(s("factors"), 4 * j + 2)
                ends = Pc[:].unsqueeze(2).broadcast_to([P, NCH, C])
                nc.vector.tensor_tensor(unit(F5), unit(F1), ends, ALU.mult).then_inc(s("factors"), 1)
                nc.vector.tensor_tensor(unit(F6), unit(F4), ends, ALU.mult).then_inc(s("factors"), 1)
                dve.wait_ge(s("p_bonus"), j + 1)
                nc.vector.tensor_tensor(slices(k), three(1), slices(v), ALU.mult).then_inc(s("bonus"), 1)
                for n, (bank, dst) in enumerate(((0, bTm), (0, vTm))):
                    dve.wait_ge(s("p_turn"), 4 * j + 2 + 2 * n)
                    nc.vector.tensor_copy(dst[:], ps[:, bank:bank + 2, :].rearrange("p b (i c) -> p (b i) c", c=P)
                                          ).then_inc(s("turned_d"), 1)
                eye = const("eye").unsqueeze(1).broadcast_to([P, 2 * NT, C])
                link(nc.vector.tensor_copy(Tm[:], eye))
                link(nc.vector.tensor_copy(TT[:], eye))
                for name in dve_steps:
                    for half in range(2):
                        dve.wait_ge(*computed(name, j, half))
                        u = slice(8 * half, 8 * half + 8)
                        bank = (computed(name, j, half)[1] - 1) % 8
                        out = ps[:, bank, :].rearrange("p (u c) -> p u c", c=C)

                        def all8(m):
                            return m.unsqueeze(1).broadcast_to([P, 8, C])

                        if name == "M":
                            ins = nc.vector.copy_predicated(Tm[:, u], all8(lvl[:, 0]), out)
                        elif name == "MT":
                            nc.vector.tensor_tensor(MT[:, u], out, all8(const("after")), ALU.mult)
                            ins = nc.vector.copy_predicated(TT[:, u], all8(lvl[:, 1]), out)
                        elif name in ("MkT", "NbT", "NkT"):
                            dst = {"MkT": MkT, "NbT": NbT, "NkT": NkT}[name]
                            ins = nc.vector.tensor_tensor(dst[:, u], out, all8(const("after" if name == "MkT" else "upto")),
                                                          ALU.mult)
                        elif name[0] == "Z":
                            up = name[1] == "T"
                            n = int(name[-1]) + 1
                            ins = nc.vector.copy_predicated((TT if up else Tm)[:, u], all8(lvl[:, 2 * n + up]), out)
                        elif name == "A":
                            dst = Aff[:, j, u, :]
                            link(nc.vector.tensor_tensor(dst, all8(const("eye")),
                                                         Pc[:, half::2].unsqueeze(2).broadcast_to([P, 8, C]), ALU.mult))
                            ins = nc.vector.tensor_tensor(dst, dst, out, ALU.add)
                        else:
                            dst = r[:, q].rearrange("p (u q c) -> p q u c", q=2, c=C)[:, half]
                            ins = nc.vector.tensor_tensor(dst, dst, out, ALU.add)
                        ins.then_inc(s("unit_dve"), 1)
            dve.wait_ge(*evacuated("E", NJ - 1, 1))
            dve.wait_ge(*evacuated("O", NJ - 1, 1))
            nc.vector.tensor_copy(St[:, 1], Ein[:, :, 0, :]).then_inc(s("state_ready"), 1)
            for c in range(1, NCH):
                dve.wait_ge(s("state_mm"), c)
                nc.vector.tensor_tensor(St[:, (c + 1) % 4], ps[:, c % 2, 0:NJ * C].rearrange("p (j v) -> p j v", v=C),
                                        Ein[:, :, chunk_at(c), :], ALU.add).then_inc(s("state_ready"), 1)
                dve.wait_ge(s("o_mm"), c)
                o = PT[:, 8:12, PO + c * C:PO + (c + 1) * C]
                nc.vector.tensor_tensor(o, o, ps[:, 2 + c % 2, 0:NJ * C].rearrange("p (j t) -> p j t", t=C),
                                        ALU.add).then_inc(s("o_added"), 1)
            dve.wait_ge(s("wkv_in"), 16 * 5)

            def over_v(i):
                return V6[:, i, :].unsqueeze(1).broadcast_to([P, 32, HD])

            def over_k(x):
                return x[:].unsqueeze(2).broadcast_to([P, 32, HD])

            link(nc.vector.tensor_tensor(sTmp[:], sWKV[:], over_v(0), ALU.mult))
            link(nc.vector.tensor_reduce(sa[:], sTmp[:], AX.X, ALU.add))
            link(nc.vector.tensor_tensor(sWKV[:], sWKV[:], over_v(1), ALU.mult))
            link(nc.vector.tensor_tensor(sTmp[:], over_k(sa), over_v(3), ALU.mult))
            link(nc.vector.tensor_tensor(sWKV[:], sWKV[:], sTmp[:], ALU.subtract))
            link(nc.vector.tensor_tensor(sTmp[:], over_k(V32), over_v(2), ALU.mult))
            link(nc.vector.tensor_tensor(sWKV[:], sWKV[:], sTmp[:], ALU.add))
            link(nc.vector.tensor_tensor(sTmp[:], sWKV[:], over_v(4), ALU.mult))
            nc.vector.tensor_reduce(Osm[:], sTmp[:], AX.X, ALU.add).then_inc(s("sample_o"), 1)

            for j in range(NJ):
                Y, X = PT[:, j, PO:PW], PT[:, XB[j % 2], PO:PW]
                dve.wait_ge(s("gn_mean"), j + 1)
                nc.vector.scalar_tensor_tensor(slices(Y), three(0), -1.0 / HD, slices(PT[:, 8 + j, PO:PW]), ALU.mult,
                                               ALU.add).then_inc(s("centred"), 1)
                dve.wait_ge(s("gn_std"), j + 1)
                link(nc.vector.reciprocal(X, X))
                link(nc.vector.tensor_tensor(Y, Y, X, ALU.mult))
                link(nc.vector.tensor_scalar(Y, Y, param("rwkv_ln_w", j), param("rwkv_ln_b", j), ALU.mult, ALU.add))
                link(nc.vector.tensor_tensor(Y, Y, PT[:, 4 + j, PO:PW], ALU.add))
                dve.wait_ge(s("gn_gate"), j + 1)
                nc.vector.tensor_tensor(slices(Y), three(0), slices(Y), ALU.mult).then_inc(s("gated"), 1)
                dve.wait_ge(s("mix_hi"), 2 * j + 2)
                nc.vector.tensor_tensor(XS[:, j, 1], Y, XS[:, j, 0].bitcast(F32), ALU.subtract).then_inc(s("mix_ready"), 1)
                nc.vector.tensor_tensor(XS[:, 4 + j, 1], PT[:, 14 + j, PO:PW], XS[:, 4 + j, 0].bitcast(F32),
                                        ALU.subtract).then_inc(s("mix_ready"), 1)
            link(nc.vector.tensor_tensor(gate[:, 0], mod[:, 16:24], params("norm_post_mix").unsqueeze(2).broadcast_to([P, KD, 9]), ALU.mult))
            link(nc.vector.tensor_tensor(gate[:, 1], mod[:, 40:48], params("norm_post_ffn").unsqueeze(2).broadcast_to([P, KD, 9]), ALU.mult))
            norm_scale(gs2, "norm_pre_ffn", 32)
            wl = [0]

            def low_out(n):
                dve.wait_ge(w_hi, PC + n + 1)
                w_low(n % 2, n % 4).then_inc(w_lo, 1)

            def add_square(k, src, total, first):
                dve.wait_ge(s("sq_c"), first + k + 1)
                if k == 0:
                    nc.vector.tensor_copy(total, src).then_inc(s("sq_added"), 1)
                else:
                    dve.wait_ge(s("sq_added"), first + k)
                    nc.vector.tensor_tensor(total, total, src, ALU.add).then_inc(s("sq_added"), 1)

            low_out(0)
            low_out(1)
            for n in range(KD):
                if n + 2 < KD:
                    low_out(n + 2)
                add_square(n, sq2[:, n % 2], sqs[:], 0)
            dve.wait_ge(s("sq_added"), KD)
            nc.vector.memset(sc_mod[:, 0:1], 0.0).then_inc(s("sq_sum"), 1)
            dve.wait_ge(s("std2"), 1)
            link(nc.vector.reciprocal(rsC[:], rsC[:]))
            dve.wait_ge(s("x2_in"), 16)
            dve.wait_ge(s("out_out"), KD)
            for k in range(KD):
                link(nc.vector.tensor_tensor(MO[:, k], MO[:, k], rsC[:], ALU.mult))
                link(nc.vector.tensor_tensor(MO[:, k, T:N], MO[:, k, T:N], gate[:, 0, k, 1:9], ALU.mult))
                link(nc.vector.tensor_tensor(X2[:, k, T:N], X2[:, k, T:N], MO[:, k, T:N], ALU.add))
                nc.vector.scalar_tensor_tensor(X2[:, k, 0:T], MO[:, k, 0:T], gate[:, 0, k, 0:1], X2[:, k, 0:T], ALU.mult,
                                               ALU.add).then_inc(s("x1_ready"), 1)
                if k >= 1:
                    add_square(k - 1, sq2[:, (k - 1) % 2], sqs[:], KD)
            add_square(KD - 1, sq2[:, 1], sqs[:], KD)
            dve.wait_ge(s("sq_added"), 2 * KD)
            nc.vector.memset(sc_mod[:, 1:2], 0.0).then_inc(s("sq_sum"), 1)
            dve.wait_ge(s("std2"), 2)
            link(nc.vector.reciprocal(rsC[:], rsC[:]))

            def low3(slot, count):
                dve.wait_ge(s("w3_hi"), count)
                nc.vector.tensor_tensor(spl3[:, slot, 1], raw3[:, slot], spl3[:, slot, 0].bitcast(F32),
                                        ALU.subtract).then_inc(s("w3_lo"), 1)

            def low_h(k):
                dve.wait_ge(s("h2_hi"), k + 1)
                nc.vector.tensor_tensor(XS[:, k, 1], MO[:, k], XS[:, k, 0].bitcast(F32), ALU.subtract).then_inc(s("h2_lo"), 1)

            for m in range(3):
                low3(m, m + 1)
            for k in range(KD):
                link(nc.vector.tensor_tensor(MO[:, k], X2[:, k], rsC[:], ALU.mult))
                link(nc.vector.tensor_tensor(MO[:, k, T:N], MO[:, k, T:N], gs2[:, k, 1:9], ALU.mult))
                link(nc.vector.tensor_tensor(MO[:, k, T:N], MO[:, k, T:N], mod[:, 24 + k, 1:9], ALU.add))
                nc.vector.tensor_scalar(MO[:, k, 0:T], MO[:, k, 0:T], gs2[:, k, 0:1], mod[:, 24 + k, 0:1], ALU.mult,
                                        ALU.add).then_inc(s("h2_ready"), 1)
                if k >= 1:
                    low_h(k - 1)
            low_h(KD - 1)
            dve.wait_ge(s("x1_out"), 16 * KD)
            dve.wait_ge(s("h2_lo"), KD)
            link(nc.vector.memset(acc[:], 0.0))
            dve.wait_ge(s("conv_in"), 16)

            def taps(n):
                a = PARAM_AT["ffn_conv_w"][0] + n * 2 * FC
                return par[:, a:a + 2 * FC].unsqueeze(2).broadcast_to([P, 2 * FC, NS])

            cu = ftail[:, :, 0:NS]
            link(nc.vector.tensor_tensor(conv_add[:], conv_st[:, 0], taps(0), ALU.mult))
            link(nc.vector.tensor_tensor(cu, conv_st[:, 1], taps(1), ALU.mult))
            nc.vector.tensor_tensor(conv_add[:], conv_add[:], cu, ALU.add).then_inc(s("g_done"), 1)
            dve.wait_ge(s("g_done"), 1)

            def conv(c, chunk, count):
                dve.wait_ge(s("up_out"), count)
                z, u = Z[:, c], U[:, c]
                for n in (1, 0):
                    d = CW - 1 - n
                    a = PARAM_AT["ffn_conv_w"][0] + n * 2 * FC
                    link(nc.vector.scalar_tensor_tensor(z[:, d:T], u[:, 0:T - d], col(a, chunk), z[:, d:T],
                                                        ALU.mult, ALU.add))
                link(nc.vector.tensor_copy(at_chunk(ftail, chunk), u[:, T - 2:N]))
                nc.vector.tensor_tensor(z[:, T:N], z[:, T:N], at_chunk(conv_add, chunk), ALU.add
                                        ).then_inc(s("conv_done"), 1)

            def form(pair, slot):
                dve.wait_ge(s("silu_done"), pair + 1)
                dve.wait_ge(s("conv_done"), pair * 2 + 2)
                nc.vector.tensor_tensor(G[:], Z[:, 0], Z[:, 1], ALU.mult).then_inc(s("g_done"), 1)
                dve.wait_ge(s("g_hi"), pair + 1)
                nc.vector.tensor_tensor(act2[:, slot, 1], G[:], act2[:, slot, 0].bitcast(F32), ALU.subtract
                                        ).then_inc(s("g_lo"), 1)
                dve.wait_ge(s("g_lo"), pair + 1)

            low3(0, 4)
            conv(0, 0, 1)
            conv(1, FC, 2)
            form(0, 0)
            low3(1, 5)
            conv(0, 1, 3)
            low3(2, 6)
            low3(0, 7)
            conv(1, FC + 1, 4)
            form(1, 1)

            def add_down(i, last):
                for k in range(KD):
                    y = k + 1
                    dve.wait_ge(s("ffn_mm"), i * 12 - (8 if last else 7) + y)
                    bs = (y - 1) % 2 if last else y % 2
                    nc.vector.tensor_tensor(slices(acc[:, k]), slices(acc[:, k]), three(bs), ALU.add
                                            ).then_inc(s("down_out"), 1)

            def dve_body(i, last):
                low3(1, i * 6 + 2)
                conv(0, i * 2, i * 4 + 1)
                add_down(i, False)
                low3(2, i * 6 + 3)
                low3(0, i * 6 + 4)
                conv(1, i * 2 + FC, i * 4 + 2)
                form(i * 2, 0)
                low3(1, i * 6 + 5)
                conv(0, i * 2 + 1, i * 4 + 3)
                low3(2, i * 6 + 6)
                if not last:
                    low3(0, i * 6 + 7)
                conv(1, i * 2 + (FC + 1), i * 4 + 4)
                form(i * 2 + 1, 1)

            rounds, links = FC // 2 - 2, 12
            with dve.Fori(1, 1 + rounds) as i:
                past[0] = i * links - links
                before = mark[0]
                dve_body(i, False)
                assert mark[0] - before == links
            mark[0] += (rounds - 1) * links
            past[0] = 0
            dve_body(FC // 2 - 1, True)
            add_down(FC // 2, True)
            for k in range(KD):
                add_square(k, Z[:, k % 2], sqF[:], 2 * KD)
            dve.wait_ge(s("sq_added"), 3 * KD)
            nc.vector.memset(sc_mod[:, 2:3], 0.0).then_inc(s("sq_sum"), 1)
            dve.wait_ge(s("std2"), 3)
            link(nc.vector.reciprocal(G[:], G[:]))
            dve.wait_ge(s("x1_in"), 16)
            for k in range(KD):
                link(nc.vector.tensor_tensor(acc[:, k], acc[:, k], G[:], ALU.mult))
                link(nc.vector.tensor_tensor(acc[:, k, T:N], acc[:, k, T:N], gate[:, 1, k, 1:9], ALU.mult))
                link(nc.vector.tensor_tensor(acc[:, k, T:N], acc[:, k, T:N], X1[:, k, T:N], ALU.add))
                nc.vector.scalar_tensor_tensor(acc[:, k, 0:T], acc[:, k, 0:T], gate[:, 1, k, 0:1], X1[:, k, 0:T], ALU.mult,
                                               ALU.add).then_inc(s("y_ready"), 1)


def _consts():
    i = np.arange(P)
    c = {}
    c["ident"] = np.eye(P)
    c["swap"] = (i[:, None] == (i[None, :] ^ 32))
    c["headsum"] = (i[:, None] // HD == i[None, :] // HD)
    c["ones"] = np.ones((P, P))
    same = i[:, None] // C == i[None, :] // C
    c["cumsum"] = np.concatenate([same & (i[:, None] <= i[None, :]), same & (i[:, None] < i[None, :])], 1)
    t = np.arange(C)
    c["after"] = (i % C)[:, None] < t[None, :]
    c["upto"] = (i % C)[:, None] <= t[None, :]
    c["eye"] = (i % C)[:, None] == t[None, :]
    k = np.arange(2 * P)[None, :]
    c["window"] = np.where((k <= i[:, None] + P) & (k > i[:, None]), 0.0, MASKED)
    out = np.concatenate([np.asarray(c[n], np.float32).reshape(P, w) for n, w in CONSTS], 1)
    lv = []
    for b in (1,) + LEVELS:
        r, q = (i % C)[:, None], t[None, :]
        m = (r // (2 * b) == q // (2 * b)) & (r // b > q // b)
        lv += [m, (r // (2 * b) == q // (2 * b)) & (r // b < q // b)]
    return out, np.stack(lv, 1).astype(np.uint32)


def _rope(past):
    pos = np.concatenate([np.arange(T), np.full(NS, past)]).astype(np.float32)
    half = HD // 2
    inv = (10000.0 ** (-np.arange(half) / half)).astype(np.float32)
    ang = (pos[:, None] * inv[None, :]).astype(np.float32)
    cos, sin = np.cos(ang.astype(np.float64)).T, np.sin(ang.astype(np.float64)).T
    d = np.arange(P)
    sign = np.where(d % HD < half, -1.0, 1.0)[:, None]
    return np.stack([cos[d % half], sin[d % half] * sign], 1).astype(np.float32)


def _features(a):
    a = np.asarray(a)
    return np.moveaxis(a.reshape(a.shape[:-1] + (-1, P)), -1, 0)


def _tiles(w):
    k, n = w.shape[0] // P, w.shape[1] // P
    return np.ascontiguousarray(w.reshape(k, P, n, P).transpose(2, 1, 0, 3)).reshape(n, P, k * P)


def host_arrays(v):
    v = {k: np.asarray(a) for k, a in v.items()}
    a = {}
    x = np.concatenate([v["x_prompt"][0], v["x_sample"][:, 0]], 0)
    a["xT"] = np.ascontiguousarray(_features(x).transpose(0, 2, 1))
    c = np.concatenate([v["c_prompt"], v["c_sample"]], 0)
    a["cT"] = np.ascontiguousarray(_features(c).transpose(0, 2, 1))
    a["ada"] = _tiles(v["w_ada"][0])
    pair = np.concatenate([np.r_[j * HD:(j + 1) * HD, (4 + j) * HD:(5 + j) * HD] for j in range(4)])
    q0 = RC * P
    cols = np.concatenate([np.arange(q0), q0 + pair, np.arange(q0 + RW, PC * P)])
    a["w_in"] = _tiles(v["w_in"][0][:, cols])
    rows = np.concatenate([np.arange(RW), RW + pair])
    a["w_out"] = _tiles(v["w_out"][0][rows])
    a["up"] = _tiles(v["ffn_w_up"][0])
    a["down"] = np.ascontiguousarray(v["ffn_w_down"][0].reshape(FC, P, D))
    a["consts"], a["levels"] = _consts()
    a["rope"] = _rope(8192)
    pars = []
    for name, width in PARAMS:
        if name == "sinks":
            p = np.broadcast_to(v["swa_sinks"][0][None, :], (P, 8))
        elif name == "sink_rows":
            p = np.tile(v["swa_sinks"][0], 16)[:, None]
        elif name == "rwkv_r_k":
            p = _features(v[name].reshape(-1))
        elif name == "b_ada":
            p = _features(v[name][0])
        else:
            p = _features(v[name].reshape(-1))
        pars.append(p.reshape(P, width))
    a["params"] = np.ascontiguousarray(np.concatenate(pars, 1))
    a["shift_st"] = np.ascontiguousarray(_features(v["state_rwkv_shift"][0]).transpose(0, 2, 1))
    a["conv_st"] = np.ascontiguousarray(_features(v["state_ffn_conv"][0]).transpose(0, 2, 3, 1))
    a["lora"] = np.concatenate([v["rwkv_w_up"][0], v["rwkv_a_up"][0]], 0)
    a["g_up"] = np.ascontiguousarray(v["rwkv_g_up"][0])
    w = v["state_rwkv_wkv"][0].reshape(NS, 8, 2, 32, HD)
    a["wkv"] = np.ascontiguousarray(w.transpose(2, 0, 1, 3, 4)).reshape(P, 32 * HD)
    a["cache_k"] = np.ascontiguousarray(v["cache_swa_k"][0]).reshape(NS, P, P)
    a["cache_v"] = np.ascontiguousarray(v["cache_swa_v"][0]).reshape(NS, P, P)
    return a


OUTPUTS = [("o_y", [P, KD, N]), ("o_shift", [P, RC, NS + 1]), ("o_ks", [NS, P, P]), ("o_vs", [NS, P, P]),
           ("o_kvp", [P, 2, P]), ("o_wkvs", [P, 32, HD]), ("o_wkvp", [P, NJ, HD]), ("o_tail", [P, 2 * FC, NS + 2]),
           ("o_prev", [P, 2 * FC, NS])]


def unpack(r):
    y = np.ascontiguousarray(r["o_y"].transpose(2, 1, 0)).reshape(N, D)
    shift = np.ascontiguousarray(r["o_shift"].transpose(2, 1, 0)).reshape(NS + 1, RC * P)
    kvp = r["o_kvp"].transpose(1, 2, 0).reshape(2, 1, 1, P, 2, HD)
    wkvp = r["o_wkvp"].reshape(2, HD, NJ, HD).transpose(2, 0, 3, 1).reshape(1, 1, 2 * NJ, HD, HD)
    wkvs = r["o_wkvs"].reshape(2, NS, 8, 32, HD).transpose(1, 2, 0, 3, 4).reshape(1, NS, 8, HD, HD)
    tail = np.ascontiguousarray(r["o_tail"].transpose(2, 1, 0)).reshape(NS + 2, 2 * FF)
    prev = np.ascontiguousarray(r["o_prev"].transpose(2, 1, 0)).reshape(NS, 2 * FF)
    convs = np.stack([prev, tail[2:]], 1)[None]
    got = (y[None, :T], y[T:, None], wkvp, shift[:1][None], kvp[0], kvp[1], tail[None, None, :2], wkvs,
           shift[1:][None], r["o_ks"].reshape(1, NS, P, 2, HD), r["o_vs"].reshape(1, NS, P, 2, HD), convs)
    return tuple(np.ascontiguousarray(a) for a in got)


def kernel(**inputs):
    import concourse.bacc as bacc
    from concourse.bass_utils import run_bass_kernel_spmd

    nc = bacc.Bacc("TRN2", target_bir_lowering=False, num_devices=1)
    arrays = host_arrays(inputs)
    io = {n: nc.dram_tensor(n, a.shape, mybir.dt.from_np(a.dtype), kind="ExternalInput").ap()
          for n, a in arrays.items()}
    for n, shape in OUTPUTS:
        io[n] = nc.dram_tensor(n, shape, F32, kind="ExternalOutput").ap()
    build_program(nc, io)
    r = run_bass_kernel_spmd(nc, [arrays], core_ids=[0])
    return unpack(r.results[0])
```

```python
from contextlib import ExitStack

import numpy as np
import concourse.bass as bass
from concourse import mybir

F32 = mybir.dt.float32
F32R = mybir.dt.float32r
U32 = mybir.dt.uint32
ALU = mybir.AluOpType
ACT = mybir.ActivationFunctionType
AX = mybir.AxisListType

P = 128
D = 1024
KD = D // P
T = 1024
NS = 8
N = T + NS
SL = N // 3
HD = 64
RW = 512
NJ = RW // P
RC = 14
PC = 20
FF = 2816
FC = FF // P
CW = 3
C = 64
NCH = T // C
NT = T // P
PW = N + 2
PO = 2
KAPPA = float(np.exp(np.float32(-0.5)))
NORM_EPS = 1e-6
GN_EPS = 64e-5
MASKED = -1e30
NORM_FLOOR = 1e-24
SCALE = HD ** -0.5
LEVELS = (2, 4, 8, 16, 32)

CONSTS = [("ident", P), ("swap", P), ("headsum", P), ("ones", P), ("cumsum", 2 * P),
          ("after", C), ("upto", C), ("eye", C), ("window", 2 * P)]
PARAMS = [("b_ada", 48), ("norm_pre_mix", 8), ("norm_post_mix", 8), ("norm_pre_ffn", 8),
          ("norm_post_ffn", 8), ("rwkv_mu", RC), ("rwkv_w0", 4), ("rwkv_a0", 4), ("rwkv_k_k", 4),
          ("rwkv_k_a", 4), ("rwkv_r_k", 4), ("rwkv_ln_w", 4), ("rwkv_ln_b", 4),
          ("ffn_conv_w", CW * 2 * FC), ("ffn_conv_b", 2 * FC), ("sinks", 8), ("sink_rows", 1)]


def columns(table):
    at, n = {}, 0
    for name, width in table:
        at[name] = (n, n + width)
        n += width
    return at, n


CONST_AT, CONST_N = columns(CONSTS)
PARAM_AT, PARAM_N = columns(PARAMS)


def build_program(nc, io):
    ctx = ExitStack()
    with ctx:
        base = (nc.sbuf_base + 63) // 64 * 64
        end = nc.sbuf_base + nc.sbuf_bytes_remaining

        def sb(name, shape, dt, off):
            size = int(np.prod(shape[1:])) * 4
            assert base + off + size <= end, (name, off, size, end - base)
            return nc.alloc_sbuf_tensor_at(name, shape, dt, offset=base + off)

        def place(names, at):
            out = []
            for name, shape, dt in names:
                out.append(sb(name, shape, dt, at))
                at += (int(np.prod(shape[1:])) * 4 + 31) // 32 * 32
            return out, at

        def sem(name):
            return ctx.enter_context(nc.semaphore(name))

        (cst, lvl, par, mod, cT, cTs, shift_st, tail_shift, conv_add, lora, g_up, gs1, gs2, gate, Pc, eps,
         sc_mod), at = place([
            ("cst", [P, CONST_N], F32), ("lvl", [P, 2 * (len(LEVELS) + 1), C], U32), ("par", [P, PARAM_N], F32),
            ("mod", [P, 48, 9], F32), ("cT", [P, KD, 9], F32), ("cTs", [P, KD, 9], F32),
            ("shift_st", [P, RC, NS], F32), ("tail_shift", [P, RC, NS + 1], F32),
            ("conv_add", [P, 2 * FC, NS], F32), ("lora", [P, RW], F32), ("g_up", [P, RW], F32),
            ("gs1", [P, KD, 9], F32), ("gs2", [P, KD, 9], F32), ("gate", [P, 2, KD, 9], F32),
            ("Pc", [P, NCH], F32), ("eps", [P, 4], F32),
            ("sc_mod", [P, 4], F32)], 0)
        PT0 = (at + 63) // 64 * 64
        (PT,), REM = place([("PT", [P, PC, PW], F32)], PT0)
        (xT,), _ = place([("xT", [P, KD, N], F32)], PT0 + 12 * PW * 4)
        (XS,), RING = place([("XS", [P, KD, 2, N], F32R)], REM)
        (raw, spl), TMP = place([("raw", [P, 4, D], F32), ("spl", [P, 2, 2, D], F32R)], RING)
        (rs,), _ = place([("rs", [P, N], F32)], TMP)
        (ada_row,), _ = place([("ada_row", [9, 512], F32)], TMP + 8 * N)

        (rope, S4, PR, VA, Kf, Vf, KTs, kvrow, sS, sP, sPT, mx, nm, sk, den, rd), at = place([
            ("rope", [P, 2, N], F32), ("S4", [P, 3, 4, 2 * P], F32), ("PR", [P, 2, 4, 2, P], F32),
            ("VA", [P, NT, P], F32), ("Kf", [P, NS, P], F32), ("Vf", [P, NS, P], F32), ("KTs", [P, NS, P], F32),
            ("kvrow", [NS, 2, P], F32), ("sS", [P, 64], F32), ("sP", [64, P], F32), ("sPT", [P, 64], F32),
            ("mx", [P, 3, 4], F32), ("nm", [P, 3, 4], F32), ("sk", [P, 3, 4], F32), ("den", [P, 3, 4], F32),
            ("rd", [P, 3, 4], F32)], REM)
        assert at <= RING, (at, RING)
        (dif,), _ = place([("dif", [P, 2, N], F32)], TMP)
        (difP,), at = place([("difP", [P, 3, N], F32)], at)
        assert at <= RING, (at, RING)
        NU = 18
        (UNI, AB, BB, KB, WO, SMP), FB = place([
            ("UNI", [P, NU, NCH, C], F32), ("AB", [P, NCH, P], F32), ("BB", [P, NCH, P], F32), ("KB", [P, NCH, P], F32),
            ("WO", [P, NJ, C], F32), ("SMP", [P, NJ, 6, NS], F32)], REM)
        (Alpha, R, Aff, Beta, Tm, aTm, W1, bTm, NbT, Yc, kTm, TT, NkT, vTm, _, _, Ein, St) = (
            UNI[:, n] for n in range(NU))
        ALPHA_R_AFF, BETA_T, A_W1, B_NBT = UNI[:, 0:3], UNI[:, 3:5], UNI[:, 5:7], UNI[:, 7:9]
        TB = UNI[:, 14:16].rearrange("p n u c -> p (n u c)").rearrange("p (u s) -> p u s", s=P)
        (F0, F1), at = place([("F0", [P, N], F32), ("F1", [P, N], F32)], FB)
        F4, F3 = (UNI[:, n:n + 2].rearrange("p n u c -> p (n u c)")[:, 0:N] for n in (6, 9))
        F5, F6 = PT[:, 19, PO:PW], PT[:, 18, PO:PW]
        (SM48, OR), at2 = place([("SM48", [48, RW], F32), ("OR", [NS, RW], F32)], FB)
        assert at2 <= FB + 4 * N
        (V6, V32, Osm, sa), at2 = place([
            ("V6", [P, 6, HD], F32), ("V32", [P, 32], F32), ("Osm", [P, 32], F32), ("sa", [P, 32], F32)], FB + 4 * N)
        assert at2 <= at
        sTmp = AB[:].rearrange("p u c -> p (u c)").rearrange("p (v k) -> p v k", k=HD)
        sWKV = KB[:].rearrange("p u c -> p (u c)").rearrange("p (v k) -> p v k", k=HD)
        (MO, X2, sqs, sq2, rsC), at2 = place([
            ("MO", [P, KD, N], F32), ("X2", [P, KD, N], F32), ("sqs", [P, N], F32), ("sq2", [P, 2, N], F32),
            ("rsC", [P, N], F32)], PT0)
        assert at2 <= REM
        (acc, U, Z, G, act2, ftail, conv_st, sqF), at2 = place([
            ("acc", [P, KD, N], F32), ("U", [P, 2, N], F32), ("Z", [P, 2, N], F32), ("G", [P, N], F32),
            ("act2", [P, 2, 2, N], F32R), ("ftail", [P, 2 * FC, NS + 2], F32), ("conv_st", [P, 2, 2 * FC, NS], F32),
            ("sqF", [P, N], F32)], PT0)
        assert at2 <= REM
        (raw3, spl3), at2 = place([("raw3", [P, 3, D], F32), ("spl3", [P, 3, 2, D], F32R)], RING)
        (X1,), _ = place([("X1", [P, KD, N], F32)], REM)
        x1_dram = nc.dram_tensor("x1_dram", [P, KD, N], F32).ap()
        scr_a = nc.dram_tensor("scr_a", [6, NS, RW], F32).ap()
        scr_o = nc.dram_tensor("scr_o", [NS, 8, 2, 32], F32).ap()

        def hm(j):
            return PT[:, j, PO:PO + T].rearrange("p (u c) -> p u c", c=C)

        def unit(f):
            return f[:, 0:T].rearrange("p (u c) -> p u c", c=C)

        SGt = aTm.rearrange("p u c -> p (u c)").rearrange("p (n c) -> p n c", c=P)

        ps = ctx.enter_context(nc.psum_tensor("ps", [P, 8, 512], F32))

        def const(name):
            a, b = CONST_AT[name]
            return cst[:, a:b]

        def param(name, n):
            return par[:, PARAM_AT[name][0] + n:PARAM_AT[name][0] + n + 1]

        def params(name):
            return par[:, PARAM_AT[name][0]:PARAM_AT[name][1]]

        def slices(ap):
            return ap.rearrange("p (s t) -> p s t", s=3)

        def three(bank_set):
            return ps[:, 3 * bank_set:3 * bank_set + 3, 0:SL]

        def col(first, n):
            return par[:, bass.ds(n + first, 1)]

        def at_chunk(t, n):
            return t[:, bass.ds(n, 1), :].rearrange("p o c -> p (o c)")

        def one(ap, index):
            return ap[bass.ds(index, 1)].rearrange("o p n -> (o p) n")

        sqA = [PT[:, 0, 0:N], PT[:, 1, 0:N]]
        hA = [PT[:, 2, 0:N], PT[:, 3, 0:N]]

        ones, ident, bones = const("ones"), const("ident"), const("headsum")

        dve_step, act_step = sem("dve_step"), sem("act_step")
        consts_in, x_in, small_out = sem("consts_in"), sem("x_in"), sem("small_out")
        raw_in = [sem(f"raw_in{i}") for i in range(4)]
        zeros_set, silu_c, ada_used, mod_ready = sem("zeros_set"), sem("silu_c"), sem("ada_used"), sem("mod_ready")
        sq_ready, sumsq_ready, std_ready = sem("sq_ready"), sem("sumsq_ready"), sem("std_ready")
        sq_used = sem("sq_used")
        h_ready, h_hi, h_lo = sem("h_ready"), sem("h_hi"), sem("h_lo")
        w_hi, w_lo = sem("w_hi"), sem("w_lo")
        proj_ready, proj_out = sem("proj_ready"), sem("proj_out")
        S = {}
        LAST_LEVEL = len(LEVELS) - 1
        GROUPS = [("M", "aT"), ("MT", "NbT", "bT"), ("MkT", "NkT", "kT")]
        for n in range(len(LEVELS)):
            GROUPS += [(f"Y{n}",), (f"Z{n}",) if n < LAST_LEVEL else ("W1",), (f"ZT{n}",)]
        GROUPS += [("G", "H"), ("A", "RG"), ("E",), ("O",)]
        FIRST_BANK = {0: (0, 2), 1: (4, 0), 2: (4, 0), len(GROUPS) - 4: (0, 2), len(GROUPS) - 3: (0, 2),
                      len(GROUPS) - 2: (0, 1), len(GROUPS) - 1: (2, 3)}
        for n in range(3, len(GROUPS) - 4):
            FIRST_BANK[n] = (2 * n - 2) % 8, (2 * n - 1) % 8
        STEPS = [x for group in GROUPS for x in group]
        GROUP_OF = {x: n for n, group in enumerate(GROUPS) for x in group}
        ON_ACT = {"aT", "bT", "kT", "W1", "H", "E", "O"} | {f"Y{n}" for n in range(len(LEVELS))}
        dve_steps = [x for x in STEPS if x not in ON_ACT]
        act_steps = [x for x in STEPS if x in ON_ACT]

        def evacuated(name, pair, half):
            order = act_steps if name in ON_ACT else dve_steps
            return s("unit_act" if name in ON_ACT else "unit_dve"), (pair * len(order) + order.index(name)) * 2 + half + 1

        def computed(name, pair, half):
            return s("unit_mm"), (pair * len(GROUPS) + GROUP_OF[name]) * 2 + half + 1

        def y_copies(pair, level, half):
            return (pair * len(LEVELS) + level) * 2 + half + 1

        def t_copies(pair, level, half):
            return (pair * (len(LEVELS) + 1) + level) * 2 + half + 1

        WIDTH = {1: 1, 2: 2, 3: 4}

        def banks_of(group, half):
            first = FIRST_BANK[group][half]
            return range(first, first + WIDTH[len(GROUPS[group])])

        def results(name, half):
            n, x = GROUP_OF[name], GROUPS[GROUP_OF[name]].index(name)
            b = banks_of(n, half)
            all_of = ps[:, b[0]:b[-1] + 1, :].rearrange("p b (c s) -> p (b c) s", s=len(b) * C)
            return all_of[:, :, x * C:(x + 1) * C]

        def before_in(bank, group, half):
            for back in range(1, 2 * len(GROUPS) + 1):
                g = group * 2 + half - back
                n, h = g // 2 % len(GROUPS), g % 2
                if bank in banks_of(n, h):
                    return n, h, g < 0
            return None

        def overlapped(chain, prep):
            order = []
            for c in range(NCH):
                if chain:
                    order.append(("chain", c))
                if prep and c < len(PREP):
                    order.append((PREP[c], None))
            if prep:
                order.append(("ends", None))
            return order

        PREP = ["decay", "rate", "log", "norm", "cum", "kk", "bonus", "alpha", "beta", "kappa", "product", "values"]

        def s(name):
            if name not in S:
                S[name] = sem(name)
            return S[name]

        JOBS = 2 * FC + KD * (FC // 2)
        block = ctx.enter_context(nc.Block())
        ADA_A, ADA_B = 16, 32

        @block.sync
        def _(sp):
            def dma(dst, src, signal):
                return nc.sync.dma_start(dst, src).then_inc(signal, 16)

            dma(cT[:], io["cT"], s("c_in"))
            for n in range(4):
                dma(raw[:, n], io["ada"][n], raw_in[n])
            for i, (dst, src) in enumerate([(cst, "consts"), (lvl, "levels"), (par, "params"), (shift_st, "shift_st"),
                                            (lora, "lora"), (g_up, "g_up")]):
                dma(dst[:], io[src], consts_in)
            dma(xT[:], io["xT"], x_in)

            def load(tile, slot, used, count):
                sp.wait_ge(used, count)
                dma(raw[:, slot], tile, raw_in[slot])

            def tiles(name, first, count, used):
                with sp.Fori(0, (count - first) // 4) as i:
                    for j in range(4):
                        load(one(io[name], i * 4 + (first + j)), j, used, i * 4 + (first - 3 + j))

            tiles("ada", 4, ADA_A, ada_used)
            for n in range(4):
                load(io["w_in"][n], n, ada_used, ADA_A - 3 + n)
            tiles("w_in", 4, PC, w_lo)
            for n in range(4):
                load(io["ada"][ADA_A + n], n, w_lo, PC - 3 + n)
            sp.wait_ge(s("shift_saved"), 1)
            dma(io["o_shift"], tail_shift[:], small_out)
            dma(io["o_ks"][:, 0:P - 1, :], io["cache_k"][:, 1:P, :], s("cache_out"))
            dma(io["o_vs"][:, 0:P - 1, :], io["cache_v"][:, 1:P, :], s("cache_out"))
            sp.wait_ge(s("kvrow_ready"), 1)
            dma(io["o_ks"][:, P - 1, :], kvrow[:, 0, :], s("cache_out"))
            dma(io["o_vs"][:, P - 1, :], kvrow[:, 1, :], s("cache_out"))
            dma(io["o_kvp"], PT[:, 18:20, PW - NS - P:PW - NS], s("kvp_out"))
            sp.wait_ge(s("cache_out"), 64)
            dma(Kf[:], io["o_ks"].rearrange("b s d -> s b d"), s("cache_in"))
            dma(Vf[:], io["o_vs"].rearrange("b s d -> s b d"), s("cache_in"))
            with sp.Fori(0, (ADA_B - 4) // 4) as i:
                for j in range(4):
                    load(one(io["ada"], i * 4 + (ADA_A + 4 + j)), j, ada_used, i * 4 + (ADA_A + 1 + j))
            sp.wait_ge(s("sm48_ready"), 1)
            dma(scr_a.rearrange("q b c -> (q b) c"), SM48[:], s("scr_out"))
            sp.wait_ge(s("scr_out"), 16)
            sp.wait_ge(*computed("W1", NJ - 1, 1))
            dma(sWKV, io["wkv"].rearrange("p (v k) -> p v k", k=HD), s("wkv_in"))
            sp.wait_ge(*computed("H", NJ - 1, 1))
            for vh in range(2):
                dma(V6[64 * vh:64 * vh + 64], scr_a.rearrange("q b (h k) -> (b h) q k", k=HD), s("wkv_in"))
                dma(V32[64 * vh:64 * vh + 64], scr_a[5].rearrange("b (h u v) -> (b h) u v", u=2, v=32)[:, vh], s("wkv_in"))
            sp.wait_ge(s("sample_o"), 1)
            dma(io["o_wkvs"], sWKV, s("states_out"))
            for vh in range(2):
                dma(scr_o.rearrange("b h u v -> (b h) u v")[:, vh], Osm[64 * vh:64 * vh + 64], s("scro_out"))
            sp.wait_ge(s("scro_out"), 32)
            dma(OR[:], scr_o.rearrange("b h u v -> b (h u v)"), s("or_in"))
            sp.wait_ge(s("state_ready"), NJ * NCH)
            dma(io["o_wkvp"], WO[:], s("states_out"))
            sp.wait_ge(s("o_sample"), 1)
            sp.wait_ge(s("states_out"), 32)
            for n in range(4):
                dma(raw[:, n], io["w_out"][n], raw_in[n])
            for n in range(4, KD):
                sp.wait_ge(w_lo, PC + n - 3)
                dma(raw[:, n % 4], io["w_out"][n], raw_in[n % 4])
            sp.wait_ge(s("mix_ready"), 8)
            dma(X2[:], io["xT"], s("x2_in"))
            for k in range(KD):
                sp.wait_ge(s("x1_ready"), k + 1)
                dma(x1_dram[:, k], X2[:, k], s("x1_out"))
            sp.wait_ge(w_lo, PC + KD)
            sp.wait_ge(s("out_ready"), KD)

            def tile(src, slot, count):
                if count is not None:
                    sp.wait_ge(s("w3_lo"), count)
                dma(raw3[:, slot], src, s(f"raw3_in{slot}"))

            for m, c in enumerate((0, FC, 1, FC + 1)):
                tile(io["up"][c], m % 3, None if m < 3 else m - 2)
            sp.wait_ge(s("h2_lo"), KD)
            dma(conv_st[:], io["conv_st"], s("conv_in"))
            with sp.Fori(1, FC // 2) as i:
                for x, (name, off) in enumerate((("up", 0), ("down", -2), ("down", -1), ("up", FC), ("up", 1),
                                                 ("up", FC + 1))):
                    tile(one(io[name], i * 2 + off), (1 + x) % 3, i * 6 + (x - 4))
            for x in range(2):
                tile(io["down"][FC - 2 + x], (1 + x) % 3, 3 * FC + x - 4)
            sp.wait_ge(s("x1_out"), 16 * KD)
            sp.wait_ge(s("ffn_mm"), JOBS - KD)
            dma(X1[:], x1_dram, s("x1_in"))
            sp.wait_ge(s("conv_done"), 2 * FC)
            dma(io["o_tail"], ftail[:], small_out)
            dma(io["o_prev"], conv_st[:, 1], small_out)
            for k in range(KD):
                sp.wait_ge(s("y_ready"), k + 1)
                dma(io["o_y"][:, k], acc[:, k], s("y_out"))
            sp.wait_ge(s("y_out"), 16 * KD)
            sp.wait_ge(small_out, 16 * 3)
            sp.wait_ge(s("kvp_out"), 16)


        XB = (12, 18)

        @block.tensor
        def _(pe):
            def sum_squares(square_of, ready, used):
                for k in range(KD):
                    pe.wait_ge(ready, k + 1)
                    for t in range(3):
                        mm = nc.tensor.matmul(ps[:, 3 + t, 0:SL], ones, square_of(k)[:, t * SL:(t + 1) * SL],
                                              start=(k == 0), stop=(k == KD - 1))
                    mm.then_inc(used, 1)

            def ada_tile(n, bank, loads):
                pe.wait_ge(raw_in[n % 4], loads * 16)
                for x in range(2):
                    k = n % 4 * 2 + x
                    mm = nc.tensor.matmul(ps[0:9, bank, :], cTs[:, k, :], raw[:, n % 4, x * 512:(x + 1) * 512],
                                          start=(k == 0), stop=(k == KD - 1))
                mm.then_inc(ada_used, 1)

            def ada_turn(g, bank, at):
                pe.wait_ge(s("ada_row"), g + 1)
                for i in range(4):
                    mm = nc.tensor.transpose(ps[:, bank, at + i * 9:at + i * 9 + 9], ada_row[:, i * P:(i + 1) * P],
                                             ident[0:9, 0:9])
                mm.then_inc(s("ada_turned"), 1)

            def product(bank_set, w, x, x_ready=None):
                for k in range(KD):
                    if x_ready is not None:
                        pe.wait_ge(x_ready, k + 1)
                    for n, (a, b) in enumerate(((0, 0), (0, 1), (1, 0))):
                        for t in range(3):
                            mm = nc.tensor.matmul(ps[:, 3 * bank_set + t, 0:SL], w[:, a, k * P:(k + 1) * P],
                                                  x[:, k, b, t * SL:(t + 1) * SL],
                                                  start=(k == 0 and n == 0), stop=(k == KD - 1 and n == 2))
                return mm

            pe.wait_ge(silu_c, 1)
            for g in range(ADA_A // 4):
                for x in range(4):
                    ada_tile(4 * g + x, 6 + g % 2, g + 1)
                if g == 0:
                    pe.wait_ge(consts_in, 16 * 6)
                    sum_squares(lambda k: sqA[k % 2], sq_ready, sq_used)
                else:
                    ada_turn(g - 1, 0, (g - 1) * 36)
            ada_turn(ADA_A // 4 - 1, 0, ADA_A * 9 - 36)
            for n in range(4):
                pe.wait_ge(w_lo, n + 1)
                if n >= 2:
                    pe.wait_ge(proj_out, n - 1)
                product(n % 2, spl[:, n % 2], XS[:], h_lo if n == 0 else None).then_inc(proj_ready, 1)
            with pe.Fori(0, (PC - 4) // 2) as i:
                for j in range(2):
                    pe.wait_ge(w_lo, i * 2 + (5 + j))
                    pe.wait_ge(proj_out, i * 2 + (3 + j))
                    product(j, spl[:, j], XS[:]).then_inc(proj_ready, 1)
            pe.wait_ge(proj_out, PC)
            for n, c in enumerate((18, 14, 15, 16, 17)):
                if n >= 2:
                    pe.wait_ge(s("rotated"), n - 1)
                for t in range(3):
                    mm = nc.tensor.matmul(ps[:, 3 * (n % 2) + t, 0:SL], const("swap"),
                                          PT[:, c, PO + t * SL:PO + (t + 1) * SL], start=True, stop=True)
                mm.then_inc(s("swapped"), 1)
                if n in (0, 1):
                    if n == 1:
                        pe.wait_ge(s("v_turned"), 1)
                    for i in range(4):
                        mm = nc.tensor.transpose(ps[:, 6, i * P:(i + 1) * P],
                                                 PT[:, 19, PO + (4 * n + i) * P:PO + (4 * n + i + 1) * P], ident)
                    mm.then_inc(s("v_turns"), 1)
            pe.wait_ge(s("v_turned"), 2)
            pe.wait_ge(s("rotated"), 1)
            for i, c in enumerate((18, 19)):
                mm = nc.tensor.transpose(ps[0:NS, 6, i * P:(i + 1) * P], PT[:, c, PO + T:PW], ident)
            mm.then_inc(s("kvrow_turned"), 1)

            def scores(u):
                i, kv = u // 2, u % 2
                lo = P if i == 0 else 0
                h = slice(HD * kv, HD * kv + HD)
                if u >= 2:
                    pe.wait_ge(s("masked"), u - 1)
                for j in range(4):
                    mm = nc.tensor.matmul(ps[:, 2 * (u % 2) + j // 2, (j % 2) * 2 * P + lo:(j % 2 + 1) * 2 * P],
                                          PT[h, 14 + j, PO + i * P:PO + (i + 1) * P],
                                          PT[h, 18, PO + (i - 1) * P + lo:PO + (i + 1) * P], start=True, stop=True)
                mm.then_inc(s("scored"), 1)

            def turn_probs(u):
                i = u // 2
                pe.wait_ge(s("probs"), u + 1)
                if u >= 1:
                    pe.wait_ge(s("probs_turned"), u)
                for j in range(4):
                    for kt in range(2):
                        if i == 0 and kt == 0:
                            continue
                        mm = nc.tensor.transpose(ps[:, 4 + j // 2, ((j % 2) * 2 + kt) * P:((j % 2) * 2 + kt + 1) * P],
                                                 S4[:, u % 3, j, kt * P:(kt + 1) * P], ident)
                mm.then_inc(s("probs_turns"), 1)

            def values(u):
                i, kv = u // 2, u % 2
                pe.wait_ge(s("probs_turned"), u + 1)
                if u >= 1:
                    pe.wait_ge(s("mixed"), u)
                else:
                    pe.wait_ge(s("kvrow_ready"), 1)
                kts = (1,) if i == 0 else (0, 1)
                for j in range(4):
                    for kt in kts:
                        mm = nc.tensor.matmul(ps[HD * kv:HD * kv + HD, 6, j * P:(j + 1) * P],
                                              VA[:, i - 1 + kt, HD * kv:HD * kv + HD], PR[:, u % 2, j, kt, :],
                                              start=(kt == kts[0]), stop=(kt == 1))
                mm.then_inc(s("valued"), 1)

            pe.wait_ge(s("rotated"), 5)
            pe.wait_ge(mod_ready, 1)
            scores(0)
            scores(1)
            for u in range(2 * NT):
                if u + 2 < 2 * NT:
                    scores(u + 2)
                g = (ADA_A + 2 * u) // 4
                if u % 2 == 0 and u >= 2:
                    ada_turn(g - 1, 7, 0)
                turn_probs(u)
                if u % 2 == 0 and u >= 2:
                    pe.wait_ge(s("mod_added"), g - ADA_A // 4)
                for n in (2 * u, 2 * u + 1):
                    ada_tile(n, 7, (ADA_A + PC) // 4 + n // 4 + 1)
                values(u)
            ada_turn((ADA_A + ADA_B) // 4 - 1, 7, 0)
            pe.wait_ge(s("cache_in"), 32)
            pe.wait_ge(s("masked"), 2 * NT)
            for b in range(NS):
                mm = nc.tensor.transpose(ps[:, b // 4, (b % 4) * P:(b % 4 + 1) * P], Kf[:, b, :], ident)
            mm.then_inc(s("sk_turns"), 1)
            pe.wait_ge(s("sk_turned"), 1)
            for b in range(NS):
                for kv in range(2):
                    h = slice(HD * kv, HD * kv + HD)
                    mm = nc.tensor.matmul(ps[:, 2 + kv, b * 4:b * 4 + 4], KTs[h, b, :],
                                          PT[h, 14:18, PO + T + b], start=True, stop=True)
            mm.then_inc(s("s_scored"), 1)
            pe.wait_ge(s("s_copied"), 1)
            nc.tensor.transpose(ps[0:64, 0, 0:P], sS[:], ident).then_inc(s("s_turns"), 1)
            pe.wait_ge(s("s_probs"), 1)
            nc.tensor.transpose(ps[:, 2, 0:64], sP[:], ident[0:64, 0:64]).then_inc(s("s_turns"), 1)
            pe.wait_ge(s("s_turned"), 1)
            pe.wait_ge(s("mixed"), 2 * NT)
            for b in range(NS):
                for kv in range(2):
                    mm = nc.tensor.matmul(ps[HD * kv:HD * kv + HD, 6, b * 4:b * 4 + 4],
                                          Vf[:, b, HD * kv:HD * kv + HD], sPT[:, b * 8 + kv * 4:b * 8 + kv * 4 + 4],
                                          start=True, stop=True)
            mm.then_inc(s("s_valued"), 1)
            pe.wait_ge(s("s_mixed"), 1)

            def by_head_sum(bank, src):
                for t in range(3):
                    mm = nc.tensor.matmul(ps[:, bank + t, 0:SL], bones, src[:, t * SL:(t + 1) * SL],
                                          start=True, stop=True)
                return mm

            def prepare(piece, j):
                cols = slice(j * P, (j + 1) * P)
                if piece in ("decay", "rate"):
                    if piece == "rate":
                        pe.wait_ge(s("sig_decay"), j + 1)
                    elif j == 0:
                        pe.wait_ge(s("tanh_w"), 1)
                    else:
                        pe.wait_ge(s("v_tokens"), j)
                    h = slice(0, 64) if piece == "decay" else slice(64, P)
                    for t in range(3):
                        mm = nc.tensor.matmul(ps[:, 4 + t, 0:SL], lora[h, cols], PT[h, 12, PO + t * SL:PO + (t + 1) * SL],
                                              start=True, stop=True)
                    mm.then_inc(s("p_" + piece), 1)
                elif piece == "log":
                    pe.wait_ge(s("sig_rate"), j + 1)
                    for i in range(NT):
                        mm = nc.tensor.transpose(ps[:, 4 + i // 4, (i % 4) * P:(i % 4 + 1) * P],
                                                 F0[:, i * P:(i + 1) * P], ident)
                    mm.then_inc(s("p_sgt"), 1)
                elif piece == "norm":
                    pe.wait_ge(s("sgt_copied"), j + 1)
                    by_head_sum(4, F3).then_inc(s("p_norm"), 1)
                elif piece == "cum":
                    pe.wait_ge(s("k_floor"), j + 1)
                    for m in range(4):
                        if m == 3:
                            pe.wait_ge(s("decays"), j * 4 + 1)
                        for i in (2 * m, 2 * m + 1):
                            mm = nc.tensor.matmul(ps[:, 4 + m % 3, (i % 2) * 2 * P:(i % 2 + 1) * 2 * P], SGt[:, i],
                                                  const("cumsum"), start=True, stop=True)
                        mm.then_inc(s("p_cum"), 1)
                elif piece == "bonus":
                    pe.wait_ge(s("decays"), 4 * (j + 1))
                    pe.wait_ge(s("rkk"), j + 1)
                    by_head_sum(4, F0).then_inc(s("p_bonus"), 1)
                elif piece == "values":
                    pe.wait_ge(s("bonus"), j + 1)
                    for c in range(NCH):
                        for hh in range(2):
                            h = slice(HD * hh, HD * hh + HD)
                            mm = nc.tensor.matmul(ps[h, 4 + c // 8, (c % 8) * C:(c % 8 + 1) * C],
                                                  PT[h, 8 + j, PO + c * C:PO + (c + 1) * C], ident[h, h],
                                                  start=True, stop=True)
                    mm.then_inc(s("p_values"), 1)

            def chunks(j):
                def tiles_of(half):
                    for c in range(8 * half, 8 * half + 8):
                        for hh in range(2):
                            yield slice(HD * hh, HD * hh + HD), c

                def free_banks(group, half):
                    for bank in banks_of(group, half):
                        n, h, earlier = before_in(bank, group, half)
                        if not earlier or j >= 1:
                            for name in GROUPS[n]:
                                pe.wait_ge(*evacuated(name, j - earlier, h))

                def step(name, half, *terms):
                    free_banks(GROUP_OF[name], half)
                    for h, c in tiles_of(half):
                        out = results(name, half)[h, c % 8]
                        for i, (a, b) in enumerate(terms):
                            mm = nc.tensor.matmul(out, a[h, c], b[h, c], start=(i == 0), stop=(i == len(terms) - 1))
                    mm.then_inc(s("unit_mm"), 1)

                def both(name, half, stationary, moving):
                    group = GROUP_OF[name]
                    free_banks(group, half)
                    bank = banks_of(group, half)[0]
                    flat = moving.rearrange("p u c -> p (u c)")
                    for c in range(8 * half, 8 * half + 8):
                        n = C if c % 8 == 7 else 2 * C
                        mm = nc.tensor.matmul(ps[:, bank, c % 8 * C:c % 8 * C + n], stationary[:, c],
                                              flat[:, c * C:c * C + n], start=True, stop=True)
                    mm.then_inc(s("unit_mm"), 1)

                def wide(name, half, stationary, moving):
                    group = GROUP_OF[name]
                    free_banks(group, half)
                    n, first = len(GROUPS[group]), banks_of(group, half)[0]
                    per = 8 // WIDTH[n]
                    for c in range(8 * half, 8 * half + 8):
                        at = c % per * (C * 8 // per)
                        mm = nc.tensor.matmul(ps[:, first + c % 8 // per, at:at + n * C], stationary[:, c],
                                              moving[:, :, c], start=True, stop=True)
                    mm.then_inc(s("unit_mm"), 1)

                pe.wait_ge(s("alpha_bd"), j + 1)
                pe.wait_ge(s("beta_bd"), j + 1)
                pe.wait_ge(s("eyes"), j + 1)
                for half in range(2):
                    wide("M", half, AB, BETA_T)
                pe.wait_ge(s("ends_ready"), j + 1)
                pe.wait_ge(s("v_tokens"), j + 1)
                if j == NJ - 1:
                    pe.wait_ge(s("sm48_ready"), 1)
                for half in range(2):
                    wide("MT", half, BB, ALPHA_R_AFF)
                for half in range(2):
                    wide("MkT", half, KB, ALPHA_R_AFF)
                for n in range(len(LEVELS)):
                    before = "MT" if n == 0 else f"ZT{n - 1}"
                    for half in range(2):
                        pe.wait_ge(*evacuated("MT", j, half))
                        pe.wait_ge(*evacuated("M" if n == 0 else f"Z{n - 1}", j, half))
                        both(f"Y{n}", half, BB, Tm)
                    for half in range(2):
                        if n < LAST_LEVEL:
                            pe.wait_ge(*evacuated(f"Y{n}", j, half))
                            pe.wait_ge(*evacuated(before, j, half))
                            pe.wait_ge(s("t_first"), t_copies(j, n, half))
                            both(f"Z{n}", half, TB, Yc)
                        else:
                            pe.wait_ge(*evacuated("MkT", j, half))
                            both("W1", half, KB, vTm)
                    for half in range(2):
                        pe.wait_ge(*evacuated(f"Y{n}", j, half))
                        pe.wait_ge(s("y_second"), y_copies(j, n, half))
                        pe.wait_ge(*evacuated(before, j, half))
                        both(f"ZT{n}", half, AB, TT)
                for half in range(2):
                    pe.wait_ge(*evacuated(f"ZT{LAST_LEVEL}", j, half))
                    pe.wait_ge(s("t_first"), t_copies(j, LAST_LEVEL + 1, half))
                    pe.wait_ge(*evacuated("W1", j, half))
                    wide("G", half, TB, A_W1)
                for half in range(2):
                    pe.wait_ge(*evacuated("G", j, half))
                    wide("A", half, BB, B_NBT)
                for half in range(2):
                    pe.wait_ge(*evacuated("H", j, half))
                    step("E", half, (bTm, hm(j)), (kTm, vTm))

                def chain(c):
                    if c >= 1:
                        pe.wait_ge(s("state_ready"), j * NCH + c)
                        for hh in range(2):
                            h = slice(HD * hh, HD * hh + HD)
                            mm = nc.tensor.matmul(ps[h, 7, 0:C], Aff[h, c], St[h, c], start=True, stop=True)
                        mm.then_inc(s("state_mm"), 1)
                    if c % 8 == 0:
                        free_banks(GROUP_OF["O"], c // 8)
                    if c == 0:
                        pe.wait_ge(*evacuated("RG", j, 1))
                    for hh in range(2):
                        h = slice(HD * hh, HD * hh + HD)
                        out = results("O", c // 8)[h, c % 8]
                        nc.tensor.matmul(out, hm(j)[h, c], NbT[h, c], start=True, stop=False)
                        mm = nc.tensor.matmul(out, vTm[h, c], NkT[h, c], start=False, stop=(c == 0))
                        if c >= 1:
                            mm = nc.tensor.matmul(out, St[h, c], R[h, c], start=False, stop=True)
                    if c % 8 == 7:
                        mm.then_inc(s("unit_mm"), 1)

                return chain

            chain = None
            for j in range(NJ + 1):
                for piece, c in overlapped(chain is not None, j < NJ):
                    if piece == "chain":
                        chain(c)
                    else:
                        prepare(piece, j)
                if j == NJ - 1:
                    pe.wait_ge(s("smp_ready"), NJ)
                    for x in range(NJ):
                        mm = nc.tensor.transpose(ps[0:48, 6, x * P:(x + 1) * P], SMP[:, x].rearrange("p q b -> p (q b)"),
                                                 ident)
                    mm.then_inc(s("smp_turns"), 1)
                if j < NJ:
                    chain = chunks(j)
            pe.wait_ge(s("or_in"), 16)
            for j in range(NJ):
                mm = nc.tensor.transpose(ps[:, 5, j * NS:(j + 1) * NS], OR[:, j * P:(j + 1) * P], ident[0:NS, 0:NS])
            mm.then_inc(s("or_turns"), 1)

            pe.wait_ge(s("o_sample"), 1)
            pe.wait_ge(*evacuated("O", NJ - 1, 1))
            pe.wait_ge(s("sig_g"), 1)
            for j in range(NJ):
                if j >= 1:
                    pe.wait_ge(s("gated"), j)
                by_head_sum(0, PT[:, 8 + j, PO:PW]).then_inc(s("gn_mean"), 1)
                pe.wait_ge(s("gn_square"), j + 1)
                by_head_sum(3, PT[:, XB[j % 2], PO:PW]).then_inc(s("gn_var"), 1)
                for t in range(3):
                    mm = nc.tensor.matmul(ps[:, t, 0:SL], g_up[:, j * P:(j + 1) * P],
                                          PT[:, 13, PO + t * SL:PO + (t + 1) * SL], start=True, stop=True)
                mm.then_inc(s("gn_gate"), 1)
            pe.wait_ge(s("mix_ready"), 8)
            pe.wait_ge(s("gated"), NJ)
            for n in range(KD):
                pe.wait_ge(w_lo, PC + n + 1)
                if n >= 2:
                    pe.wait_ge(s("out_out"), n - 1)
                product(n % 2, spl[:, n % 2], XS[:]).then_inc(s("out_ready"), 1)
            for n in range(2):
                pe.wait_ge(s("sq_sum"), n + 1)
                pe.wait_ge(s("out_out"), KD)
                for t in range(3):
                    mm = nc.tensor.matmul(ps[:, 3 * n + t, 0:SL], ones, sqs[:, t * SL:(t + 1) * SL],
                                          start=True, stop=True)
                mm.then_inc(s("sq_total"), 1)
            pe.wait_ge(s("std2"), 2)

            def up(i, x, off, w3, waits):
                pe.wait_ge(s("w3_lo"), w3)
                for name, count in waits:
                    pe.wait_ge(s(name), count)
                product(off % 2, spl3[:, (1 + x) % 3], XS[:]).then_inc(s("ffn_mm"), 1)

            def down(i, w3):
                pe.wait_ge(s("w3_lo"), w3)
                pe.wait_ge(s("g_lo"), i * 2)
                for k in range(KD):
                    y = k + 1
                    if y == 1:
                        pe.wait_ge(s("up_out"), i * 4)
                    elif y == 2:
                        pe.wait_ge(s("up_out"), up2(i))
                    else:
                        pe.wait_ge(s("down_out"), i * 8 + (y - 10))
                    first = down_slot(i)
                    for f in range(2):
                        w = spl3[:, (first + f) % 3]
                        for n, (a, b) in enumerate(((0, 0), (0, 1), (1, 0))):
                            for t in range(3):
                                mm = nc.tensor.matmul(ps[:, 3 * (down_set(i, y)) + t, 0:SL], w[:, a, k * P:(k + 1) * P],
                                                      act2[:, f, b, t * SL:(t + 1) * SL],
                                                      start=(f == 0 and n == 0), stop=(f == 1 and n == 2))
                    mm.then_inc(s("ffn_mm"), 1)

            LAST = FC // 2

            def is_last(i):
                return isinstance(i, int) and i == LAST

            def up2(i):
                return i * 4 if is_last(i) else i * 4 + 1

            def down_slot(i):
                return 1 if is_last(i) else 2

            def down_set(i, y):
                return (y - 1) % 2 if is_last(i) else y % 2

            pe.wait_ge(s("h2_lo"), KD)
            for m in range(4):
                pe.wait_ge(s("w3_lo"), m + 1)
                if m >= 2:
                    pe.wait_ge(s("up_out"), m - 1)
                product(m % 2, spl3[:, m % 3], XS[:]).then_inc(s("ffn_mm"), 1)
            with pe.Fori(1, LAST) as i:
                up(i, 0, 0, i * 6 - 1, [("up_out", i * 4 - 1)])
                down(i, i * 6 + 1)
                up(i, 3, 9, i * 6 + 2, [("down_out", i * 8 - 1)])
                up(i, 4, 10, i * 6 + 3, [("down_out", i * 8)])
                up(i, 5, 11, i * 6 + 4, [("up_out", i * 4 + 2)])
            down(LAST, 3 * FC)
            pe.wait_ge(s("sq_sum"), 3)
            pe.wait_ge(s("down_out"), KD * LAST)
            for t in range(3):
                mm = nc.tensor.matmul(ps[:, t, 0:SL], ones, sqF[:, t * SL:(t + 1) * SL], start=True, stop=True)
            mm.then_inc(s("sq_total"), 1)

        @block.scalar
        def _(act):
            mark = [0]

            def link(ins):
                mark[0] += 1
                ins.then_inc(act_step, 1)
                act.wait_ge(act_step, mark[0])

            def inverse_root(dst, src, bias, scale):
                link(nc.scalar.activation(dst, src, ACT.Ln, bias=bias, scale=scale))
                return nc.scalar.activation(dst, dst, ACT.Exp, scale=-0.5)

            act.wait_ge(s("c_in"), 16)
            nc.scalar.activation(cTs[:], cT[:], ACT.Silu).then_inc(silu_c, 1)
            act.wait_ge(x_in, 16)

            def ada_out(g, bank):
                act.wait_ge(ada_used, 4 * (g + 1))
                if g >= 1:
                    act.wait_ge(s("ada_turned"), g)
                nc.scalar.activation(ada_row[:], ps[0:9, bank, :], ACT.Copy).then_inc(s("ada_row"), 1)

            for k in range(KD):
                if k >= 2:
                    act.wait_ge(sq_used, k - 1)
                nc.scalar.activation(sqA[k % 2], xT[:, k], ACT.Square).then_inc(sq_ready, 1)
            act.wait_ge(zeros_set, 1)
            act.wait_ge(sq_used, KD)
            inverse_root(slices(rs[:]), three(1), eps[:, 0:1], 1.0 / D).then_inc(std_ready, 1)
            for g in range(ADA_A // 4):
                ada_out(g, 6 + g % 2)
            def whi(slot2, slot4):
                nc.scalar.activation(spl[:, slot2, 0], raw[:, slot4], ACT.Copy).then_inc(w_hi, 1)
            for n in range(2):
                act.wait_ge(raw_in[n], (ADA_A // 4 + 1) * 16)
                whi(n, n)
            for k in range(KD):
                act.wait_ge(h_ready, k + 1)
                nc.scalar.activation(XS[:, k, 0], hA[k % 2], ACT.Copy).then_inc(h_hi, 1)

            def evac(n, bank_set):
                nc.scalar.activation(PT[:, bass.ds(n, 1), PO:PW].rearrange("p o (s t) -> p (o s) t", s=3),
                                     three(bank_set), ACT.Copy).then_inc(proj_out, 1)

            for n in range(2):
                act.wait_ge(proj_ready, n + 1)
                act.wait_ge(raw_in[n + 2], (ADA_A // 4 + 1) * 16)
                whi(n, n + 2)
                evac(n, n)
            with act.Fori(0, (PC - 4) // 4) as i:
                for j in range(4):
                    act.wait_ge(proj_ready, i * 4 + (3 + j))
                    act.wait_ge(raw_in[j], (i + (ADA_A // 4 + 2)) * 16)
                    whi(j % 2, j)
                    evac(i * 4 + (2 + j), j % 2)
            for n in range(PC - 2, PC):
                act.wait_ge(proj_ready, n + 1)
                evac(n, n % 2)

            nc.scalar.dma_start(rope[:], io["rope"]).then_inc(s("rope_in"), 16)
            for n in range(2):
                act.wait_ge(s("v_turns"), n + 1)
                nc.scalar.activation(VA[:, 4 * n:4 * n + 4, :], ps[:, 6, :].rearrange("p (i c) -> p i c", c=P),
                                     ACT.Copy).then_inc(s("v_turned"), 1)
            act.wait_ge(s("kvrow_turned"), 1)
            nc.scalar.activation(kvrow[:], ps[0:NS, 6, 0:2 * P].rearrange("p (i c) -> p i c", c=P),
                                 ACT.Copy).then_inc(s("kvrow_ready"), 1)

            def exps(u):
                i = u // 2
                lo = P if i == 0 else 0
                act.wait_ge(s("maxed"), u + 1)
                for j in range(4):
                    nc.scalar.activation(S4[:, u % 3, j, lo:], S4[:, u % 3, j, lo:], ACT.Exp, bias=nm[:, u % 3, j:j + 1],
                                         accum_out=den[:, u % 3, j:j + 1])
                nc.scalar.activation(sk[:, u % 3, :], sk[:, u % 3, :], ACT.Exp).then_inc(s("exped"), 1)

            def move(u):
                i, kv = u // 2, u % 2
                act.wait_ge(s("probs_turns"), u + 1)
                kt = slice(1, 2) if i == 0 else slice(0, 2)
                nc.scalar.activation(PR[:, u % 2, :, kt, :],
                                     ps[:, 4:6, :].rearrange("p b (j k c) -> p (b j) k c", k=2, c=P)[:, :, kt, :],
                                     ACT.Copy).then_inc(s("probs_turned"), 1)
                act.wait_ge(s("valued"), u + 1)
                nc.scalar.activation(PT[HD * kv:HD * kv + HD, 14:18, PO + i * P:PO + (i + 1) * P],
                                     ps[HD * kv:HD * kv + HD, 6, :].rearrange("p (j c) -> p j c", c=P),
                                     ACT.Copy).then_inc(s("mixed"), 1)

            for u in range(2 * NT):
                exps(u)
                if u >= 1:
                    move(u - 1)
                if u >= 2 and u % 2 == 0:
                    ada_out(ADA_A // 4 + u // 2 - 1, 7)
            move(2 * NT - 1)
            ada_out((ADA_A + ADA_B) // 4 - 1, 7)
            act.wait_ge(s("sk_turns"), 1)
            nc.scalar.activation(KTs[:], ps[:, 0:2, :].rearrange("p b (i c) -> p (b i) c", c=P),
                                 ACT.Copy).then_inc(s("sk_turned"), 1)
            act.wait_ge(s("s_scored"), 1)
            nc.scalar.activation(sS[:].rearrange("p (b v g) -> p v b g", v=2, g=4),
                                 ps[:, 2:4, 0:32].rearrange("p v (b g) -> p v b g", g=4), ACT.Copy).then_inc(s("s_copied"), 1)
            act.wait_ge(s("s_maxed"), 1)
            nc.scalar.activation(sP[:], sP[:], ACT.Exp, bias=nm[0:64, 0, 0:1], accum_out=den[0:64, 0, 0:1])
            nc.scalar.activation(sk[0:64, 0, 0:1], sk[0:64, 0, 0:1], ACT.Exp).then_inc(s("s_exped"), 1)
            act.wait_ge(s("s_turns"), 2)
            nc.scalar.activation(sPT[:], ps[:, 2, 0:64], ACT.Copy).then_inc(s("s_turned"), 1)
            act.wait_ge(s("s_valued"), 1)
            nc.scalar.activation(PT[:, 14:18, PO + T:PW], ps[:, 6, 0:32].rearrange("p (b j) -> p j b", j=4),
                                 ACT.Copy).then_inc(s("s_mixed"), 1)

            act.wait_ge(s("shifted"), RC)
            nc.scalar.activation(PT[0:64, 12, PO:PW], PT[0:64, 12, PO:PW], ACT.Tanh).then_inc(s("tanh_w"), 1)
            nc.scalar.activation(PT[:, 13, PO:PW], PT[:, 13, PO:PW], ACT.Sigmoid).then_inc(s("sig_g"), 1)
            def prepare(piece, j):
                if piece == "decay":
                    if j >= 1:
                        act.wait_ge(*computed("E", j - 1, 1))
                        act.wait_ge(s("smp_ready"), j)
                    act.wait_ge(s("p_decay"), j + 1)
                    nc.scalar.activation(slices(F0[:]), ps[:, 4:7, 0:SL], ACT.Sigmoid, bias=param("rwkv_w0", j)
                                         ).then_inc(s("sig_decay"), 1)
                elif piece == "rate":
                    act.wait_ge(s("p_rate"), j + 1)
                    nc.scalar.activation(slices(F1[:]), ps[:, 4:7, 0:SL], ACT.Sigmoid, bias=param("rwkv_a0", j)
                                         ).then_inc(s("sig_rate"), 1)
                elif piece == "log":
                    nc.scalar.activation(F3, PT[:, 4 + j, PO:PW], ACT.Square, scale=param("rwkv_k_k", j)
                                         ).then_inc(s("k_square"), 1)
                    act.wait_ge(s("p_sgt"), j + 1)
                    nc.scalar.activation(SGt, ps[:, 4:6, :].rearrange("p b (i c) -> p (b i) c", c=P),
                                         ACT.Copy).then_inc(s("sgt_copied"), 1)
                elif piece == "norm":
                    act.wait_ge(s("k_floor"), j + 1)
                    inverse_root(F3, F3, eps[:, 2:3], 1.0).then_inc(s("k_norm"), 1)
                elif piece == "cum":
                    act.wait_ge(s("sig_decay"), j + 1)
                    nc.scalar.activation(SMP[:, j, 1, :], F0[:, T:N], ACT.Exp, scale=-KAPPA)
                    for m in range(4):
                        act.wait_ge(s("p_cum"), 4 * j + m + 1)
                        cum = ps[:, 4 + m % 3, :].rearrange("p (i x t) -> p i x t", x=2, t=P)
                        q = slice(2 * m * P, (2 * m + 2) * P)
                        for f, x, sign in ((F5, 0, -1), (F6, 0, 1), (Alpha.rearrange("p u c -> p (u c)"), 1, -1)):
                            ins = nc.scalar.activation(f[:, q].rearrange("p (i t) -> p i t", t=P), cum[:, :, x, :],
                                                       ACT.Exp, scale=sign * KAPPA)
                        ins.then_inc(s("decays"), 1)
                elif piece == "ends":
                    act.wait_ge(s("alpha"), j + 1)
                    if j == 0:
                        act.wait_ge(s("bd_zero"), 4)
                    for h in (slice(0, HD), slice(HD, P)):
                        ins = nc.scalar.activation(AB[h, :, h], Alpha[h], ACT.Copy)
                    ins.then_inc(s("alpha_bd"), 1)
                    act.wait_ge(s("p_values"), j + 1)
                    if j >= 1:
                        act.wait_ge(*computed("O", j - 1, 1))
                    nc.scalar.activation(vTm, ps[:, 4:6, :].rearrange("p b (i c) -> p (b i) c", c=C),
                                         ACT.Copy).then_inc(s("v_tokens"), 1)

            def evacuate(name, j, half):
                u = slice(8 * half, 8 * half + 8)
                src = results(name, half)
                act.wait_ge(*computed(name, j, half))
                for other in GROUPS[GROUP_OF[name]]:
                    if other not in ON_ACT:
                        act.wait_ge(*evacuated(other, j, half))
                if name[0] == "Y":
                    nc.scalar.activation(Yc[:, u], src, ACT.Copy).then_inc(s("y_compact"), 1)
                    nc.scalar.activation(AB[0:HD, u, 0:HD], src[0:HD], ACT.Copy).then_inc(s("unit_act"), 1)
                    return
                if name == "O":
                    dst = PT[:, 8 + j, PO:PO + T].rearrange("p (u c) -> p u c", c=C)
                else:
                    dst = {"aT": aTm, "bT": bTm, "kT": kTm, "W1": W1, "H": hm(j), "E": Ein}[name]
                nc.scalar.activation(dst[:, u], src, ACT.Copy).then_inc(s("unit_act"), 1)

            def first_head(j, level, half):
                u = slice(8 * half, 8 * half + 8)
                act.wait_ge(*evacuated("MT" if level == 0 else f"ZT{level - 1}", j, half))
                nc.scalar.activation(TB[0:HD, u, 0:HD], TT[0:HD, u], ACT.Copy).then_inc(s("t_first"), 1)

            for j in range(NJ + 1):
                for piece, c in overlapped(j >= 1, j < NJ):
                    if piece != "chain":
                        prepare(piece, j)
                    elif c % 8 == 7:
                        evacuate("O", j - 1, c // 8)
                if j == NJ - 1:
                    act.wait_ge(s("smp_turns"), 1)
                    act.wait_ge(s("bonus"), NJ)
                    nc.scalar.activation(SM48[:], ps[0:48, 6, :], ACT.Copy).then_inc(s("sm48_ready"), 1)
                if j < NJ:
                    for name in [x for x in STEPS[:-1] if x in ON_ACT or x == "MT" or x[:2] == "ZT"]:
                        for half in range(2):
                            if name in ON_ACT:
                                evacuate(name, j, half)
                            else:
                                first_head(j, 0 if name == "MT" else int(name[2:]) + 1, half)
            act.wait_ge(s("or_turns"), 1)
            nc.scalar.activation(PT[:, 8:12, PO + T:PW], ps[:, 5, 0:4 * NS].rearrange("p (j b) -> p j b", b=NS),
                                 ACT.Copy).then_inc(s("o_sample"), 1)
            for j in range(NJ):
                X = PT[:, XB[j % 2], PO:PW]
                act.wait_ge(s("centred"), j + 1)
                nc.scalar.activation(X, PT[:, j, PO:PW], ACT.Square).then_inc(s("gn_square"), 1)
                act.wait_ge(s("gn_var"), j + 1)
                inverse_root(slices(X), three(1), eps[:, 1:2], 1.0 / HD).then_inc(s("gn_std"), 1)
                act.wait_ge(s("gated"), j + 1)
                if j == 0:
                    act.wait_ge(s("states_out"), 32)
                nc.scalar.activation(XS[:, j, 0], PT[:, j, PO:PW], ACT.Copy).then_inc(s("mix_hi"), 1)
                nc.scalar.activation(XS[:, 4 + j, 0], PT[:, 14 + j, PO:PW], ACT.Copy).then_inc(s("mix_hi"), 1)
            def whi_out(n):
                act.wait_ge(raw_in[n % 4], ((ADA_A + ADA_B + PC + n) // 4 + 1) * 16)
                whi(n % 2, n % 4)

            whi_out(0)
            whi_out(1)
            for n in range(KD):
                act.wait_ge(s("out_ready"), n + 1)
                if n + 2 < KD:
                    whi_out(n + 2)
                if n >= 2:
                    act.wait_ge(s("sq_added"), n - 1)
                nc.scalar.activation(slices(sq2[:, n % 2]), three(n % 2), ACT.Square).then_inc(s("sq_c"), 1)
                nc.scalar.activation(slices(MO[:, n]), three(n % 2), ACT.Copy).then_inc(s("out_out"), 1)
            act.wait_ge(s("sq_total"), 1)
            inverse_root(slices(rsC[:]), three(0), eps[:, 0:1], 1.0 / D).then_inc(s("std2"), 1)
            for k in range(KD):
                act.wait_ge(s("x1_ready"), k + 1)
                if k >= 2:
                    act.wait_ge(s("sq_added"), KD + k - 1)
                nc.scalar.activation(sq2[:, k % 2], X2[:, k], ACT.Square).then_inc(s("sq_c"), 1)
            act.wait_ge(s("sq_total"), 2)
            inverse_root(slices(rsC[:]), three(1), eps[:, 0:1], 1.0 / D).then_inc(s("std2"), 1)

            def w3(m_slot, in_count, used):
                act.wait_ge(s(f"raw3_in{m_slot}"), in_count * 16)
                if used is not None:
                    act.wait_ge(s("ffn_mm"), used)
                nc.scalar.activation(spl3[:, m_slot, 0], raw3[:, m_slot], ACT.Copy).then_inc(s("w3_hi"), 1)

            for m in range(3):
                w3(m, 1, None)
            for k in range(KD):
                act.wait_ge(s("h2_ready"), k + 1)
                nc.scalar.activation(XS[:, k, 0], MO[:, k], ACT.Copy).then_inc(s("h2_hi"), 1)

            def evac_up(c, chunk, job, bank_set, before):
                act.wait_ge(s("ffn_mm"), job)
                act.wait_ge(s("g_done"), before)
                nc.scalar.activation(slices(U[:, c]), three(bank_set), ACT.Copy)
                a = PARAM_AT["ffn_conv_w"][0] + 2 * 2 * FC
                b = PARAM_AT["ffn_conv_b"][0]
                nc.scalar.activation(slices(Z[:, c]), three(bank_set), ACT.Identity, bias=col(b, chunk),
                                     scale=col(a, chunk)).then_inc(s("up_out"), 1)

            def gate_up(pair, slot):
                act.wait_ge(s("conv_done"), pair * 2 + 1)
                nc.scalar.activation(Z[:, 0], Z[:, 0], ACT.Silu).then_inc(s("silu_done"), 1)
                act.wait_ge(s("g_done"), pair + 2)
                nc.scalar.activation(act2[:, slot, 0], G[:], ACT.Copy).then_inc(s("g_hi"), 1)

            act.wait_ge(s("ffn_mm"), 1)
            w3(0, 2, 1)
            evac_up(0, 0, 1, 0, 1)
            evac_up(1, FC, 2, 1, 1)
            gate_up(0, 0)
            w3(1, 2, 2)
            evac_up(0, 1, 3, 0, 2)
            w3(2, 2, 3)
            w3(0, 3, 4)
            evac_up(1, FC + 1, 4, 1, 2)
            gate_up(1, 1)

            def act_body(i, last):
                w3(1, i * 2 + 1, i * 12 - 7)
                evac_up(0, i * 2, i * 12 - 7, 0, i * 2 + 1)
                w3(2, i * 2 + 1, i * 12 + 1)
                w3(0, i * 2 + 2, i * 12 + 1)
                evac_up(1, i * 2 + FC, i * 12 + 2, 1, i * 2 + 1)
                gate_up(i * 2, 0)
                w3(1, i * 2 + 2, i * 12 + 2)
                evac_up(0, i * 2 + 1, i * 12 + 3, 0, i * 2 + 2)
                w3(2, i * 2 + 2, i * 12 + 3)
                if not last:
                    w3(0, i * 2 + 3, i * 12 + 4)
                evac_up(1, i * 2 + (FC + 1), i * 12 + 4, 1, i * 2 + 2)
                gate_up(i * 2 + 1, 1)

            with act.Fori(1, FC // 2 - 1) as i:
                act_body(i, False)
            act_body(FC // 2 - 1, True)
            for k in range(KD):
                act.wait_ge(s("down_out"), KD * (FC // 2 - 1) + k + 1)
                if k >= 2:
                    act.wait_ge(s("sq_added"), 2 * KD + k - 1)
                nc.scalar.activation(Z[:, k % 2], acc[:, k], ACT.Square).then_inc(s("sq_c"), 1)
            act.wait_ge(s("sq_total"), 3)
            inverse_root(slices(G[:]), three(0), eps[:, 0:1], 1.0 / D).then_inc(s("std2"), 1)

        @block.gpsimd
        def _(pool):
            pool.wait_ge(consts_in, 16 * 6)
            pool.wait_ge(mod_ready, 1)
            pool.wait_ge(s("shift_saved"), 1)
            pool.wait_ge(s("rotated"), 5)
            for n, c in enumerate((12, 13, 0, 4, 8, 1, 5, 9, 2, 6, 10, 3, 7, 11)):
                d = difP[:, n % 3]
                x = PT[:, c, PO:PW]
                nc.gpsimd.tensor_tensor(d[:, 0:T], PT[:, c, PO - 1:PO - 1 + T], PT[:, c, PO:PO + T], ALU.subtract)
                nc.gpsimd.tensor_tensor(d[:, T:N], shift_st[:, c], PT[:, c, PO + T:PW], ALU.subtract
                                        ).then_inc(s("shift_step"), 1)
                pool.wait_ge(s("shift_step"), 2 * n + 1)
                nc.gpsimd.tensor_tensor(d, d, param("rwkv_mu", c).broadcast_to([P, N]), ALU.mult
                                        ).then_inc(s("shift_step"), 1)
                pool.wait_ge(s("shift_step"), 2 * n + 2)
                nc.gpsimd.tensor_tensor(x, x, d, ALU.add).then_inc(s("shifted"), 1)
            pool.wait_ge(s("s_mixed"), 1)
            for b in (AB[:], BB[:], KB[:], TB):
                nc.gpsimd.memset(b, 0.0).then_inc(s("bd_zero"), 1)
            eye = const("eye").unsqueeze(1).broadcast_to([P, NCH, C])
            for j in range(NJ):
                if j >= 1:
                    pool.wait_ge(*computed("G", j - 1, 1))
                    pool.wait_ge(s("t_first"), t_copies(j - 1, LAST_LEVEL + 1, 1))
                nc.gpsimd.tensor_copy(Tm, eye)
                nc.gpsimd.tensor_copy(TT, eye).then_inc(s("eyes"), 1)

        @block.vector
        def _(dve):
            mark, past = [0], [0]

            def link(ins):
                mark[0] += 1
                ins.then_inc(dve_step, 1)
                dve.wait_ge(dve_step, mark[0] + past[0])

            link(nc.vector.memset(eps[:, 0:1], NORM_EPS))
            link(nc.vector.memset(eps[:, 2:3], 0.0))
            nc.vector.memset(eps[:, 1:2], GN_EPS).then_inc(zeros_set, 1)
            dve.wait_ge(consts_in, 16 * 6)
            dve.wait_ge(std_ready, 1)

            def modulation(first, count, bank):
                dve.wait_ge(s("ada_turned"), (first + count) // 4)
                a = PARAM_AT["b_ada"][0] + first
                return nc.vector.tensor_tensor(mod[:, first:first + count, :],
                                               ps[:, bank, 0:count * 9].rearrange("p (n c) -> p n c", c=9),
                                               par[:, a:a + count].unsqueeze(2).broadcast_to([P, count, 9]), ALU.add)

            def norm_scale(out, name, chunk):
                link(nc.vector.tensor_scalar(out[:], mod[:, chunk:chunk + KD, :], 1.0, None, ALU.add))
                link(nc.vector.tensor_tensor(out[:], out[:], params(name).unsqueeze(2).broadcast_to([P, KD, 9]),
                                             ALU.mult))

            for k in range(KD):
                ins = nc.vector.tensor_tensor(xT[:, k], xT[:, k], rs[:], ALU.mult)
            link(ins)
            link(modulation(0, ADA_A, 0))
            norm_scale(gs1, "norm_pre_mix", 8)
            def w_low(slot2, slot4):
                return nc.vector.tensor_tensor(spl[:, slot2, 1], raw[:, slot4], spl[:, slot2, 0].bitcast(F32),
                                               ALU.subtract)
            for n in range(2):
                dve.wait_ge(w_hi, n + 1)
                w_low(n, n).then_inc(w_lo, 1)
            def low(k):
                dve.wait_ge(h_hi, k + 1)
                nc.vector.tensor_tensor(XS[:, k, 1], hA[k % 2], XS[:, k, 0].bitcast(F32),
                                        ALU.subtract).then_inc(h_lo, 1)
            for k in range(KD):
                if k >= 2:
                    dve.wait_ge(h_lo, k - 1)
                link(nc.vector.tensor_tensor(hA[k % 2][:, T:N], xT[:, k, T:N], gs1[:, k, 1:9], ALU.mult))
                link(nc.vector.tensor_tensor(hA[k % 2][:, T:N], hA[k % 2][:, T:N], mod[:, k, 1:9], ALU.add))
                nc.vector.tensor_scalar(hA[k % 2][:, 0:T], xT[:, k, 0:T], gs1[:, k, 0:1], mod[:, k, 0:1],
                                        ALU.mult, ALU.add).then_inc(h_ready, 1)
                if k >= 1:
                    low(k - 1)
            low(KD - 1)
            for n in range(2):
                dve.wait_ge(w_hi, n + 3)
                w_low(n, n + 2).then_inc(w_lo, 1)
            with dve.Fori(0, (PC - 4) // 4) as i:
                for j in range(4):
                    dve.wait_ge(w_hi, i * 4 + (5 + j))
                    w_low(j % 2, j).then_inc(w_lo, 1)
            nc.vector.memset(PT[:, :, 0:PO], 0.0).then_inc(mod_ready, 1)
            dve.wait_ge(proj_out, PC)
            dve.wait_ge(mod_ready, 1)
            nc.vector.tensor_copy(tail_shift[:], PT[:, 0:RC, PW - NS - 1:PW]).then_inc(s("shift_saved"), 1)
            dve.wait_ge(s("rope_in"), 16)
            for n, c in enumerate((18, 14, 15, 16, 17)):
                if n >= 1:
                    dve.wait_ge(s("rotated"), n)
                link(nc.vector.tensor_tensor(dif[:, 0], PT[:, c, PO:PW], rope[:, 0], ALU.mult))
                dve.wait_ge(s("swapped"), n + 1)
                link(nc.vector.tensor_tensor(slices(dif[:, 1]), three(n % 2), slices(rope[:, 1]), ALU.mult))
                ins = nc.vector.tensor_tensor(PT[:, c, PO:PW], dif[:, 0], dif[:, 1], ALU.add)
                ins.then_inc(s("rotated"), 1)
            dve.wait_ge(s("rotated"), 5)

            def mask_max(u):
                i, kv, v, b = u // 2, u % 2, u % 3, u % 2
                lo = P if i == 0 else 0
                dve.wait_ge(s("scored"), u + 1)
                if u >= 3:
                    dve.wait_ge(s("probs_turns"), u - 2)
                win = const("window")[:, lo:].unsqueeze(1).broadcast_to([P, 4, 2 * P - lo])
                sc = ps[:, 2 * b:2 * b + 2, :].rearrange("p b (j k) -> p (b j) k", j=2)[:, :, lo:]
                nc.vector.scalar_tensor_tensor(S4[:, v, :, lo:], sc, SCALE, win, ALU.mult, ALU.add).then_inc(s("masked"), 1)
                dve.wait_ge(s("masked"), u + 1)
                link(nc.vector.tensor_reduce(mx[:, v], S4[:, v, :, lo:], AX.X, ALU.max))
                a = PARAM_AT["sinks"][0] + 4 * kv
                link(nc.vector.tensor_tensor(mx[:, v], mx[:, v], par[:, a:a + 4], ALU.max))
                link(nc.vector.tensor_tensor(sk[:, v], par[:, a:a + 4], mx[:, v], ALU.subtract))
                nc.vector.tensor_scalar(nm[:, v], mx[:, v], -1.0, None, ALU.mult).then_inc(s("maxed"), 1)

            def normalise(u):
                i, v = u // 2, u % 3
                lo = P if i == 0 else 0
                dve.wait_ge(s("exped"), u + 1)
                link(nc.vector.tensor_tensor(den[:, v], den[:, v], sk[:, v], ALU.add))
                link(nc.vector.reciprocal(rd[:, v], den[:, v]))
                nc.vector.tensor_tensor(S4[:, v, :, lo:], S4[:, v, :, lo:],
                                        rd[:, v].unsqueeze(2).broadcast_to([P, 4, 2 * P - lo]),
                                        ALU.mult).then_inc(s("probs"), 1)

            mask_max(0)
            mask_max(1)
            for u in range(2 * NT):
                normalise(u)
                if u + 2 < 2 * NT:
                    mask_max(u + 2)
                if u >= 2 and u % 2 == 0:
                    modulation(ADA_A + 2 * u - 4, 4, 7).then_inc(s("mod_added"), 1)
            modulation(ADA_A + ADA_B - 4, 4, 7).then_inc(s("mod_added"), 1)
            dve.wait_ge(s("mod_added"), ADA_B // 4)
            dve.wait_ge(s("s_turns"), 1)
            link(nc.vector.tensor_scalar(sP[:], ps[0:64, 0, 0:P], SCALE, None, ALU.mult))
            link(nc.vector.tensor_reduce(mx[0:64, 0, 0:1], sP[:], AX.X, ALU.max))
            srow = par[0:64, PARAM_AT["sink_rows"][0]:PARAM_AT["sink_rows"][1]]
            link(nc.vector.tensor_tensor(mx[0:64, 0, 0:1], mx[0:64, 0, 0:1], srow, ALU.max))
            link(nc.vector.tensor_tensor(sk[0:64, 0, 0:1], srow, mx[0:64, 0, 0:1], ALU.subtract))
            nc.vector.tensor_scalar(nm[0:64, 0, 0:1], mx[0:64, 0, 0:1], -1.0, None, ALU.mult).then_inc(s("s_maxed"), 1)
            dve.wait_ge(s("s_exped"), 1)
            link(nc.vector.tensor_tensor(den[0:64, 0, 0:1], den[0:64, 0, 0:1], sk[0:64, 0, 0:1], ALU.add))
            link(nc.vector.reciprocal(rd[0:64, 0, 0:1], den[0:64, 0, 0:1]))
            nc.vector.tensor_scalar(sP[:], sP[:], rd[0:64, 0, 0:1], None, ALU.mult).then_inc(s("s_probs"), 1)
            link(nc.vector.tensor_scalar(sc_mod[:], params("rwkv_k_a"), -1.0, 1.0, ALU.mult, ALU.add))

            dve.wait_ge(s("s_mixed"), 1)
            def prepare(piece, j):
                r, k, v = (PT[:, c + j, PO:PW] for c in (0, 4, 8))
                q = slice(0, T)
                if piece == "rate":
                    dve.wait_ge(s("sig_rate"), j + 1)
                    if j >= 1:
                        dve.wait_ge(*computed("E", j - 1, 1))
                    link(nc.vector.tensor_scalar(F4[:], F1[:], param("rwkv_k_a", j), sc_mod[:, j:j + 1], ALU.mult, ALU.add))
                elif piece == "log":
                    link(nc.vector.tensor_tensor(F4[:], F4[:], k, ALU.mult))
                elif piece == "norm":
                    dve.wait_ge(s("p_norm"), j + 1)
                    if j >= 1:
                        dve.wait_ge(*computed("E", j - 1, 1))
                    nc.vector.tensor_scalar(slices(F3), ps[:, 4:7, 0:SL], NORM_FLOOR, None, ALU.max
                                            ).then_inc(s("k_floor"), 1)
                elif piece == "cum":
                    dve.wait_ge(s("p_sgt"), j + 1)
                    dve.wait_ge(s("decays"), 4 * j + 1)
                    nc.vector.scalar_tensor_tensor(F0[:], r, param("rwkv_r_k", j), F4[:], ALU.mult, ALU.mult
                                                   ).then_inc(s("rkk"), 1)
                elif piece == "kk":
                    dve.wait_ge(s("k_norm"), j + 1)
                    link(nc.vector.scalar_tensor_tensor(F3, k, param("rwkv_k_k", j), F3, ALU.mult, ALU.mult))
                elif piece == "bonus":
                    link(nc.vector.tensor_tensor(F1[:], F1[:], F3, ALU.mult))
                elif piece == "alpha":
                    dve.wait_ge(s("decays"), 4 * (j + 1))
                    for n, src in ((0, F3[:, T:N]), (2, F4[:, T:N]), (3, F1[:, T:N]), (4, r[:, T:N]), (5, v[:, T:N])):
                        ins = nc.vector.tensor_copy(SMP[:, j, n, :], src)
                    ins.then_inc(s("smp_ready"), 1)
                    nc.vector.scalar_tensor_tensor(Alpha, unit(F3), -1.0, Alpha, ALU.mult, ALU.mult
                                                   ).then_inc(s("alpha"), 1)
                elif piece == "beta":
                    if j == 0:
                        dve.wait_ge(s("bd_zero"), 4)
                    link(nc.vector.tensor_tensor(Beta, unit(F1), unit(F6), ALU.mult))
                    for h in (slice(0, HD), slice(HD, P)):
                        ins = nc.vector.tensor_copy(BB[h, :, h], Beta[h])
                    ins.then_inc(s("beta_bd"), 1)
                elif piece == "kappa":
                    for h in (slice(0, HD), slice(HD, P)):
                        ins = nc.vector.tensor_tensor(KB[h, :, h], unit(F4)[h], unit(F6)[h], ALU.mult)
                elif piece == "product":
                    dve.wait_ge(s("p_bonus"), j + 1)
                    nc.vector.tensor_tensor(slices(k), ps[:, 4:7, 0:SL], slices(v), ALU.mult).then_inc(s("bonus"), 1)
                elif piece == "ends":
                    dve.wait_ge(s("rkk"), j + 1)
                    if j >= 1:
                        dve.wait_ge(*computed("O", j - 1, 1))
                    nc.vector.tensor_tensor(R, unit(r), unit(F5), ALU.mult)
                    nc.vector.tensor_tensor(Aff, const("eye").unsqueeze(1).broadcast_to([P, NCH, C]),
                                            F5[:, C - 1:T:C].unsqueeze(2).broadcast_to([P, NCH, C]), ALU.mult
                                            ).then_inc(s("ends_ready"), 1)

            def all8(m):
                return m.unsqueeze(1).broadcast_to([P, 8, C])

            def below(dst, u, out):
                for h in (slice(0, HD), slice(HD, P)):
                    ins = nc.vector.tensor_tensor(dst[h, u, h], out[h],
                                                  const("after")[h].unsqueeze(1).broadcast_to([HD, 8, C]), ALU.mult)
                return ins

            def evacuate(name, j, half):
                u = slice(8 * half, 8 * half + 8)
                out = results(name, half)
                dve.wait_ge(*computed(name, j, half))
                if name == "MT":
                    below(BB, u, out)
                    link(nc.vector.copy_predicated(TT[:, u], all8(lvl[:, 1]), out))
                    ins = nc.vector.tensor_copy(TB[HD:P, u, HD:P], TT[HD:P, u])
                elif name == "M":
                    if half == 0:
                        dve.wait_ge(s("eyes"), j + 1)
                    ins = nc.vector.copy_predicated(Tm[:, u], all8(lvl[:, 0]), out)
                elif name == "MkT":
                    ins = below(KB, u, out)
                elif name in ("NbT", "NkT"):
                    ins = nc.vector.tensor_tensor((NbT if name == "NbT" else NkT)[:, u], out, all8(const("upto")), ALU.mult)
                elif name[0:2] == "ZT":
                    n = int(name[2:]) + 1
                    ins = nc.vector.copy_predicated(TT[:, u], all8(lvl[:, 2 * n + 1]), out)
                    link(ins)
                    ins = nc.vector.tensor_copy(TB[HD:P, u, HD:P], TT[HD:P, u])
                elif name[0] == "Z":
                    n = int(name[1:]) + 1
                    ins = nc.vector.copy_predicated(Tm[:, u], all8(lvl[:, 2 * n]), out)
                elif name == "G":
                    for h in (slice(0, HD), slice(HD, P)):
                        ins = nc.vector.tensor_copy(BB[h, u, h], out[h])
                else:
                    dst = (Aff if name == "A" else R)[:, u]
                    ins = nc.vector.tensor_tensor(dst, dst, out, ALU.add)
                ins.then_inc(s("unit_dve"), 1)

            def chain(j, c):
                if c == 0:
                    dve.wait_ge(*evacuated("E", j, 1))
                    nc.vector.tensor_copy(St[:, 1], Ein[:, 0]).then_inc(s("state_ready"), 1)
                    return
                dve.wait_ge(s("state_mm"), j * (NCH - 1) + c)
                dst = St[:, c + 1] if c + 1 < NCH else WO[:, j]
                nc.vector.tensor_tensor(dst, ps[:, 7, 0:C], Ein[:, c], ALU.add).then_inc(s("state_ready"), 1)

            def over_v(i):
                return V6[:, i, :].unsqueeze(1).broadcast_to([P, 32, HD])

            def over_k(x):
                return x[:].unsqueeze(2).broadcast_to([P, 32, HD])

            def sample(n):
                if n == 0:
                    dve.wait_ge(s("wkv_in"), 16 * 5)
                    link(nc.vector.tensor_tensor(sTmp, sWKV, over_v(0), ALU.mult))
                elif n == 1:
                    link(nc.vector.tensor_reduce(sa[:], sTmp, AX.X, ALU.add))
                elif n == 2:
                    link(nc.vector.tensor_tensor(sWKV, sWKV, over_v(1), ALU.mult))
                elif n == 3:
                    link(nc.vector.tensor_tensor(sTmp, over_k(sa), over_v(3), ALU.mult))
                elif n == 4:
                    link(nc.vector.tensor_tensor(sWKV, sWKV, sTmp, ALU.subtract))
                elif n == 5:
                    link(nc.vector.tensor_tensor(sTmp, over_k(V32), over_v(2), ALU.mult))
                elif n == 6:
                    link(nc.vector.tensor_tensor(sWKV, sWKV, sTmp, ALU.add))
                elif n == 7:
                    link(nc.vector.tensor_tensor(sTmp, sWKV, over_v(4), ALU.mult))
                elif n == 8:
                    nc.vector.tensor_reduce(Osm[:], sTmp, AX.X, ALU.add).then_inc(s("sample_o"), 1)

            for j in range(NJ + 1):
                for piece, c in overlapped(j >= 1, j < NJ):
                    if piece != "chain":
                        prepare(piece, j)
                    else:
                        chain(j - 1, c)
                        if j == NJ and c >= 5:
                            sample(c - 5)
                if j < NJ:
                    for name in STEPS:
                        for half in range(2):
                            if name[0] == "Y":
                                u = slice(8 * half, 8 * half + 8)
                                dve.wait_ge(s("y_compact"), y_copies(j, int(name[1:]), half))
                                nc.vector.tensor_copy(AB[HD:P, u, HD:P], Yc[HD:P, u]).then_inc(s("y_second"), 1)
                            elif name in dve_steps:
                                evacuate(name, j, half)

            for j in range(NJ):
                Y, X = PT[:, j, PO:PW], PT[:, XB[j % 2], PO:PW]
                dve.wait_ge(s("gn_mean"), j + 1)
                nc.vector.scalar_tensor_tensor(slices(Y), three(0), -1.0 / HD, slices(PT[:, 8 + j, PO:PW]), ALU.mult,
                                               ALU.add).then_inc(s("centred"), 1)
                dve.wait_ge(s("gn_std"), j + 1)
                link(nc.vector.tensor_tensor(Y, Y, X, ALU.mult))
                link(nc.vector.tensor_scalar(Y, Y, param("rwkv_ln_w", j), param("rwkv_ln_b", j), ALU.mult, ALU.add))
                link(nc.vector.tensor_tensor(Y, Y, PT[:, 4 + j, PO:PW], ALU.add))
                dve.wait_ge(s("gn_gate"), j + 1)
                nc.vector.tensor_tensor(slices(Y), three(0), slices(Y), ALU.mult).then_inc(s("gated"), 1)
                dve.wait_ge(s("mix_hi"), 2 * j + 2)
                nc.vector.tensor_tensor(XS[:, j, 1], Y, XS[:, j, 0].bitcast(F32), ALU.subtract).then_inc(s("mix_ready"), 1)
                nc.vector.tensor_tensor(XS[:, 4 + j, 1], PT[:, 14 + j, PO:PW], XS[:, 4 + j, 0].bitcast(F32),
                                        ALU.subtract).then_inc(s("mix_ready"), 1)
            link(nc.vector.tensor_tensor(gate[:, 0], mod[:, 16:24], params("norm_post_mix").unsqueeze(2).broadcast_to([P, KD, 9]), ALU.mult))
            link(nc.vector.tensor_tensor(gate[:, 1], mod[:, 40:48], params("norm_post_ffn").unsqueeze(2).broadcast_to([P, KD, 9]), ALU.mult))
            norm_scale(gs2, "norm_pre_ffn", 32)
            wl = [0]

            def low_out(n):
                dve.wait_ge(w_hi, PC + n + 1)
                w_low(n % 2, n % 4).then_inc(w_lo, 1)

            def add_square(k, src, total, first):
                dve.wait_ge(s("sq_c"), first + k + 1)
                if k == 0:
                    nc.vector.tensor_copy(total, src).then_inc(s("sq_added"), 1)
                else:
                    dve.wait_ge(s("sq_added"), first + k)
                    nc.vector.tensor_tensor(total, total, src, ALU.add).then_inc(s("sq_added"), 1)

            low_out(0)
            low_out(1)
            for n in range(KD):
                if n + 2 < KD:
                    low_out(n + 2)
                add_square(n, sq2[:, n % 2], sqs[:], 0)
            dve.wait_ge(s("sq_added"), KD)
            nc.vector.memset(sc_mod[:, 0:1], 0.0).then_inc(s("sq_sum"), 1)
            dve.wait_ge(s("std2"), 1)
            dve.wait_ge(s("x2_in"), 16)
            dve.wait_ge(s("out_out"), KD)
            for k in range(KD):
                link(nc.vector.tensor_tensor(MO[:, k], MO[:, k], rsC[:], ALU.mult))
                link(nc.vector.tensor_tensor(MO[:, k, T:N], MO[:, k, T:N], gate[:, 0, k, 1:9], ALU.mult))
                link(nc.vector.tensor_tensor(X2[:, k, T:N], X2[:, k, T:N], MO[:, k, T:N], ALU.add))
                nc.vector.scalar_tensor_tensor(X2[:, k, 0:T], MO[:, k, 0:T], gate[:, 0, k, 0:1], X2[:, k, 0:T], ALU.mult,
                                               ALU.add).then_inc(s("x1_ready"), 1)
                if k >= 1:
                    add_square(k - 1, sq2[:, (k - 1) % 2], sqs[:], KD)
            add_square(KD - 1, sq2[:, 1], sqs[:], KD)
            dve.wait_ge(s("sq_added"), 2 * KD)
            nc.vector.memset(sc_mod[:, 1:2], 0.0).then_inc(s("sq_sum"), 1)
            dve.wait_ge(s("std2"), 2)

            def low3(slot, count):
                dve.wait_ge(s("w3_hi"), count)
                nc.vector.tensor_tensor(spl3[:, slot, 1], raw3[:, slot], spl3[:, slot, 0].bitcast(F32),
                                        ALU.subtract).then_inc(s("w3_lo"), 1)

            def low_h(k):
                dve.wait_ge(s("h2_hi"), k + 1)
                nc.vector.tensor_tensor(XS[:, k, 1], MO[:, k], XS[:, k, 0].bitcast(F32), ALU.subtract).then_inc(s("h2_lo"), 1)

            for m in range(3):
                low3(m, m + 1)
            for k in range(KD):
                link(nc.vector.tensor_tensor(MO[:, k], X2[:, k], rsC[:], ALU.mult))
                link(nc.vector.tensor_tensor(MO[:, k, T:N], MO[:, k, T:N], gs2[:, k, 1:9], ALU.mult))
                link(nc.vector.tensor_tensor(MO[:, k, T:N], MO[:, k, T:N], mod[:, 24 + k, 1:9], ALU.add))
                nc.vector.tensor_scalar(MO[:, k, 0:T], MO[:, k, 0:T], gs2[:, k, 0:1], mod[:, 24 + k, 0:1], ALU.mult,
                                        ALU.add).then_inc(s("h2_ready"), 1)
                if k >= 1:
                    low_h(k - 1)
            low_h(KD - 1)
            dve.wait_ge(s("x1_out"), 16 * KD)
            dve.wait_ge(s("h2_lo"), KD)
            link(nc.vector.memset(acc[:], 0.0))
            dve.wait_ge(s("conv_in"), 16)

            def taps(n):
                a = PARAM_AT["ffn_conv_w"][0] + n * 2 * FC
                return par[:, a:a + 2 * FC].unsqueeze(2).broadcast_to([P, 2 * FC, NS])

            cu = ftail[:, :, 0:NS]
            link(nc.vector.tensor_tensor(conv_add[:], conv_st[:, 0], taps(0), ALU.mult))
            link(nc.vector.tensor_tensor(cu, conv_st[:, 1], taps(1), ALU.mult))
            nc.vector.tensor_tensor(conv_add[:], conv_add[:], cu, ALU.add).then_inc(s("g_done"), 1)
            dve.wait_ge(s("g_done"), 1)

            def conv(c, chunk, count):
                dve.wait_ge(s("up_out"), count)
                z, u = Z[:, c], U[:, c]
                for n in (1, 0):
                    d = CW - 1 - n
                    a = PARAM_AT["ffn_conv_w"][0] + n * 2 * FC
                    link(nc.vector.scalar_tensor_tensor(z[:, d:T], u[:, 0:T - d], col(a, chunk), z[:, d:T],
                                                        ALU.mult, ALU.add))
                link(nc.vector.tensor_copy(at_chunk(ftail, chunk), u[:, T - 2:N]))
                nc.vector.tensor_tensor(z[:, T:N], z[:, T:N], at_chunk(conv_add, chunk), ALU.add
                                        ).then_inc(s("conv_done"), 1)

            def form(pair, slot):
                dve.wait_ge(s("silu_done"), pair + 1)
                dve.wait_ge(s("conv_done"), pair * 2 + 2)
                nc.vector.tensor_tensor(G[:], Z[:, 0], Z[:, 1], ALU.mult).then_inc(s("g_done"), 1)
                dve.wait_ge(s("g_hi"), pair + 1)
                nc.vector.tensor_tensor(act2[:, slot, 1], G[:], act2[:, slot, 0].bitcast(F32), ALU.subtract
                                        ).then_inc(s("g_lo"), 1)
                dve.wait_ge(s("g_lo"), pair + 1)

            low3(0, 4)
            conv(0, 0, 1)
            conv(1, FC, 2)
            form(0, 0)
            low3(1, 5)
            conv(0, 1, 3)
            low3(2, 6)
            low3(0, 7)
            conv(1, FC + 1, 4)
            form(1, 1)

            def add_down(i, last):
                for k in range(KD):
                    y = k + 1
                    dve.wait_ge(s("ffn_mm"), i * 12 - (8 if last else 7) + y)
                    bs = (y - 1) % 2 if last else y % 2
                    nc.vector.tensor_tensor(slices(acc[:, k]), slices(acc[:, k]), three(bs), ALU.add
                                            ).then_inc(s("down_out"), 1)

            def dve_body(i, last):
                low3(1, i * 6 + 2)
                conv(0, i * 2, i * 4 + 1)
                add_down(i, False)
                low3(2, i * 6 + 3)
                low3(0, i * 6 + 4)
                conv(1, i * 2 + FC, i * 4 + 2)
                form(i * 2, 0)
                low3(1, i * 6 + 5)
                conv(0, i * 2 + 1, i * 4 + 3)
                low3(2, i * 6 + 6)
                if not last:
                    low3(0, i * 6 + 7)
                conv(1, i * 2 + (FC + 1), i * 4 + 4)
                form(i * 2 + 1, 1)

            rounds, links = FC // 2 - 2, 12
            with dve.Fori(1, 1 + rounds) as i:
                past[0] = i * links - links
                before = mark[0]
                dve_body(i, False)
                assert mark[0] - before == links
            mark[0] += (rounds - 1) * links
            past[0] = 0
            dve_body(FC // 2 - 1, True)
            add_down(FC // 2, True)
            for k in range(KD):
                add_square(k, Z[:, k % 2], sqF[:], 2 * KD)
            dve.wait_ge(s("sq_added"), 3 * KD)
            nc.vector.memset(sc_mod[:, 2:3], 0.0).then_inc(s("sq_sum"), 1)
            dve.wait_ge(s("std2"), 3)
            dve.wait_ge(s("x1_in"), 16)
            for k in range(KD):
                link(nc.vector.tensor_tensor(acc[:, k], acc[:, k], G[:], ALU.mult))
                link(nc.vector.tensor_tensor(acc[:, k, T:N], acc[:, k, T:N], gate[:, 1, k, 1:9], ALU.mult))
                link(nc.vector.tensor_tensor(acc[:, k, T:N], acc[:, k, T:N], X1[:, k, T:N], ALU.add))
                nc.vector.scalar_tensor_tensor(acc[:, k, 0:T], acc[:, k, 0:T], gate[:, 1, k, 0:1], X1[:, k, 0:T], ALU.mult,
                                               ALU.add).then_inc(s("y_ready"), 1)


def _consts():
    i = np.arange(P)
    c = {}
    c["ident"] = np.eye(P)
    c["swap"] = (i[:, None] == (i[None, :] ^ 32))
    c["headsum"] = (i[:, None] // HD == i[None, :] // HD)
    c["ones"] = np.ones((P, P))
    same = i[:, None] // C == i[None, :] // C
    c["cumsum"] = np.concatenate([same & (i[:, None] <= i[None, :]), same & (i[:, None] < i[None, :])], 1)
    t = np.arange(C)
    c["after"] = (i % C)[:, None] < t[None, :]
    c["upto"] = (i % C)[:, None] <= t[None, :]
    c["eye"] = (i % C)[:, None] == t[None, :]
    k = np.arange(2 * P)[None, :]
    c["window"] = np.where((k <= i[:, None] + P) & (k > i[:, None]), 0.0, MASKED)
    out = np.concatenate([np.asarray(c[n], np.float32).reshape(P, w) for n, w in CONSTS], 1)
    lv = []
    for b in (1,) + LEVELS:
        r, q = (i % C)[:, None], t[None, :]
        m = (r // (2 * b) == q // (2 * b)) & (r // b > q // b)
        lv += [m, (r // (2 * b) == q // (2 * b)) & (r // b < q // b)]
    return out, np.stack(lv, 1).astype(np.uint32)


def _rope(past):
    pos = np.concatenate([np.arange(T), np.full(NS, past)]).astype(np.float32)
    half = HD // 2
    inv = (10000.0 ** (-np.arange(half) / half)).astype(np.float32)
    ang = (pos[:, None] * inv[None, :]).astype(np.float32)
    cos, sin = np.cos(ang.astype(np.float64)).T, np.sin(ang.astype(np.float64)).T
    d = np.arange(P)
    sign = np.where(d % HD < half, -1.0, 1.0)[:, None]
    return np.stack([cos[d % half], sin[d % half] * sign], 1).astype(np.float32)


def _features(a):
    a = np.asarray(a)
    return np.moveaxis(a.reshape(a.shape[:-1] + (-1, P)), -1, 0)


def _tiles(w):
    k, n = w.shape[0] // P, w.shape[1] // P
    return np.ascontiguousarray(w.reshape(k, P, n, P).transpose(2, 1, 0, 3)).reshape(n, P, k * P)


def host_arrays(v):
    v = {k: np.asarray(a) for k, a in v.items()}
    a = {}
    x = np.concatenate([v["x_prompt"][0], v["x_sample"][:, 0]], 0)
    a["xT"] = np.ascontiguousarray(_features(x).transpose(0, 2, 1))
    c = np.concatenate([v["c_prompt"], v["c_sample"]], 0)
    a["cT"] = np.ascontiguousarray(_features(c).transpose(0, 2, 1))
    a["ada"] = np.ascontiguousarray(v["w_ada"][0].reshape(4, 2, P, 12, 512).transpose(3, 0, 2, 1, 4)).reshape(48, P, D)
    pair = np.concatenate([np.r_[j * HD:(j + 1) * HD, (4 + j) * HD:(5 + j) * HD] for j in range(4)])
    q0 = RC * P
    cols = np.concatenate([np.arange(q0), q0 + pair, np.arange(q0 + RW, PC * P)])
    a["w_in"] = _tiles(v["w_in"][0][:, cols])
    rows = np.concatenate([np.arange(RW), RW + pair])
    a["w_out"] = _tiles(v["w_out"][0][rows])
    a["up"] = _tiles(v["ffn_w_up"][0])
    a["down"] = np.ascontiguousarray(v["ffn_w_down"][0].reshape(FC, P, D))
    a["consts"], a["levels"] = _consts()
    a["rope"] = _rope(8192)
    pars = []
    for name, width in PARAMS:
        if name == "sinks":
            p = np.broadcast_to(v["swa_sinks"][0][None, :], (P, 8))
        elif name == "sink_rows":
            p = np.tile(v["swa_sinks"][0], 16)[:, None]
        elif name == "rwkv_r_k":
            p = _features(v[name].reshape(-1))
        elif name == "b_ada":
            p = _features(v[name][0])
        else:
            p = _features(v[name].reshape(-1))
        pars.append(p.reshape(P, width))
    a["params"] = np.ascontiguousarray(np.concatenate(pars, 1))
    a["shift_st"] = np.ascontiguousarray(_features(v["state_rwkv_shift"][0]).transpose(0, 2, 1))
    a["conv_st"] = np.ascontiguousarray(_features(v["state_ffn_conv"][0]).transpose(0, 2, 3, 1))
    a["lora"] = np.concatenate([v["rwkv_w_up"][0], v["rwkv_a_up"][0]], 0)
    a["g_up"] = np.ascontiguousarray(v["rwkv_g_up"][0])
    w = v["state_rwkv_wkv"][0].reshape(NS, 8, 2, 32, HD)
    a["wkv"] = np.ascontiguousarray(w.transpose(2, 0, 1, 3, 4)).reshape(P, 32 * HD)
    a["cache_k"] = np.ascontiguousarray(v["cache_swa_k"][0]).reshape(NS, P, P)
    a["cache_v"] = np.ascontiguousarray(v["cache_swa_v"][0]).reshape(NS, P, P)
    return a


OUTPUTS = [("o_y", [P, KD, N]), ("o_shift", [P, RC, NS + 1]), ("o_ks", [NS, P, P]), ("o_vs", [NS, P, P]),
           ("o_kvp", [P, 2, P]), ("o_wkvs", [P, 32, HD]), ("o_wkvp", [P, NJ, HD]), ("o_tail", [P, 2 * FC, NS + 2]),
           ("o_prev", [P, 2 * FC, NS])]


def unpack(r):
    y = np.ascontiguousarray(r["o_y"].transpose(2, 1, 0)).reshape(N, D)
    shift = np.ascontiguousarray(r["o_shift"].transpose(2, 1, 0)).reshape(NS + 1, RC * P)
    kvp = r["o_kvp"].transpose(1, 2, 0).reshape(2, 1, 1, P, 2, HD)
    wkvp = r["o_wkvp"].reshape(2, HD, NJ, HD).transpose(2, 0, 3, 1).reshape(1, 1, 2 * NJ, HD, HD)
    wkvs = r["o_wkvs"].reshape(2, NS, 8, 32, HD).transpose(1, 2, 0, 3, 4).reshape(1, NS, 8, HD, HD)
    tail = np.ascontiguousarray(r["o_tail"].transpose(2, 1, 0)).reshape(NS + 2, 2 * FF)
    prev = np.ascontiguousarray(r["o_prev"].transpose(2, 1, 0)).reshape(NS, 2 * FF)
    convs = np.stack([prev, tail[2:]], 1)[None]
    got = (y[None, :T], y[T:, None], wkvp, shift[:1][None], kvp[0], kvp[1], tail[None, None, :2], wkvs,
           shift[1:][None], r["o_ks"].reshape(1, NS, P, 2, HD), r["o_vs"].reshape(1, NS, P, 2, HD), convs)
    return tuple(np.ascontiguousarray(a) for a in got)


def kernel(**inputs):
    import concourse.bacc as bacc
    from concourse.bass_utils import run_bass_kernel_spmd

    nc = bacc.Bacc("TRN2", target_bir_lowering=False, num_devices=1)
    arrays = host_arrays(inputs)
    io = {n: nc.dram_tensor(n, a.shape, mybir.dt.from_np(a.dtype), kind="ExternalInput").ap()
          for n, a in arrays.items()}
    for n, shape in OUTPUTS:
        io[n] = nc.dram_tensor(n, shape, F32, kind="ExternalOutput").ap()
    build_program(nc, io)
    r = run_bass_kernel_spmd(nc, [arrays], core_ids=[0])
    return unpack(r.results[0])
```

```python
from contextlib import ExitStack

import numpy as np
import concourse.bass as bass
from concourse import mybir

F32 = mybir.dt.float32
F32R = mybir.dt.float32r
U32 = mybir.dt.uint32
ALU = mybir.AluOpType
ACT = mybir.ActivationFunctionType
AX = mybir.AxisListType

P = 128
D = 1024
KD = D // P
T = 1024
NS = 8
N = T + NS
SL = N // 3
HD = 64
RW = 512
NJ = RW // P
RC = 14
PC = 20
FF = 2816
FC = FF // P
CW = 3
C = 64
NCH = T // C
NT = T // P
PW = N + 2
PO = 2
KAPPA = float(np.exp(np.float32(-0.5)))
NORM_EPS = 1e-6
GN_EPS = 64e-5
MASKED = -1e30
NORM_FLOOR = 1e-24
SCALE = HD ** -0.5
LEVELS = (2, 4, 8, 16, 32)

CONSTS = [("ident", P), ("swap", P), ("headsum", P), ("ones", P), ("cumsum", 2 * P),
          ("after", C), ("upto", C), ("eye", C), ("window", 2 * P)]
PARAMS = [("b_ada", 48), ("norm_pre_mix", 8), ("norm_post_mix", 8), ("norm_pre_ffn", 8),
          ("norm_post_ffn", 8), ("rwkv_mu", RC), ("rwkv_w0", 4), ("rwkv_a0", 4), ("rwkv_k_k", 4),
          ("rwkv_k_a", 4), ("rwkv_r_k", 4), ("rwkv_ln_w", 4), ("rwkv_ln_b", 4),
          ("ffn_conv_w", CW * 2 * FC), ("ffn_conv_b", 2 * FC), ("sinks", 8), ("sink_rows", 1)]


def columns(table):
    at, n = {}, 0
    for name, width in table:
        at[name] = (n, n + width)
        n += width
    return at, n


CONST_AT, CONST_N = columns(CONSTS)
PARAM_AT, PARAM_N = columns(PARAMS)


def build_program(nc, io):
    ctx = ExitStack()
    with ctx:
        base = (nc.sbuf_base + 63) // 64 * 64
        end = nc.sbuf_base + nc.sbuf_bytes_remaining

        def sb(name, shape, dt, off):
            size = int(np.prod(shape[1:])) * 4
            assert base + off + size <= end, (name, off, size, end - base)
            return nc.alloc_sbuf_tensor_at(name, shape, dt, offset=base + off)

        def place(names, at):
            out = []
            for name, shape, dt in names:
                out.append(sb(name, shape, dt, at))
                at += (int(np.prod(shape[1:])) * 4 + 31) // 32 * 32
            return out, at

        def sem(name):
            return ctx.enter_context(nc.semaphore(name))

        (cst, lvl, par, mod, cT, cTs, shift_st, tail_shift, conv_add, lora, g_up, gs1, gs2, gate, Pc, eps,
         sc_mod), at = place([
            ("cst", [P, CONST_N], F32), ("lvl", [P, 2 * (len(LEVELS) + 1), C], U32), ("par", [P, PARAM_N], F32),
            ("mod", [P, 48, 9], F32), ("cT", [P, KD, 9], F32), ("cTs", [P, KD, 9], F32),
            ("shift_st", [P, RC, NS], F32), ("tail_shift", [P, RC, NS + 1], F32),
            ("conv_add", [P, 2 * FC, NS], F32), ("lora", [P, RW], F32), ("g_up", [P, RW], F32),
            ("gs1", [P, KD, 9], F32), ("gs2", [P, KD, 9], F32), ("gate", [P, 2, KD, 9], F32),
            ("Pc", [P, NCH], F32), ("eps", [P, 4], F32),
            ("sc_mod", [P, 4], F32)], 0)
        PT0 = (at + 63) // 64 * 64
        (PT,), REM = place([("PT", [P, PC, PW], F32)], PT0)
        (xT,), _ = place([("xT", [P, KD, N], F32)], PT0 + 12 * PW * 4)
        (XS,), RING = place([("XS", [P, KD, 2, N], F32R)], REM)
        (raw, spl), TMP = place([("raw", [P, 4, D], F32), ("spl", [P, 2, 2, D], F32R)], RING)
        (rs,), _ = place([("rs", [P, N], F32)], TMP)
        (ada_row,), _ = place([("ada_row", [9, 512], F32)], TMP + 8 * N)

        (rope, S4, PR, VA, Kf, Vf, KTs, kvrow, sS, sP, sPT, mx, nm, sk, den, rd), at = place([
            ("rope", [P, 2, N], F32), ("S4", [P, 3, 4, 2 * P], F32), ("PR", [P, 2, 4, 2, P], F32),
            ("VA", [P, NT, P], F32), ("Kf", [P, NS, P], F32), ("Vf", [P, NS, P], F32), ("KTs", [P, NS, P], F32),
            ("kvrow", [NS, 2, P], F32), ("sS", [P, 64], F32), ("sP", [64, P], F32), ("sPT", [P, 64], F32),
            ("mx", [P, 3, 4], F32), ("nm", [P, 3, 4], F32), ("sk", [P, 3, 4], F32), ("den", [P, 3, 4], F32),
            ("rd", [P, 3, 4], F32)], REM)
        assert at <= RING, (at, RING)
        (dif,), _ = place([("dif", [P, 2, N], F32)], TMP)
        (difP, Kz), at = place([("difP", [P, N], F32), ("Kz", [P, 2, T], F32)], at)
        assert at <= RING, (at, RING)
        NU = 18
        (UNI, AB, BB, KB, WO, SMP), FB = place([
            ("UNI", [P, NU, NCH, C], F32), ("AB", [P, NCH, P], F32), ("BB", [P, NCH, P], F32), ("KB", [P, NCH, P], F32),
            ("WO", [P, NJ, C], F32), ("SMP", [P, NJ, 6, NS], F32)], REM)
        (Alpha, R, Aff, Beta, Tm, aTm, W1, bTm, NbT, Yc, kTm, TT, NkT, vTm, _, _, Ein, St) = (
            UNI[:, n] for n in range(NU))
        ALPHA_R_AFF, BETA_T, A_W1, B_NBT = UNI[:, 0:3], UNI[:, 3:5], UNI[:, 5:7], UNI[:, 7:9]
        TB = UNI[:, 14:16].rearrange("p n u c -> p (n u c)").rearrange("p (u s) -> p u s", s=P)
        (F0, F1), at = place([("F0", [P, N], F32), ("F1", [P, N], F32)], FB)
        F4, F3 = PT[:, 18, PO:PW], PT[:, 19, PO:PW]
        F5, F6 = (UNI[:, n].rearrange("p u c -> p (u c)") for n in (5, 9))
        (V6, V32, Osm, sa), _ = place([
            ("V6", [P, 6, HD], F32), ("V32", [P, 32], F32), ("Osm", [P, 32], F32), ("sa", [P, 32], F32)], at)
        (sTmp,), at2 = place([("sTmp", [P, 32, HD], F32)], FB)
        assert at2 <= at
        sTmp = sTmp[:]
        SM48, OR = PT[0:48, 12, 0:RW], PT[0:NS, 12, RW:2 * RW]
        sWKV = PT[:, 18:20].rearrange("p c w -> p (c w)")[:, 0:32 * HD].rearrange("p (v k) -> p v k", k=HD)
        (MO, X2, sqs, sq2, rsC), at2 = place([
            ("MO", [P, KD, N], F32), ("X2", [P, KD, N], F32), ("sqs", [P, N], F32), ("sq2", [P, 2, N], F32),
            ("rsC", [P, N], F32)], PT0)
        assert at2 <= REM
        (acc, U, Z, G, act2, ftail, conv_st, sqF), at2 = place([
            ("acc", [P, KD, N], F32), ("U", [P, 2, N], F32), ("Z", [P, 2, N], F32), ("G", [P, N], F32),
            ("act2", [P, 2, 2, N], F32R), ("ftail", [P, 2 * FC, NS + 2], F32), ("conv_st", [P, 2, 2 * FC, NS], F32),
            ("sqF", [P, N], F32)], PT0)
        assert at2 <= REM
        (raw3, spl3), at2 = place([("raw3", [P, 3, D], F32), ("spl3", [P, 3, 2, D], F32R)], RING)
        (X1,), _ = place([("X1", [P, KD, N], F32)], REM)
        x1_dram = nc.dram_tensor("x1_dram", [P, KD, N], F32).ap()
        scr_a = nc.dram_tensor("scr_a", [6, NS, RW], F32).ap()
        scr_o = nc.dram_tensor("scr_o", [NS, 8, 2, 32], F32).ap()

        def hm(j):
            return PT[:, j, PO:PO + T].rearrange("p (u c) -> p u c", c=C)

        def unit(f):
            return f[:, 0:T].rearrange("p (u c) -> p u c", c=C)

        SGt = Beta.rearrange("p u c -> p (u c)").rearrange("p (n c) -> p n c", c=P)

        ps = ctx.enter_context(nc.psum_tensor("ps", [P, 8, 512], F32))

        def const(name):
            a, b = CONST_AT[name]
            return cst[:, a:b]

        def param(name, n):
            return par[:, PARAM_AT[name][0] + n:PARAM_AT[name][0] + n + 1]

        def params(name):
            return par[:, PARAM_AT[name][0]:PARAM_AT[name][1]]

        def slices(ap):
            return ap.rearrange("p (s t) -> p s t", s=3)

        def three(bank_set):
            return ps[:, 3 * bank_set:3 * bank_set + 3, 0:SL]

        def col(first, n):
            return par[:, bass.ds(n + first, 1)]

        def at_chunk(t, n):
            return t[:, bass.ds(n, 1), :].rearrange("p o c -> p (o c)")

        def one(ap, index):
            return ap[bass.ds(index, 1)].rearrange("o p n -> (o p) n")

        sqA = [PT[:, 0, 0:N], PT[:, 1, 0:N]]
        sqA_sum = PT[:, 2, 0:N]

        ones, ident, bones = const("ones"), const("ident"), const("headsum")

        dve_step, act_step = sem("dve_step"), sem("act_step")
        consts_in, small_out = sem("consts_in"), sem("small_out")
        x_in = [sem(f"x_in{i}") for i in range(4)]
        raw_in = [sem(f"raw_in{i}") for i in range(4)]
        zeros_set, silu_c, ada_used, mod_ready = sem("zeros_set"), sem("silu_c"), sem("ada_used"), sem("mod_ready")
        sq_ready, sumsq_ready, std_ready = sem("sq_ready"), sem("sumsq_ready"), sem("std_ready")
        sq_used = sem("sq_used")
        h_ready, h_hi, h_lo = sem("h_ready"), sem("h_hi"), sem("h_lo")
        w_hi, w_lo = sem("w_hi"), sem("w_lo")
        proj_ready, proj_out = sem("proj_ready"), sem("proj_out")
        S = {}
        LAST_LEVEL = len(LEVELS) - 1
        GROUPS = [("M", "aT"), ("MT", "NbT", "bT"), ("MkT", "NkT", "kT")]
        for n in range(len(LEVELS)):
            GROUPS += [(f"Y{n}",), (f"Z{n}",) if n < LAST_LEVEL else ("W1",), (f"ZT{n}",)]
        GROUPS += [("G", "H"), ("A", "RG"), ("E",), ("O",)]
        FIRST_BANK = {0: (0, 2), 1: (4, 0), 2: (4, 0), len(GROUPS) - 4: (0, 2), len(GROUPS) - 3: (0, 2),
                      len(GROUPS) - 2: (0, 1), len(GROUPS) - 1: (2, 3)}
        for n in range(3, len(GROUPS) - 4):
            FIRST_BANK[n] = (2 * n - 2) % 4, (2 * n - 1) % 4
        STEPS = [x for group in GROUPS for x in group]
        GROUP_OF = {x: n for n, group in enumerate(GROUPS) for x in group}
        ON_ACT = {"aT", "bT", "kT", "W1", "H", "E", "O"} | {f"Y{n}" for n in range(len(LEVELS))}
        halves = [(x, half) for group in GROUPS for half in range(2) for x in group]
        dve_steps = [(x, half) for x, half in halves if x not in ON_ACT]
        act_steps = [(x, half) for x, half in halves if x in ON_ACT]

        def evacuated(name, pair, half):
            order = act_steps if name in ON_ACT else dve_steps
            return s("unit_act" if name in ON_ACT else "unit_dve"), pair * len(order) + order.index((name, half)) + 1

        def computed(name, pair, half):
            return s("unit_mm"), (pair * len(GROUPS) + GROUP_OF[name]) * 2 + half + 1

        def y_copies(pair, level, half):
            return (pair * len(LEVELS) + level) * 2 + half + 1

        def t_copies(pair, level, half):
            return (pair * (len(LEVELS) + 1) + level) * 2 + half + 1

        WIDTH = {1: 1, 2: 2, 3: 4}

        def banks_of(group, half):
            first = FIRST_BANK[group][half]
            return range(first, first + WIDTH[len(GROUPS[group])])

        def results(name, half):
            n, x = GROUP_OF[name], GROUPS[GROUP_OF[name]].index(name)
            b = banks_of(n, half)
            all_of = ps[:, b[0]:b[-1] + 1, :].rearrange("p b (c s) -> p (b c) s", s=len(b) * C)
            return all_of[:, :, x * C:(x + 1) * C]

        def before_in(bank, group, half):
            for back in range(1, 2 * len(GROUPS) + 1):
                g = group * 2 + half - back
                n, h = g // 2 % len(GROUPS), g % 2
                if bank in banks_of(n, h):
                    return n, h, g < 0
            return None

        EARLY = {"ZT0": ["decay"], "ZT1": ["rate"], "ZT2": ["log"], "ZT3": ["norm"], "ZT4": ["kk", "bonus"]}
        SAMPLE_STEPS = 5
        LATE = {0: "cum", 2: "alpha", 4: "beta", 6: "kappa", 8: "values"}

        def overlapped(chain, prep):
            order = []
            if not chain:
                first = [piece for pieces in EARLY.values() for piece in pieces]
                for n, piece in enumerate(first):
                    order.append((piece, None))
                    if n < SAMPLE_STEPS:
                        order.append(("sample", n))
            for c in range(NCH):
                if prep and c in LATE:
                    order.append((LATE[c], None))
                if chain:
                    order.append(("chain", c))
            if prep:
                order.append(("ends", None))
            return order

        def s(name):
            if name not in S:
                S[name] = sem(name)
            return S[name]

        JOBS = 2 * FC + KD * (FC // 2)
        block = ctx.enter_context(nc.Block())
        ADA_A, ADA_B = 16, 32

        @block.sync
        def _(sp):
            def dma(dst, src, signal):
                return nc.sync.dma_start(dst, src).then_inc(signal, 16)

            dma(cT[:], io["cT"], s("c_in"))
            for n in range(4):
                dma(raw[:, n], io["ada"][n], raw_in[n])
            for i, (dst, src) in enumerate([(cst, "consts"), (lvl, "levels"), (par, "params"), (shift_st, "shift_st"),
                                            (lora, "lora"), (g_up, "g_up")]):
                dma(dst[:], io[src], consts_in)
            for i in range(4):
                dma(xT[:, 2 * i:2 * i + 2], io["xT"][:, 2 * i:2 * i + 2], x_in[i])

            def load(tile, slot, used, count):
                sp.wait_ge(used, count)
                dma(raw[:, slot], tile, raw_in[slot])

            def tiles(name, first, count, used):
                with sp.Fori(0, (count - first) // 4) as i:
                    for j in range(4):
                        load(one(io[name], i * 4 + (first + j)), j, used, i * 4 + (first - 3 + j))

            tiles("ada", 4, ADA_A, ada_used)
            for n in range(4):
                load(io["w_in"][n], n, ada_used, ADA_A - 3 + n)
            tiles("w_in", 4, PC, w_lo)
            for n in range(4):
                load(io["ada"][ADA_A + n], n, w_lo, PC - 3 + n)
            sp.wait_ge(s("shift_saved"), 1)
            dma(io["o_shift"], tail_shift[:], small_out)
            dma(io["o_ks"][:, 0:P - 1, :], io["cache_k"][:, 1:P, :], s("cache_out"))
            dma(io["o_vs"][:, 0:P - 1, :], io["cache_v"][:, 1:P, :], s("cache_out"))
            sp.wait_ge(s("kvrow_ready"), 1)
            dma(io["o_ks"][:, P - 1, :], kvrow[:, 0, :], s("cache_out"))
            dma(io["o_vs"][:, P - 1, :], kvrow[:, 1, :], s("cache_out"))
            dma(io["o_kvp"], PT[:, 18:20, PW - NS - P:PW - NS], s("kvp_out"))
            sp.wait_ge(s("cache_out"), 64)
            dma(Kf[:], io["o_ks"].rearrange("b s d -> s b d"), s("cache_in"))
            dma(Vf[:], io["o_vs"].rearrange("b s d -> s b d"), s("cache_in"))
            with sp.Fori(0, (ADA_B - 4) // 4) as i:
                for j in range(4):
                    load(one(io["ada"], i * 4 + (ADA_A + 4 + j)), j, ada_used, i * 4 + (ADA_A + 1 + j))
            sp.wait_ge(s("sm48_ready"), 1)
            dma(scr_a.rearrange("q b c -> (q b) c"), SM48, s("scr_out"))
            sp.wait_ge(s("scr_out"), 16)
            sp.wait_ge(s("ends_ready"), NJ)
            dma(sWKV, io["wkv"].rearrange("p (v k) -> p v k", k=HD), s("wkv_in"))
            for vh in range(2):
                dma(V6[64 * vh:64 * vh + 64], scr_a.rearrange("q b (h k) -> (b h) q k", k=HD), s("wkv_in"))
                dma(V32[64 * vh:64 * vh + 64], scr_a[5].rearrange("b (h u v) -> (b h) u v", u=2, v=32)[:, vh], s("wkv_in"))
            sp.wait_ge(s("sample_o"), 1)
            dma(io["o_wkvs"], sWKV, s("wkvs_out"))
            for vh in range(2):
                dma(scr_o.rearrange("b h u v -> (b h) u v")[:, vh], Osm[64 * vh:64 * vh + 64], s("scro_out"))
            sp.wait_ge(s("scro_out"), 32)
            dma(OR, scr_o.rearrange("b h u v -> b (h u v)"), s("or_in"))
            sp.wait_ge(s("state_ready"), NJ * NCH)
            dma(io["o_wkvp"], WO[:], s("states_out"))
            sp.wait_ge(s("o_sample"), 1)
            sp.wait_ge(s("states_out"), 16)
            sp.wait_ge(s("wkvs_out"), 16)
            for n in range(4):
                dma(raw[:, n], io["w_out"][n], raw_in[n])
            for n in range(4, KD):
                sp.wait_ge(w_lo, PC + n - 3)
                dma(raw[:, n % 4], io["w_out"][n], raw_in[n % 4])
            sp.wait_ge(s("mix_lo_a"), NJ)
            sp.wait_ge(s("mix_lo_r"), NJ)
            dma(X2[:], io["xT"], s("x2_in"))
            sp.wait_ge(w_lo, PC + KD)
            sp.wait_ge(s("out_ready"), KD)

            def tile(src, slot, count):
                if count is not None:
                    sp.wait_ge(s("w3_lo"), count)
                dma(raw3[:, slot], src, s(f"raw3_in{slot}"))

            for m, c in enumerate((0, FC, 1, FC + 1)):
                if m == 3:
                    for k in range(KD):
                        sp.wait_ge(s("x1_ready"), k + 1)
                        dma(x1_dram[:, k], X2[:, k], s("x1_out"))
                tile(io["up"][c], m % 3, None if m < 3 else m - 2)
            sp.wait_ge(s("h2_lo"), KD)
            dma(conv_st[:], io["conv_st"], s("conv_in"))
            with sp.Fori(1, FC // 2) as i:
                for x, (name, off) in enumerate((("up", 0), ("down", -2), ("down", -1), ("up", FC), ("up", 1),
                                                 ("up", FC + 1))):
                    tile(one(io[name], i * 2 + off), (1 + x) % 3, i * 6 + (x - 4))
            for x in range(2):
                tile(io["down"][FC - 2 + x], (1 + x) % 3, 3 * FC + x - 4)
            sp.wait_ge(s("x1_out"), 16 * KD)
            sp.wait_ge(s("ffn_mm"), JOBS - KD)
            dma(X1[:], x1_dram, s("x1_in"))
            sp.wait_ge(s("conv_done"), 2 * FC)
            dma(io["o_tail"], ftail[:], small_out)
            dma(io["o_prev"], conv_st[:, 1], small_out)
            for k in range(KD):
                sp.wait_ge(s("y_ready"), k + 1)
                dma(io["o_y"][:, k], acc[:, k], s("y_out"))
            sp.wait_ge(s("y_out"), 16 * KD)
            sp.wait_ge(small_out, 16 * 3)
            sp.wait_ge(s("kvp_out"), 16)


        XG = [PT[:, 12, PO:PW], PT[:, 18, PO:PW], dif[:, 0], dif[:, 1]]
        POOL_FROM = 5

        @block.tensor
        def _(pe):
            def ada_tile(n, bank, loads):
                pe.wait_ge(raw_in[n % 4], loads * 16)
                for x in range(2):
                    k = n % 4 * 2 + x
                    mm = nc.tensor.matmul(ps[0:9, bank, :], cTs[:, k, :], raw[:, n % 4, x * 512:(x + 1) * 512],
                                          start=(k == 0), stop=(k == KD - 1))
                mm.then_inc(ada_used, 1)

            def ada_turn(g, bank, at):
                pe.wait_ge(s("ada_row"), g + 1)
                for i in range(4):
                    mm = nc.tensor.transpose(ps[:, bank, at + i * 9:at + i * 9 + 9], ada_row[:, i * P:(i + 1) * P],
                                             ident[0:9, 0:9])
                mm.then_inc(s("ada_turned"), 1)

            def product(bank_set, w, x, x_ready=None, order=range(KD)):
                for k in order:
                    if x_ready is not None:
                        pe.wait_ge(*x_ready(k))
                    for n, (a, b) in enumerate(((0, 0), (0, 1), (1, 0))):
                        for t in range(3):
                            mm = nc.tensor.matmul(ps[:, 3 * bank_set + t, 0:SL], w[:, a, k * P:(k + 1) * P],
                                                  x[:, k, b, t * SL:(t + 1) * SL],
                                                  start=(k == order[0] and n == 0), stop=(k == order[-1] and n == 2))
                return mm

            pe.wait_ge(silu_c, 1)
            for g in range(ADA_A // 4):
                for x in range(4):
                    ada_tile(4 * g + x, 6 + g % 2, g + 1)
                if g == 1:
                    pe.wait_ge(consts_in, 16 * 6)
                    pe.wait_ge(sq_used, KD)
                    for t in range(3):
                        mm = nc.tensor.matmul(ps[:, 3 + t, 0:SL], ones, sqA_sum[:, t * SL:(t + 1) * SL], start=True,
                                              stop=True)
                    mm.then_inc(sumsq_ready, 1)
                if g >= 1:
                    ada_turn(g - 1, 0, (g - 1) * 36)
            ada_turn(ADA_A // 4 - 1, 0, ADA_A * 9 - 36)
            for n in range(4):
                pe.wait_ge(w_lo, n + 1)
                if n >= 2:
                    pe.wait_ge(proj_out, n - 1)
                product(n % 2, spl[:, n % 2], XS[:], (lambda k: (h_lo, k + 1)) if n == 0 else None).then_inc(proj_ready, 1)
            with pe.Fori(0, (PC - 4) // 2) as i:
                for j in range(2):
                    pe.wait_ge(w_lo, i * 2 + (5 + j))
                    pe.wait_ge(proj_out, i * 2 + (3 + j))
                    product(j, spl[:, j], XS[:]).then_inc(proj_ready, 1)
            pe.wait_ge(proj_out, PC)
            for n, c in enumerate((18, 14, 15, 16, 17)):
                if n >= 2:
                    pe.wait_ge(s("rotated"), n - 1)
                for t in range(3):
                    mm = nc.tensor.matmul(ps[:, 3 * (n % 2) + t, 0:SL], const("swap"),
                                          PT[:, c, PO + t * SL:PO + (t + 1) * SL], start=True, stop=True)
                mm.then_inc(s("swapped"), 1)
                if n in (0, 1):
                    if n == 1:
                        pe.wait_ge(s("v_turned"), 1)
                    for i in range(4):
                        mm = nc.tensor.transpose(ps[:, 6, i * P:(i + 1) * P],
                                                 PT[:, 19, PO + (4 * n + i) * P:PO + (4 * n + i + 1) * P], ident)
                    mm.then_inc(s("v_turns"), 1)
            pe.wait_ge(s("v_turned"), 2)
            pe.wait_ge(s("rotated"), 1)
            for i, c in enumerate((18, 19)):
                mm = nc.tensor.transpose(ps[0:NS, 6, i * P:(i + 1) * P], PT[:, c, PO + T:PW], ident)
            mm.then_inc(s("kvrow_turned"), 1)

            def scores(u):
                i, kv = u // 2, u % 2
                lo = P if i == 0 else 0
                if u < 2:
                    pe.wait_ge(s("k_padded"), kv + 1)
                if u >= 2:
                    pe.wait_ge(s("masked"), u - 1)
                for j in range(4):
                    mm = nc.tensor.matmul(ps[:, 2 * (u % 2) + j // 2, (j % 2) * 2 * P + lo:(j % 2 + 1) * 2 * P],
                                          PT[:, 14 + j, PO + i * P:PO + (i + 1) * P],
                                          Kz[:, kv, (i - 1) * P + lo:(i + 1) * P], start=True, stop=True)
                mm.then_inc(s("scored"), 1)

            def turn_probs(u):
                i = u // 2
                pe.wait_ge(s("probs"), u + 1)
                if u >= 1:
                    pe.wait_ge(s("probs_turned"), u)
                for j in range(4):
                    for kt in range(2):
                        if i == 0 and kt == 0:
                            continue
                        mm = nc.tensor.transpose(ps[:, 4 + j // 2, ((j % 2) * 2 + kt) * P:((j % 2) * 2 + kt + 1) * P],
                                                 S4[:, u % 3, j, kt * P:(kt + 1) * P], ident)
                mm.then_inc(s("probs_turns"), 1)

            def values(u):
                i, kv = u // 2, u % 2
                pe.wait_ge(s("probs_turned"), u + 1)
                if u >= 1:
                    pe.wait_ge(s("mixed"), u)
                else:
                    pe.wait_ge(s("kvrow_ready"), 1)
                kts = (1,) if i == 0 else (0, 1)
                for j in range(4):
                    for kt in kts:
                        mm = nc.tensor.matmul(ps[HD * kv:HD * kv + HD, 6, j * P:(j + 1) * P],
                                              VA[:, i - 1 + kt, HD * kv:HD * kv + HD], PR[:, u % 2, j, kt, :],
                                              start=(kt == kts[0]), stop=(kt == 1))
                mm.then_inc(s("valued"), 1)

            pe.wait_ge(s("rotated"), 5)
            pe.wait_ge(mod_ready, 1)
            scores(0)
            scores(1)
            for u in range(2 * NT):
                if u + 2 < 2 * NT:
                    scores(u + 2)
                g = (ADA_A + 2 * u) // 4
                if u % 2 == 0 and u >= 2:
                    ada_turn(g - 1, 7, 0)
                turn_probs(u)
                if u % 2 == 0 and u >= 2:
                    pe.wait_ge(s("mod_added"), g - ADA_A // 4)
                for n in (2 * u, 2 * u + 1):
                    ada_tile(n, 7, (ADA_A + PC) // 4 + n // 4 + 1)
                values(u)
            ada_turn((ADA_A + ADA_B) // 4 - 1, 7, 0)
            def sample_attention(n):
                if n == 0:
                    pe.wait_ge(s("cache_in"), 32)
                    pe.wait_ge(s("masked"), 2 * NT)
                    for b in range(NS):
                        mm = nc.tensor.transpose(ps[:, b // 4, (b % 4) * P:(b % 4 + 1) * P], Kf[:, b, :], ident)
                    mm.then_inc(s("sk_turns"), 1)
                elif n == 1:
                    pe.wait_ge(s("sk_turned"), 1)
                    for b in range(NS):
                        for kv in range(2):
                            h = slice(HD * kv, HD * kv + HD)
                            mm = nc.tensor.matmul(ps[:, 2 + kv, b * 4:b * 4 + 4], KTs[h, b, :],
                                                  PT[h, 14:18, PO + T + b], start=True, stop=True)
                    mm.then_inc(s("s_scored"), 1)
                elif n == 2:
                    pe.wait_ge(s("s_copied"), 1)
                    nc.tensor.transpose(ps[0:64, 0, 0:P], sS[:], ident).then_inc(s("s_turns"), 1)
                elif n == 3:
                    pe.wait_ge(s("s_probs"), 1)
                    nc.tensor.transpose(ps[:, 2, 0:64], sP[:], ident[0:64, 0:64]).then_inc(s("s_turns"), 1)
                elif n == 4:
                    pe.wait_ge(s("s_turned"), 1)
                    for b in range(NS):
                        for kv in range(2):
                            mm = nc.tensor.matmul(ps[HD * kv:HD * kv + HD, 1, b * 4:b * 4 + 4],
                                                  Vf[:, b, HD * kv:HD * kv + HD], sPT[:, b * 8 + kv * 4:b * 8 + kv * 4 + 4],
                                                  start=True, stop=True)
                    mm.then_inc(s("s_valued"), 1)
                    pe.wait_ge(s("s_mixed"), 1)

            def by_head_sum(bank, src):
                for t in range(3):
                    mm = nc.tensor.matmul(ps[:, bank + t, 0:SL], bones, src[:, t * SL:(t + 1) * SL],
                                          start=True, stop=True)
                return mm

            def prepare(piece, j):
                cols = slice(j * P, (j + 1) * P)
                if piece in ("decay", "rate"):
                    if piece == "rate":
                        pe.wait_ge(s("sig_decay"), j + 1)
                    elif j == 0:
                        pe.wait_ge(s("tanh_w"), 1)
                        pe.wait_ge(s("mixed"), 2 * NT)
                    else:
                        for name in GROUPS[GROUP_OF["MkT"]]:
                            pe.wait_ge(*evacuated(name, j - 1, 0))
                    h = slice(0, 64) if piece == "decay" else slice(64, P)
                    for t in range(3):
                        mm = nc.tensor.matmul(ps[:, 4 + t, 0:SL], lora[h, cols], PT[h, 12, PO + t * SL:PO + (t + 1) * SL],
                                              start=True, stop=True)
                    mm.then_inc(s("p_" + piece), 1)
                elif piece == "log":
                    pe.wait_ge(s("sig_rate"), j + 1)
                    for i in range(NT):
                        mm = nc.tensor.transpose(ps[:, 4 + i // 4, (i % 4) * P:(i % 4 + 1) * P],
                                                 F0[:, i * P:(i + 1) * P], ident)
                    mm.then_inc(s("p_sgt"), 1)
                elif piece == "norm":
                    pe.wait_ge(s("sgt_copied"), j + 1)
                    by_head_sum(4, F3).then_inc(s("p_norm"), 1)
                elif piece == "cum":
                    pe.wait_ge(s("bonus"), j + 1)
                    for m in range(4):
                        if m == 3:
                            pe.wait_ge(s("decays"), j * 4 + 1)
                        for i in (2 * m, 2 * m + 1):
                            mm = nc.tensor.matmul(ps[:, 4 + m % 3, (i % 2) * 2 * P:(i % 2 + 1) * 2 * P], SGt[:, i],
                                                  const("cumsum"), start=True, stop=True)
                        mm.then_inc(s("p_cum"), 1)
                elif piece == "bonus":
                    pe.wait_ge(s("k_floor"), j + 1)
                    pe.wait_ge(s("rkk"), j + 1)
                    by_head_sum(4, F0).then_inc(s("p_bonus"), 1)
                elif piece == "values":
                    pe.wait_ge(s("decays"), 4 * (j + 1))
                    for c in range(NCH):
                        for hh in range(2):
                            h = slice(HD * hh, HD * hh + HD)
                            mm = nc.tensor.matmul(ps[h, 4 + c // 8, (c % 8) * C:(c % 8 + 1) * C],
                                                  PT[h, 8 + j, PO + c * C:PO + (c + 1) * C], ident[h, h],
                                                  start=True, stop=True)
                    mm.then_inc(s("p_values"), 1)

            def chunks(j):
                def tiles_of(half):
                    for c in range(8 * half, 8 * half + 8):
                        for hh in range(2):
                            yield slice(HD * hh, HD * hh + HD), c

                def free_banks(group, half):
                    for bank in banks_of(group, half):
                        n, h, earlier = before_in(bank, group, half)
                        if not earlier or j >= 1:
                            for name in GROUPS[n]:
                                pe.wait_ge(*evacuated(name, j - earlier, h))

                def step(name, half, *terms):
                    free_banks(GROUP_OF[name], half)
                    for h, c in tiles_of(half):
                        out = results(name, half)[h, c % 8]
                        for i, (a, b) in enumerate(terms):
                            mm = nc.tensor.matmul(out, a[h, c], b[h, c], start=(i == 0), stop=(i == len(terms) - 1))
                    mm.then_inc(s("unit_mm"), 1)

                def both(name, half, stationary, moving):
                    group = GROUP_OF[name]
                    free_banks(group, half)
                    bank = banks_of(group, half)[0]
                    flat = moving.rearrange("p u c -> p (u c)")
                    for c in range(8 * half, 8 * half + 8):
                        n = C if c % 8 == 7 else 2 * C
                        mm = nc.tensor.matmul(ps[:, bank, c % 8 * C:c % 8 * C + n], stationary[:, c],
                                              flat[:, c * C:c * C + n], start=True, stop=True)
                    mm.then_inc(s("unit_mm"), 1)

                def wide(name, half, stationary, moving):
                    group = GROUP_OF[name]
                    free_banks(group, half)
                    n, first = len(GROUPS[group]), banks_of(group, half)[0]
                    per = 8 // WIDTH[n]
                    for c in range(8 * half, 8 * half + 8):
                        at = c % per * (C * 8 // per)
                        mm = nc.tensor.matmul(ps[:, first + c % 8 // per, at:at + n * C], stationary[:, c],
                                              moving[:, :, c], start=True, stop=True)
                    mm.then_inc(s("unit_mm"), 1)

                pe.wait_ge(s("alpha_bd"), j + 1)
                pe.wait_ge(s("beta_bd"), j + 1)
                pe.wait_ge(s("eyes"), j + 1)
                for half in range(2):
                    wide("M", half, AB, BETA_T)
                pe.wait_ge(s("ends_ready"), j + 1)
                pe.wait_ge(s("v_tokens"), j + 1)
                if j == NJ - 1:
                    pe.wait_ge(s("sm48_ready"), 1)
                for half in range(2):
                    wide("MT", half, BB, ALPHA_R_AFF)
                for half in range(2):
                    wide("MkT", half, KB, ALPHA_R_AFF)
                for n in range(len(LEVELS)):
                    before = "MT" if n == 0 else f"ZT{n - 1}"
                    for half in range(2):
                        pe.wait_ge(*evacuated("MT", j, half))
                        pe.wait_ge(*evacuated("M" if n == 0 else f"Z{n - 1}", j, half))
                        both(f"Y{n}", half, BB, Tm)
                    for half in range(2):
                        if n < LAST_LEVEL:
                            pe.wait_ge(*evacuated(f"Y{n}", j, half))
                            pe.wait_ge(*evacuated(before, j, half))
                            pe.wait_ge(s("t_first"), t_copies(j, n, half))
                            both(f"Z{n}", half, TB, Yc)
                        else:
                            pe.wait_ge(*evacuated("MkT", j, half))
                            both("W1", half, KB, vTm)
                    for half in range(2):
                        pe.wait_ge(*evacuated(f"Y{n}", j, half))
                        pe.wait_ge(s("y_second"), y_copies(j, n, half))
                        pe.wait_ge(*evacuated(before, j, half))
                        both(f"ZT{n}", half, AB, TT)
                    if j + 1 < NJ:
                        for piece in EARLY[f"ZT{n}"]:
                            prepare(piece, j + 1)
                for half in range(2):
                    pe.wait_ge(*evacuated(f"ZT{LAST_LEVEL}", j, half))
                    pe.wait_ge(s("t_first"), t_copies(j, LAST_LEVEL + 1, half))
                    pe.wait_ge(*evacuated("W1", j, half))
                    wide("G", half, TB, A_W1)
                for half in range(2):
                    pe.wait_ge(*evacuated("G", j, half))
                    wide("A", half, BB, B_NBT)
                for half in range(2):
                    pe.wait_ge(*evacuated("H", j, half))
                    step("E", half, (bTm, hm(j)), (kTm, vTm))

                def chain(c):
                    if c >= 1:
                        pe.wait_ge(s("state_ready"), j * NCH + c)
                        for hh in range(2):
                            h = slice(HD * hh, HD * hh + HD)
                            mm = nc.tensor.matmul(ps[h, 7, 0:C], Aff[h, c], St[h, c], start=True, stop=True)
                        mm.then_inc(s("state_mm"), 1)
                    if c % 8 == 0:
                        free_banks(GROUP_OF["O"], c // 8)
                    if c == 0:
                        pe.wait_ge(*evacuated("RG", j, 1))
                    for hh in range(2):
                        h = slice(HD * hh, HD * hh + HD)
                        out = results("O", c // 8)[h, c % 8]
                        nc.tensor.matmul(out, hm(j)[h, c], NbT[h, c], start=True, stop=False)
                        mm = nc.tensor.matmul(out, vTm[h, c], NkT[h, c], start=False, stop=(c == 0))
                        if c >= 1:
                            mm = nc.tensor.matmul(out, St[h, c], R[h, c], start=False, stop=True)
                    if c % 8 == 7:
                        mm.then_inc(s("unit_mm"), 1)

                return chain

            chain = None
            for j in range(NJ + 1):
                for piece, c in overlapped(chain is not None, j < NJ):
                    if piece == "chain":
                        chain(c)
                    elif piece == "sample":
                        sample_attention(c)
                    else:
                        prepare(piece, j)
                if j == NJ - 1:
                    pe.wait_ge(s("smp_ready"), NJ)
                    for x in range(NJ):
                        mm = nc.tensor.transpose(ps[0:48, 6, x * P:(x + 1) * P], SMP[:, x].rearrange("p q b -> p (q b)"),
                                                 ident)
                    mm.then_inc(s("smp_turns"), 1)
                if j < NJ:
                    chain = chunks(j)
            pe.wait_ge(s("or_in"), 16)
            for j in range(NJ):
                mm = nc.tensor.transpose(ps[:, 5, j * NS:(j + 1) * NS], OR[:, j * P:(j + 1) * P], ident[0:NS, 0:NS])
            mm.then_inc(s("or_turns"), 1)

            pe.wait_ge(s("o_sample"), 1)
            pe.wait_ge(*evacuated("O", NJ - 1, 1))
            pe.wait_ge(s("sig_g"), 1)
            def gn_gate(j, bank):
                for t in range(3):
                    mm = nc.tensor.matmul(ps[:, bank + t, 0:SL], g_up[:, j * P:(j + 1) * P],
                                          PT[:, 13, PO + t * SL:PO + (t + 1) * SL], start=True, stop=True)
                mm.then_inc(s("gn_gate"), 1)

            def gn_mean(j, bank):
                by_head_sum(bank, PT[:, 8 + j, PO:PW]).then_inc(s("gn_mean"), 1)

            def gn_var(j, bank):
                pe.wait_ge(s("gn_square"), j + 1)
                by_head_sum(bank, XG[j]).then_inc(s("gn_var"), 1)

            gn_mean(0, 0)
            gn_mean(1, 3)
            pe.wait_ge(s("centred"), 1)
            gn_var(0, 0)
            pe.wait_ge(s("centred"), 2)
            gn_mean(2, 3)
            pe.wait_ge(s("gn_log"), 1)
            gn_var(1, 0)
            pe.wait_ge(s("centred"), 3)
            gn_mean(3, 3)
            pe.wait_ge(s("gn_log"), 2)
            gn_var(2, 0)
            pe.wait_ge(s("centred"), 4)
            gn_gate(0, 3)
            pe.wait_ge(s("gn_log"), 3)
            gn_var(3, 0)
            pe.wait_ge(s("gated"), 1)
            gn_gate(1, 3)
            pe.wait_ge(s("gn_log"), 4)
            gn_gate(2, 0)
            pe.wait_ge(s("gated"), 2)
            gn_gate(3, 3)
            def mixed(k):
                return (s("mix_lo_a"), k - 3) if k >= 4 else (s("mix_lo_r"), k + 1)

            mix_order = list(range(4, KD)) + list(range(4))
            for n in range(KD):
                pe.wait_ge(w_lo, PC + n + 1)
                if n < 2:
                    pe.wait_ge(s("gated"), n + 3)
                else:
                    pe.wait_ge(s("out_out"), n - 1)
                product(n % 2, spl[:, n % 2], XS[:], mixed if n == 0 else None, mix_order).then_inc(s("out_ready"), 1)

            def total_of_squares(bank_set, most, added, last, count):
                pe.wait_ge(s("sq_added"), added)
                for src, start in ((most, True), (last, False)):
                    if not start:
                        pe.wait_ge(s("sq_c"), count)
                    for t in range(3):
                        mm = nc.tensor.matmul(ps[:, 3 * bank_set + t, 0:SL], ones, src[:, t * SL:(t + 1) * SL],
                                              start=start, stop=not start)
                mm.then_inc(s("sq_total"), 1)

            pe.wait_ge(s("out_out"), KD)
            total_of_squares(0, sqs, KD - 1, sq2[:, (KD - 1) % 2], KD)
            for k in range(KD):
                pe.wait_ge(s("sq_c"), KD + k + 1)
                for t in range(3):
                    mm = nc.tensor.matmul(ps[:, 3 + t, 0:SL], ones, sq2[:, k % 2, t * SL:(t + 1) * SL],
                                          start=(k == 0), stop=(k == KD - 1))
                mm.then_inc(s("sq_summed"), 1)
            pe.wait_ge(s("std2"), 2)

            def up(i, x, off, w3, waits):
                pe.wait_ge(s("w3_lo"), w3)
                for name, count in waits:
                    pe.wait_ge(s(name), count)
                product(off % 2, spl3[:, (1 + x) % 3], XS[:]).then_inc(s("ffn_mm"), 1)

            def down(i, w3):
                pe.wait_ge(s("w3_lo"), w3)
                pe.wait_ge(s("g_lo"), i * 2)
                for k in range(KD):
                    y = k + 1
                    if y == 1:
                        pe.wait_ge(s("up_out"), i * 4)
                    elif y == 2:
                        pe.wait_ge(s("up_out"), up2(i))
                    else:
                        pe.wait_ge(s("down_out"), i * 8 + (y - 10))
                    first = down_slot(i)
                    for f in range(2):
                        w = spl3[:, (first + f) % 3]
                        for n, (a, b) in enumerate(((0, 0), (0, 1), (1, 0))):
                            for t in range(3):
                                mm = nc.tensor.matmul(ps[:, 3 * (down_set(i, y)) + t, 0:SL], w[:, a, k * P:(k + 1) * P],
                                                      act2[:, f, b, t * SL:(t + 1) * SL],
                                                      start=(f == 0 and n == 0), stop=(f == 1 and n == 2))
                    mm.then_inc(s("ffn_mm"), 1)

            LAST = FC // 2

            def is_last(i):
                return isinstance(i, int) and i == LAST

            def up2(i):
                return i * 4 if is_last(i) else i * 4 + 1

            def down_slot(i):
                return 1 if is_last(i) else 2

            def down_set(i, y):
                return (y - 1) % 2 if is_last(i) else y % 2

            for m in range(4):
                pe.wait_ge(s("w3_lo"), m + 1)
                if m >= 2:
                    pe.wait_ge(s("up_out"), m - 1)
                product(m % 2, spl3[:, m % 3], XS[:], (lambda k: (s("h2_lo"), k + 1)) if m == 0 else None
                        ).then_inc(s("ffn_mm"), 1)
            with pe.Fori(1, LAST) as i:
                up(i, 0, 0, i * 6 - 1, [("up_out", i * 4 - 1)])
                down(i, i * 6 + 1)
                up(i, 3, 9, i * 6 + 2, [("down_out", i * 8 - 1)])
                up(i, 4, 10, i * 6 + 3, [("down_out", i * 8)])
                up(i, 5, 11, i * 6 + 4, [("up_out", i * 4 + 2)])
            down(LAST, 3 * FC)
            pe.wait_ge(s("down_out"), KD * LAST)
            total_of_squares(0, sqF, 2 * (KD - 1), Z[:, (KD - 1) % 2], 3 * KD)

        @block.scalar
        def _(act):
            mark = [0]

            def link(ins):
                mark[0] += 1
                ins.then_inc(act_step, 1)
                act.wait_ge(act_step, mark[0])

            def inverse_root(dst, src, bias, scale):
                link(nc.scalar.activation(dst, src, ACT.Ln, bias=bias, scale=scale))
                return nc.scalar.activation(dst, dst, ACT.Exp, scale=-0.5)

            act.wait_ge(s("c_in"), 16)
            nc.scalar.activation(cTs[:], cT[:], ACT.Silu).then_inc(silu_c, 1)

            def ada_out(g, bank):
                act.wait_ge(ada_used, 4 * (g + 1))
                if g >= 1:
                    act.wait_ge(s("ada_turned"), g)
                nc.scalar.activation(ada_row[:], ps[0:9, bank, :], ACT.Copy).then_inc(s("ada_row"), 1)

            for k in range(KD):
                if k >= 2:
                    act.wait_ge(sq_used, k - 1)
                if k % 2 == 0:
                    act.wait_ge(x_in[k // 2], 16)
                nc.scalar.activation(sqA[k % 2], xT[:, k], ACT.Square).then_inc(sq_ready, 1)
            act.wait_ge(zeros_set, 1)
            ada_out(0, 6)
            act.wait_ge(sumsq_ready, 1)
            inverse_root(slices(rs[:]), three(1), eps[:, 0:1], 1.0 / D).then_inc(std_ready, 1)
            for g in range(1, ADA_A // 4):
                ada_out(g, 6 + g % 2)
            def whi(slot2, slot4):
                nc.scalar.activation(spl[:, slot2, 0], raw[:, slot4], ACT.Copy).then_inc(w_hi, 1)
            for n in range(2):
                act.wait_ge(raw_in[n], (ADA_A // 4 + 1) * 16)
                whi(n, n)
            for k in range(KD):
                act.wait_ge(h_ready, k + 1)
                nc.scalar.activation(XS[:, k, 0], xT[:, k], ACT.Copy).then_inc(h_hi, 1)

            def evac(n, bank_set):
                nc.scalar.activation(PT[:, bass.ds(n, 1), PO:PW].rearrange("p o (s t) -> p (o s) t", s=3),
                                     three(bank_set), ACT.Copy).then_inc(proj_out, 1)

            for n in range(2):
                act.wait_ge(proj_ready, n + 1)
                act.wait_ge(raw_in[n + 2], (ADA_A // 4 + 1) * 16)
                whi(n, n + 2)
                evac(n, n)
            with act.Fori(0, (PC - 4) // 4) as i:
                for j in range(4):
                    act.wait_ge(proj_ready, i * 4 + (3 + j))
                    act.wait_ge(raw_in[j], (i + (ADA_A // 4 + 2)) * 16)
                    whi(j % 2, j)
                    evac(i * 4 + (2 + j), j % 2)
            for n in range(PC - 2, PC):
                act.wait_ge(proj_ready, n + 1)
                evac(n, n % 2)

            nc.scalar.dma_start(rope[:], io["rope"]).then_inc(s("rope_in"), 16)
            for n in range(2):
                act.wait_ge(s("v_turns"), n + 1)
                nc.scalar.activation(VA[:, 4 * n:4 * n + 4, :], ps[:, 6, :].rearrange("p (i c) -> p i c", c=P),
                                     ACT.Copy).then_inc(s("v_turned"), 1)
            act.wait_ge(s("kvrow_turned"), 1)
            nc.scalar.activation(kvrow[:], ps[0:NS, 6, 0:2 * P].rearrange("p (i c) -> p i c", c=P),
                                 ACT.Copy).then_inc(s("kvrow_ready"), 1)

            act.wait_ge(s("rotated"), 1)
            act.wait_ge(s("k_zeros"), 2)
            for kv in range(2):
                h = slice(HD * kv, HD * kv + HD)
                nc.scalar.activation(Kz[h, kv, :], PT[h, 18, PO:PO + T], ACT.Copy).then_inc(s("k_padded"), 1)

            def exps(u):
                i = u // 2
                lo = P if i == 0 else 0
                act.wait_ge(s("maxed"), u + 1)
                for j in range(4):
                    nc.scalar.activation(S4[:, u % 3, j, lo:], S4[:, u % 3, j, lo:], ACT.Exp, bias=nm[:, u % 3, j:j + 1],
                                         accum_out=den[:, u % 3, j:j + 1])
                nc.scalar.activation(sk[:, u % 3, :], sk[:, u % 3, :], ACT.Exp).then_inc(s("exped"), 1)

            def move(u):
                i, kv = u // 2, u % 2
                act.wait_ge(s("probs_turns"), u + 1)
                kt = slice(1, 2) if i == 0 else slice(0, 2)
                nc.scalar.activation(PR[:, u % 2, :, kt, :],
                                     ps[:, 4:6, :].rearrange("p b (j k c) -> p (b j) k c", k=2, c=P)[:, :, kt, :],
                                     ACT.Copy).then_inc(s("probs_turned"), 1)
                act.wait_ge(s("valued"), u + 1)
                nc.scalar.activation(PT[HD * kv:HD * kv + HD, 14:18, PO + i * P:PO + (i + 1) * P],
                                     ps[HD * kv:HD * kv + HD, 6, :].rearrange("p (j c) -> p j c", c=P),
                                     ACT.Copy).then_inc(s("mixed"), 1)

            for u in range(2 * NT):
                exps(u)
                if u >= 1:
                    move(u - 1)
                if u >= 2 and u % 2 == 0:
                    ada_out(ADA_A // 4 + u // 2 - 1, 7)
            move(2 * NT - 1)
            ada_out((ADA_A + ADA_B) // 4 - 1, 7)
            act.wait_ge(s("shifted"), RC)
            nc.scalar.activation(PT[0:64, 12, PO:PW], PT[0:64, 12, PO:PW], ACT.Tanh).then_inc(s("tanh_w"), 1)
            nc.scalar.activation(PT[:, 13, PO:PW], PT[:, 13, PO:PW], ACT.Sigmoid).then_inc(s("sig_g"), 1)
            def sample_attention(n):
                if n == 0:
                    act.wait_ge(s("sk_turns"), 1)
                    nc.scalar.activation(KTs[:], ps[:, 0:2, :].rearrange("p b (i c) -> p (b i) c", c=P),
                                         ACT.Copy).then_inc(s("sk_turned"), 1)
                elif n == 1:
                    act.wait_ge(s("s_scored"), 1)
                    nc.scalar.activation(sS[:].rearrange("p (b v g) -> p v b g", v=2, g=4),
                                         ps[:, 2:4, 0:32].rearrange("p v (b g) -> p v b g", g=4), ACT.Copy).then_inc(s("s_copied"), 1)
                elif n == 2:
                    act.wait_ge(s("s_maxed"), 1)
                    nc.scalar.activation(sP[:], sP[:], ACT.Exp, bias=nm[0:64, 0, 0:1], accum_out=den[0:64, 0, 0:1])
                    nc.scalar.activation(sk[0:64, 0, 0:1], sk[0:64, 0, 0:1], ACT.Exp).then_inc(s("s_exped"), 1)
                elif n == 3:
                    act.wait_ge(s("s_turns"), 2)
                    nc.scalar.activation(sPT[:], ps[:, 2, 0:64], ACT.Copy).then_inc(s("s_turned"), 1)
                elif n == 4:
                    act.wait_ge(s("s_valued"), 1)
                    nc.scalar.activation(PT[:, 14:18, PO + T:PW], ps[:, 1, 0:32].rearrange("p (b j) -> p j b", j=4),
                                         ACT.Copy).then_inc(s("s_mixed"), 1)

            def prepare(piece, j):
                if piece == "decay":
                    if j >= 1:
                        act.wait_ge(s("p_bonus"), j)
                    else:
                        act.wait_ge(s("kvp_out"), 16)
                    act.wait_ge(s("p_decay"), j + 1)
                    nc.scalar.activation(slices(F0[:]), ps[:, 4:7, 0:SL], ACT.Sigmoid, bias=param("rwkv_w0", j)
                                         ).then_inc(s("sig_decay"), 1)
                elif piece == "rate":
                    act.wait_ge(s("p_rate"), j + 1)
                    if j >= 1:
                        act.wait_ge(s("beta_bd"), j)
                    nc.scalar.activation(slices(F1[:]), ps[:, 4:7, 0:SL], ACT.Sigmoid, bias=param("rwkv_a0", j)
                                         ).then_inc(s("sig_rate"), 1)
                elif piece == "log":
                    nc.scalar.activation(F3, PT[:, 4 + j, PO:PW], ACT.Square, scale=param("rwkv_k_k", j)
                                         ).then_inc(s("k_square"), 1)
                    act.wait_ge(s("sig_decay"), j + 1)
                    nc.scalar.activation(SMP[:, j, 1, :], F0[:, T:N], ACT.Exp, scale=-KAPPA)
                    act.wait_ge(s("p_sgt"), j + 1)
                    nc.scalar.activation(SGt, ps[:, 4:6, :].rearrange("p b (i c) -> p (b i) c", c=P),
                                         ACT.Copy).then_inc(s("sgt_copied"), 1)
                elif piece == "norm":
                    act.wait_ge(s("k_floor"), j + 1)
                    inverse_root(F3, F3, eps[:, 2:3], 1.0).then_inc(s("k_norm"), 1)
                elif piece == "cum":
                    for m in range(4):
                        act.wait_ge(s("p_cum"), 4 * j + m + 1)
                        cum = ps[:, 4 + m % 3, :].rearrange("p (i x t) -> p i x t", x=2, t=P)
                        q = slice(2 * m * P, (2 * m + 2) * P)
                        for f, x, sign in ((F5, 0, -1), (F6, 0, 1), (Alpha.rearrange("p u c -> p (u c)"), 1, -1)):
                            ins = nc.scalar.activation(f[:, q].rearrange("p (i t) -> p i t", t=P), cum[:, :, x, :],
                                                       ACT.Exp, scale=sign * KAPPA)
                        ins.then_inc(s("decays"), 1)
                elif piece == "ends":
                    act.wait_ge(s("alpha"), j + 1)
                    if j == 0:
                        act.wait_ge(s("bd_zero"), 4)
                    for h in (slice(0, HD), slice(HD, P)):
                        ins = nc.scalar.activation(AB[h, :, h], Alpha[h], ACT.Copy)
                    ins.then_inc(s("alpha_bd"), 1)
                    act.wait_ge(s("p_values"), j + 1)
                    if j >= 1:
                        act.wait_ge(*computed("O", j - 1, 1))
                    nc.scalar.activation(vTm, ps[:, 4:6, :].rearrange("p b (i c) -> p (b i) c", c=C),
                                         ACT.Copy).then_inc(s("v_tokens"), 1)

            def evacuate(name, j, half):
                u = slice(8 * half, 8 * half + 8)
                src = results(name, half)
                act.wait_ge(*computed(name, j, half))
                for other in GROUPS[GROUP_OF[name]]:
                    if other not in ON_ACT:
                        act.wait_ge(*evacuated(other, j, half))
                if name[0] == "Y":
                    nc.scalar.activation(Yc[:, u], src, ACT.Copy).then_inc(s("y_compact"), 1)
                    nc.scalar.activation(AB[0:HD, u, 0:HD], src[0:HD], ACT.Copy).then_inc(s("unit_act"), 1)
                    return
                if name == "aT" and half == 0:
                    act.wait_ge(s("ends_ready"), j + 1)
                if name == "O":
                    dst = PT[:, 8 + j, PO:PO + T].rearrange("p (u c) -> p u c", c=C)
                else:
                    dst = {"aT": aTm, "bT": bTm, "kT": kTm, "W1": W1, "H": hm(j), "E": Ein}[name]
                nc.scalar.activation(dst[:, u], src, ACT.Copy).then_inc(s("unit_act"), 1)

            def first_head(j, level, half):
                u = slice(8 * half, 8 * half + 8)
                act.wait_ge(*evacuated("MT" if level == 0 else f"ZT{level - 1}", j, half))
                nc.scalar.activation(TB[0:HD, u, 0:HD], TT[0:HD, u], ACT.Copy).then_inc(s("t_first"), 1)

            for j in range(NJ + 1):
                for piece, c in overlapped(j >= 1, j < NJ):
                    if piece == "sample":
                        sample_attention(c)
                    elif piece != "chain":
                        prepare(piece, j)
                    elif c % 8 == 7:
                        evacuate("O", j - 1, c // 8)
                if j == NJ - 1:
                    act.wait_ge(s("smp_turns"), 1)
                    act.wait_ge(s("bonus"), NJ)
                    nc.scalar.activation(SM48, ps[0:48, 6, :], ACT.Copy).then_inc(s("sm48_ready"), 1)
                if j < NJ:
                    for name, half in halves:
                        if name == "O":
                            continue
                        if name in ON_ACT:
                            evacuate(name, j, half)
                        elif name == "MT" or name[:2] == "ZT":
                            first_head(j, 0 if name == "MT" else int(name[2:]) + 1, half)
                        if j + 1 < NJ and half == 1:
                            for piece in EARLY.get(name, []):
                                prepare(piece, j + 1)
            act.wait_ge(s("or_turns"), 1)
            nc.scalar.activation(PT[:, 8:12, PO + T:PW], ps[:, 5, 0:4 * NS].rearrange("p (j b) -> p j b", b=NS),
                                 ACT.Copy).then_inc(s("o_sample"), 1)

            def gn_square(j):
                act.wait_ge(s("centred"), j + 1)
                nc.scalar.activation(XG[j], PT[:, j, PO:PW], ACT.Square).then_inc(s("gn_square"), 1)

            def gn_log(j):
                act.wait_ge(s("gn_var"), j + 1)
                nc.scalar.activation(slices(XG[j]), ps[:, 0:3, 0:SL], ACT.Ln, bias=eps[:, 1:2], scale=1.0 / HD
                                     ).then_inc(s("gn_log"), 1)

            def gn_std(j):
                act.wait_ge(s("gn_log"), j + 1)
                nc.scalar.activation(XG[j], XG[j], ACT.Exp, scale=-0.5).then_inc(s("gn_std"), 1)

            def mix_hi(k, row, signal):
                nc.scalar.activation(XS[:, k, 0], PT[:, row, PO:PW], ACT.Copy).then_inc(s(signal), 1)

            def whi_out(n):
                act.wait_ge(raw_in[n % 4], ((ADA_A + ADA_B + PC + n) // 4 + 1) * 16)
                whi(n % 2, n % 4)

            gn_square(0)
            act.wait_ge(s("wkvs_out"), 16)
            gn_square(1)
            gn_log(0)
            act.wait_ge(s("states_out"), 16)
            mix_hi(4, 14, "mix_hi_a")
            gn_square(2)
            gn_log(1)
            gn_std(0)
            gn_std(1)
            gn_square(3)
            mix_hi(5, 15, "mix_hi_a")
            gn_log(2)
            mix_hi(6, 16, "mix_hi_a")
            gn_log(3)
            gn_std(2)
            gn_std(3)
            mix_hi(7, 17, "mix_hi_a")
            whi_out(0)
            for j in range(NJ):
                act.wait_ge(s("gated"), j + 1)
                mix_hi(j, j, "mix_hi_r")
            whi_out(1)

            for n in range(KD):
                act.wait_ge(s("out_ready"), n + 1)
                if n + 2 < KD:
                    whi_out(n + 2)
                if n >= 2:
                    act.wait_ge(s("sq_added"), n - 1)
                nc.scalar.activation(slices(sq2[:, n % 2]), three(n % 2), ACT.Square).then_inc(s("sq_c"), 1)
                nc.scalar.activation(slices(MO[:, n]), three(n % 2), ACT.Copy).then_inc(s("out_out"), 1)
            act.wait_ge(s("sq_total"), 1)
            inverse_root(slices(rsC[:]), three(0), eps[:, 0:1], 1.0 / D).then_inc(s("std2"), 1)
            for k in range(KD):
                act.wait_ge(s("x1_ready"), k + 1)
                if k >= 2:
                    act.wait_ge(s("sq_summed"), k - 1)
                nc.scalar.activation(sq2[:, k % 2], X2[:, k], ACT.Square).then_inc(s("sq_c"), 1)
            def w3(m_slot, in_count, used):
                act.wait_ge(s(f"raw3_in{m_slot}"), in_count * 16)
                if used is not None:
                    act.wait_ge(s("ffn_mm"), used)
                nc.scalar.activation(spl3[:, m_slot, 0], raw3[:, m_slot], ACT.Copy).then_inc(s("w3_hi"), 1)

            for m in range(3):
                w3(m, 1, None)
            act.wait_ge(s("sq_summed"), KD)
            inverse_root(slices(rsC[:]), three(1), eps[:, 0:1], 1.0 / D).then_inc(s("std2"), 1)

            for k in range(KD):
                act.wait_ge(s("h2_ready"), k + 1)
                nc.scalar.activation(XS[:, k, 0], MO[:, k], ACT.Copy).then_inc(s("h2_hi"), 1)

            def evac_up(c, chunk, job, bank_set, before):
                act.wait_ge(s("ffn_mm"), job)
                act.wait_ge(s("g_done"), before)
                nc.scalar.activation(slices(U[:, c]), three(bank_set), ACT.Copy)
                a = PARAM_AT["ffn_conv_w"][0] + 2 * 2 * FC
                b = PARAM_AT["ffn_conv_b"][0]
                nc.scalar.activation(slices(Z[:, c]), three(bank_set), ACT.Identity, bias=col(b, chunk),
                                     scale=col(a, chunk)).then_inc(s("up_out"), 1)

            def gate_up(pair, slot):
                act.wait_ge(s("conv_done"), pair * 2 + 1)
                nc.scalar.activation(Z[:, 0], Z[:, 0], ACT.Silu).then_inc(s("silu_done"), 1)
                act.wait_ge(s("g_done"), pair + 2)
                nc.scalar.activation(act2[:, slot, 0], G[:], ACT.Copy).then_inc(s("g_hi"), 1)

            act.wait_ge(s("ffn_mm"), 1)
            w3(0, 2, 1)
            evac_up(0, 0, 1, 0, 1)
            evac_up(1, FC, 2, 1, 1)
            gate_up(0, 0)
            w3(1, 2, 2)
            evac_up(0, 1, 3, 0, 2)
            w3(2, 2, 3)
            w3(0, 3, 4)
            evac_up(1, FC + 1, 4, 1, 2)
            gate_up(1, 1)

            def act_body(i, last):
                evac_up(0, i * 2, i * 12 - 7, 0, i * 2 + 1)
                w3(1, i * 2 + 1, i * 12 - 7)
                w3(2, i * 2 + 1, i * 12 + 1)
                w3(0, i * 2 + 2, i * 12 + 1)
                evac_up(1, i * 2 + FC, i * 12 + 2, 1, i * 2 + 1)
                gate_up(i * 2, 0)
                w3(1, i * 2 + 2, i * 12 + 2)
                evac_up(0, i * 2 + 1, i * 12 + 3, 0, i * 2 + 2)
                w3(2, i * 2 + 2, i * 12 + 3)
                if not last:
                    w3(0, i * 2 + 3, i * 12 + 4)
                evac_up(1, i * 2 + (FC + 1), i * 12 + 4, 1, i * 2 + 2)
                gate_up(i * 2 + 1, 1)

            with act.Fori(1, FC // 2 - 1) as i:
                act_body(i, False)
            act_body(FC // 2 - 1, True)
            for k in range(KD):
                act.wait_ge(s("down_out"), KD * (FC // 2 - 1) + k + 1)
                if k >= 2:
                    act.wait_ge(s("sq_added"), KD - 1 + k - 1)
                nc.scalar.activation(Z[:, k % 2], acc[:, k], ACT.Square).then_inc(s("sq_c"), 1)
            act.wait_ge(s("sq_total"), 2)
            inverse_root(slices(G[:]), three(0), eps[:, 0:1], 1.0 / D).then_inc(s("std2"), 1)

        @block.gpsimd
        def _(pool):
            pool.wait_ge(consts_in, 16 * 6)
            pool.wait_ge(mod_ready, 1)
            pool.wait_ge(proj_ready, PC)
            nc.gpsimd.memset(Kz[0:HD, 1], 0.0).then_inc(s("k_zeros"), 1)
            pool.wait_ge(s("k_zeros"), 1)
            nc.gpsimd.memset(Kz[HD:P, 0], 0.0).then_inc(s("k_zeros"), 1)
            pool.wait_ge(s("k_zeros"), 2)
            pool.wait_ge(s("shift_saved"), 1)
            pool.wait_ge(s("rotated"), 5)
            for n, c in enumerate((12, 13, 0, 4, 8, 1, 5, 9, 2, 6, 10, 3, 7, 11)):
                d = difP[:]
                if n >= 1:
                    pool.wait_ge(s("shifted"), n)
                x = PT[:, c, PO:PW]
                nc.gpsimd.tensor_tensor(d[:, 0:T], PT[:, c, PO - 1:PO - 1 + T], PT[:, c, PO:PO + T], ALU.subtract)
                nc.gpsimd.tensor_tensor(d[:, T:N], shift_st[:, c], PT[:, c, PO + T:PW], ALU.subtract
                                        ).then_inc(s("shift_step"), 1)
                pool.wait_ge(s("shift_step"), 2 * n + 1)
                nc.gpsimd.tensor_tensor(d, d, param("rwkv_mu", c).broadcast_to([P, N]), ALU.mult
                                        ).then_inc(s("shift_step"), 1)
                pool.wait_ge(s("shift_step"), 2 * n + 2)
                nc.gpsimd.tensor_tensor(x, x, d, ALU.add).then_inc(s("shifted"), 1)
            pool.wait_ge(s("s_mixed"), 1)
            for b in (AB[:], BB[:], KB[:], TB):
                nc.gpsimd.memset(b, 0.0).then_inc(s("bd_zero"), 1)
            eye = const("eye").unsqueeze(1).broadcast_to([P, NCH, C])
            for j in range(NJ):
                if j >= 1:
                    pool.wait_ge(*computed("G", j - 1, 1))
                    pool.wait_ge(s("t_first"), t_copies(j - 1, LAST_LEVEL + 1, 1))
                nc.gpsimd.tensor_copy(Tm, eye)
                nc.gpsimd.tensor_copy(TT, eye).then_inc(s("eyes"), 1)

            for j in range(NJ):
                pool.wait_ge(s("mix_hi_a"), j + 1)
                nc.gpsimd.tensor_tensor(XS[:, 4 + j, 1], PT[:, 14 + j, PO:PW], XS[:, 4 + j, 0].bitcast(F32), ALU.subtract
                                        ).then_inc(s("mix_lo_a"), 1)

            def add_squares(src, total, count, added):
                for k in range(KD - 1):
                    pool.wait_ge(s("sq_c"), count + k + 1)
                    if k == 0:
                        nc.gpsimd.tensor_copy(total, src(k)).then_inc(s("sq_added"), 1)
                    else:
                        pool.wait_ge(s("sq_added"), added + k)
                        nc.gpsimd.tensor_tensor(total, total, src(k), ALU.add).then_inc(s("sq_added"), 1)

            def scale(dst, src, by):
                for k in range(POOL_FROM, KD):
                    nc.gpsimd.tensor_tensor(dst[:, k, 0:T], src[:, k, 0:T], by[:, 0:T], ALU.mult).then_inc(s("scaled"), 1)

            add_squares(lambda k: sq2[:, k % 2], sqs[:], 0, 0)
            pool.wait_ge(s("std2"), 1)
            pool.wait_ge(s("out_out"), KD)
            scale(MO, MO, rsC)
            pool.wait_ge(s("std2"), 2)
            pool.wait_ge(s("x1_ready"), KD)
            scale(MO, X2, rsC)
            pool.wait_ge(s("h2_lo"), KD)
            nc.gpsimd.memset(acc[:], 0.0).then_inc(s("acc_zero"), 1)
            add_squares(lambda k: Z[:, k % 2], sqF[:], 2 * KD, KD - 1)
            pool.wait_ge(s("std2"), 3)
            pool.wait_ge(s("down_out"), KD * (FC // 2))
            scale(acc, acc, G)

        @block.vector
        def _(dve):
            mark, past = [0], [0]

            def link(ins):
                mark[0] += 1
                ins.then_inc(dve_step, 1)
                dve.wait_ge(dve_step, mark[0] + past[0])

            link(nc.vector.memset(eps[:, 0:1], NORM_EPS))
            link(nc.vector.memset(eps[:, 2:3], 0.0))
            nc.vector.memset(eps[:, 1:2], GN_EPS).then_inc(zeros_set, 1)
            dve.wait_ge(consts_in, 16 * 6)
            for k in range(KD):
                dve.wait_ge(sq_ready, k + 1)
                if k == 0:
                    nc.vector.tensor_copy(sqA_sum, sqA[0]).then_inc(sq_used, 1)
                else:
                    dve.wait_ge(sq_used, k)
                    nc.vector.tensor_tensor(sqA_sum, sqA_sum, sqA[k % 2], ALU.add).then_inc(sq_used, 1)
            dve.wait_ge(std_ready, 1)

            def modulation(first, count, bank):
                dve.wait_ge(s("ada_turned"), (first + count) // 4)
                a = PARAM_AT["b_ada"][0] + first
                return nc.vector.tensor_tensor(mod[:, first:first + count, :],
                                               ps[:, bank, 0:count * 9].rearrange("p (n c) -> p n c", c=9),
                                               par[:, a:a + count].unsqueeze(2).broadcast_to([P, count, 9]), ALU.add)

            def norm_scale(out, name, chunk):
                link(nc.vector.tensor_scalar(out[:], mod[:, chunk:chunk + KD, :], 1.0, None, ALU.add))
                link(nc.vector.tensor_tensor(out[:], out[:], params(name).unsqueeze(2).broadcast_to([P, KD, 9]),
                                             ALU.mult))

            for k in range(KD):
                ins = nc.vector.tensor_tensor(xT[:, k], xT[:, k], rs[:], ALU.mult)
            link(ins)
            link(modulation(0, ADA_A, 0))
            norm_scale(gs1, "norm_pre_mix", 8)
            def w_low(slot2, slot4):
                return nc.vector.tensor_tensor(spl[:, slot2, 1], raw[:, slot4], spl[:, slot2, 0].bitcast(F32),
                                               ALU.subtract)
            for n in range(2):
                dve.wait_ge(w_hi, n + 1)
                w_low(n, n).then_inc(w_lo, 1)
            def low(k):
                dve.wait_ge(h_hi, k + 1)
                nc.vector.tensor_tensor(XS[:, k, 1], xT[:, k], XS[:, k, 0].bitcast(F32),
                                        ALU.subtract).then_inc(h_lo, 1)
            xs = xT[:, :, T:N]
            link(nc.vector.tensor_tensor(xs, xs, gs1[:, :, 1:9], ALU.mult))
            link(nc.vector.tensor_tensor(xs, xs, mod[:, 0:KD, 1:9], ALU.add))
            for k in range(KD):
                nc.vector.tensor_scalar(xT[:, k, 0:T], xT[:, k, 0:T], gs1[:, k, 0:1], mod[:, k, 0:1],
                                        ALU.mult, ALU.add).then_inc(h_ready, 1)
                if k >= 1:
                    low(k - 1)
            low(KD - 1)
            for n in range(2):
                dve.wait_ge(w_hi, n + 3)
                w_low(n, n + 2).then_inc(w_lo, 1)
            with dve.Fori(0, (PC - 4) // 4) as i:
                for j in range(4):
                    dve.wait_ge(w_hi, i * 4 + (5 + j))
                    w_low(j % 2, j).then_inc(w_lo, 1)
            nc.vector.memset(PT[:, :, 0:PO], 0.0).then_inc(mod_ready, 1)
            dve.wait_ge(proj_out, PC)
            dve.wait_ge(mod_ready, 1)
            nc.vector.tensor_copy(tail_shift[:], PT[:, 0:RC, PW - NS - 1:PW]).then_inc(s("shift_saved"), 1)
            dve.wait_ge(s("rope_in"), 16)
            for n, c in enumerate((18, 14, 15, 16, 17)):
                if n >= 1:
                    dve.wait_ge(s("rotated"), n)
                link(nc.vector.tensor_tensor(dif[:, 0], PT[:, c, PO:PW], rope[:, 0], ALU.mult))
                dve.wait_ge(s("swapped"), n + 1)
                link(nc.vector.tensor_tensor(slices(dif[:, 1]), three(n % 2), slices(rope[:, 1]), ALU.mult))
                ins = nc.vector.tensor_tensor(PT[:, c, PO:PW], dif[:, 0], dif[:, 1], ALU.add)
                ins.then_inc(s("rotated"), 1)
            dve.wait_ge(s("rotated"), 5)

            def mask_max(u):
                i, kv, v, b = u // 2, u % 2, u % 3, u % 2
                lo = P if i == 0 else 0
                dve.wait_ge(s("scored"), u + 1)
                if u >= 3:
                    dve.wait_ge(s("probs_turns"), u - 2)
                win = const("window")[:, lo:].unsqueeze(1).broadcast_to([P, 4, 2 * P - lo])
                sc = ps[:, 2 * b:2 * b + 2, :].rearrange("p b (j k) -> p (b j) k", j=2)[:, :, lo:]
                nc.vector.scalar_tensor_tensor(S4[:, v, :, lo:], sc, SCALE, win, ALU.mult, ALU.add).then_inc(s("masked"), 1)
                dve.wait_ge(s("masked"), u + 1)
                link(nc.vector.tensor_reduce(mx[:, v], S4[:, v, :, lo:], AX.X, ALU.max))
                a = PARAM_AT["sinks"][0] + 4 * kv
                link(nc.vector.tensor_tensor(mx[:, v], mx[:, v], par[:, a:a + 4], ALU.max))
                link(nc.vector.tensor_tensor(sk[:, v], par[:, a:a + 4], mx[:, v], ALU.subtract))
                nc.vector.tensor_scalar(nm[:, v], mx[:, v], -1.0, None, ALU.mult).then_inc(s("maxed"), 1)

            def normalise(u):
                i, v = u // 2, u % 3
                lo = P if i == 0 else 0
                dve.wait_ge(s("exped"), u + 1)
                link(nc.vector.tensor_tensor(den[:, v], den[:, v], sk[:, v], ALU.add))
                link(nc.vector.reciprocal(rd[:, v], den[:, v]))
                nc.vector.tensor_tensor(S4[:, v, :, lo:], S4[:, v, :, lo:],
                                        rd[:, v].unsqueeze(2).broadcast_to([P, 4, 2 * P - lo]),
                                        ALU.mult).then_inc(s("probs"), 1)

            mask_max(0)
            mask_max(1)
            for u in range(2 * NT):
                normalise(u)
                if u + 2 < 2 * NT:
                    mask_max(u + 2)
                if u >= 2 and u % 2 == 0:
                    modulation(ADA_A + 2 * u - 4, 4, 7).then_inc(s("mod_added"), 1)
            modulation(ADA_A + ADA_B - 4, 4, 7).then_inc(s("mod_added"), 1)
            dve.wait_ge(s("mod_added"), ADA_B // 4)
            link(nc.vector.tensor_scalar(sc_mod[:], params("rwkv_k_a"), -1.0, 1.0, ALU.mult, ALU.add))

            def sample_attention(n):
                if n == 2:
                    dve.wait_ge(s("s_turns"), 1)
                    link(nc.vector.tensor_scalar(sP[:], ps[0:64, 0, 0:P], SCALE, None, ALU.mult))
                    link(nc.vector.tensor_reduce(mx[0:64, 0, 0:1], sP[:], AX.X, ALU.max))
                    srow = par[0:64, PARAM_AT["sink_rows"][0]:PARAM_AT["sink_rows"][1]]
                    link(nc.vector.tensor_tensor(mx[0:64, 0, 0:1], mx[0:64, 0, 0:1], srow, ALU.max))
                    link(nc.vector.tensor_tensor(sk[0:64, 0, 0:1], srow, mx[0:64, 0, 0:1], ALU.subtract))
                    nc.vector.tensor_scalar(nm[0:64, 0, 0:1], mx[0:64, 0, 0:1], -1.0, None, ALU.mult).then_inc(s("s_maxed"), 1)
                    dve.wait_ge(s("s_exped"), 1)
                    link(nc.vector.tensor_tensor(den[0:64, 0, 0:1], den[0:64, 0, 0:1], sk[0:64, 0, 0:1], ALU.add))
                    link(nc.vector.reciprocal(rd[0:64, 0, 0:1], den[0:64, 0, 0:1]))
                    nc.vector.tensor_scalar(sP[:], sP[:], rd[0:64, 0, 0:1], None, ALU.mult).then_inc(s("s_probs"), 1)
                elif n == 4:
                    dve.wait_ge(s("s_mixed"), 1)

            def prepare(piece, j):
                r, k, v = (PT[:, c + j, PO:PW] for c in (0, 4, 8))
                q = slice(0, T)
                if piece == "rate":
                    dve.wait_ge(s("sig_rate"), j + 1)
                    link(nc.vector.tensor_scalar(F4, F1[:], param("rwkv_k_a", j), sc_mod[:, j:j + 1], ALU.mult, ALU.add))
                elif piece == "log":
                    link(nc.vector.tensor_tensor(F4, F4, k, ALU.mult))
                elif piece == "norm":
                    dve.wait_ge(s("p_norm"), j + 1)
                    nc.vector.tensor_scalar(slices(F3), ps[:, 4:7, 0:SL], NORM_FLOOR, None, ALU.max
                                            ).then_inc(s("k_floor"), 1)
                elif piece == "kk":
                    dve.wait_ge(s("k_norm"), j + 1)
                    dve.wait_ge(s("sgt_copied"), j + 1)
                    nc.vector.scalar_tensor_tensor(F0[:], r, param("rwkv_r_k", j), F4, ALU.mult, ALU.mult
                                                   ).then_inc(s("rkk"), 1)
                    link(nc.vector.scalar_tensor_tensor(F3, k, param("rwkv_k_k", j), F3, ALU.mult, ALU.mult))
                    link(nc.vector.tensor_tensor(F1[:], F1[:], F3, ALU.mult))
                elif piece == "bonus":
                    dve.wait_ge(s("p_bonus"), j + 1)
                    nc.vector.tensor_tensor(slices(k), ps[:, 4:7, 0:SL], slices(v), ALU.mult).then_inc(s("bonus"), 1)
                elif piece == "alpha":
                    dve.wait_ge(s("decays"), 4 * (j + 1))
                    for n, src in ((0, F3[:, T:N]), (2, F4[:, T:N]), (3, F1[:, T:N]), (4, r[:, T:N]), (5, v[:, T:N])):
                        ins = nc.vector.tensor_copy(SMP[:, j, n, :], src)
                    ins.then_inc(s("smp_ready"), 1)
                    nc.vector.scalar_tensor_tensor(Alpha, unit(F3), -1.0, Alpha, ALU.mult, ALU.mult
                                                   ).then_inc(s("alpha"), 1)
                elif piece == "beta":
                    if j == 0:
                        dve.wait_ge(s("bd_zero"), 4)
                    link(nc.vector.tensor_tensor(Beta, unit(F1), unit(F6), ALU.mult))
                    for h in (slice(0, HD), slice(HD, P)):
                        ins = nc.vector.tensor_copy(BB[h, :, h], Beta[h])
                    ins.then_inc(s("beta_bd"), 1)
                elif piece == "kappa":
                    for h in (slice(0, HD), slice(HD, P)):
                        ins = nc.vector.tensor_tensor(KB[h, :, h], unit(F4)[h], unit(F6)[h], ALU.mult)
                elif piece == "ends":
                    dve.wait_ge(s("rkk"), j + 1)
                    if j >= 1:
                        dve.wait_ge(*computed("O", j - 1, 1))
                    nc.vector.tensor_tensor(R, unit(r), unit(F5), ALU.mult)
                    nc.vector.tensor_tensor(Aff, const("eye").unsqueeze(1).broadcast_to([P, NCH, C]),
                                            F5[:, C - 1:T:C].unsqueeze(2).broadcast_to([P, NCH, C]), ALU.mult
                                            ).then_inc(s("ends_ready"), 1)

            def all8(m):
                return m.unsqueeze(1).broadcast_to([P, 8, C])

            def below(dst, u, out):
                for h in (slice(0, HD), slice(HD, P)):
                    ins = nc.vector.tensor_tensor(dst[h, u, h], out[h],
                                                  const("after")[h].unsqueeze(1).broadcast_to([HD, 8, C]), ALU.mult)
                return ins

            def evacuate(name, j, half):
                u = slice(8 * half, 8 * half + 8)
                out = results(name, half)
                dve.wait_ge(*computed(name, j, half))
                if name == "MT":
                    below(BB, u, out)
                    link(nc.vector.copy_predicated(TT[:, u], all8(lvl[:, 1]), out))
                    ins = nc.vector.tensor_copy(TB[HD:P, u, HD:P], TT[HD:P, u])
                elif name == "M":
                    if half == 0:
                        dve.wait_ge(s("eyes"), j + 1)
                    ins = nc.vector.copy_predicated(Tm[:, u], all8(lvl[:, 0]), out)
                elif name == "MkT":
                    ins = below(KB, u, out)
                elif name in ("NbT", "NkT"):
                    ins = nc.vector.tensor_tensor((NbT if name == "NbT" else NkT)[:, u], out, all8(const("upto")), ALU.mult)
                elif name[0:2] == "ZT":
                    n = int(name[2:]) + 1
                    ins = nc.vector.copy_predicated(TT[:, u], all8(lvl[:, 2 * n + 1]), out)
                    link(ins)
                    ins = nc.vector.tensor_copy(TB[HD:P, u, HD:P], TT[HD:P, u])
                elif name[0] == "Z":
                    n = int(name[1:]) + 1
                    ins = nc.vector.copy_predicated(Tm[:, u], all8(lvl[:, 2 * n]), out)
                elif name == "G":
                    for h in (slice(0, HD), slice(HD, P)):
                        ins = nc.vector.tensor_copy(BB[h, u, h], out[h])
                else:
                    dst = (Aff if name == "A" else R)[:, u]
                    ins = nc.vector.tensor_tensor(dst, dst, out, ALU.add)
                ins.then_inc(s("unit_dve"), 1)

            def chain(j, c):
                if c == 0:
                    dve.wait_ge(*evacuated("E", j, 1))
                    nc.vector.tensor_copy(St[:, 1], Ein[:, 0]).then_inc(s("state_ready"), 1)
                    return
                dve.wait_ge(s("state_mm"), j * (NCH - 1) + c)
                dst = St[:, c + 1] if c + 1 < NCH else WO[:, j]
                nc.vector.tensor_tensor(dst, ps[:, 7, 0:C], Ein[:, c], ALU.add).then_inc(s("state_ready"), 1)

            def over_v(i):
                return V6[:, i, :].unsqueeze(1).broadcast_to([P, 32, HD])

            def over_k(x):
                return x[:].unsqueeze(2).broadcast_to([P, 32, HD])

            def sample(n):
                if n == 0:
                    dve.wait_ge(s("wkv_in"), 16 * 5)
                    link(nc.vector.tensor_tensor(sTmp, sWKV, over_v(0), ALU.mult))
                elif n == 1:
                    link(nc.vector.tensor_reduce(sa[:], sTmp, AX.X, ALU.add))
                elif n == 2:
                    link(nc.vector.tensor_tensor(sWKV, sWKV, over_v(1), ALU.mult))
                elif n == 3:
                    link(nc.vector.tensor_tensor(sTmp, over_k(sa), over_v(3), ALU.mult))
                elif n == 4:
                    link(nc.vector.tensor_tensor(sWKV, sWKV, sTmp, ALU.subtract))
                elif n == 5:
                    link(nc.vector.tensor_tensor(sTmp, over_k(V32), over_v(2), ALU.mult))
                elif n == 6:
                    link(nc.vector.tensor_tensor(sWKV, sWKV, sTmp, ALU.add))
                elif n == 7:
                    link(nc.vector.tensor_tensor(sTmp, sWKV, over_v(4), ALU.mult))
                elif n == 8:
                    nc.vector.tensor_reduce(Osm[:], sTmp, AX.X, ALU.add).then_inc(s("sample_o"), 1)

            SAMPLE_AT = ["Y1", "Z1", "Y2", "Z2", "Y3", "Z3", "Y4", "W1"]
            for j in range(NJ + 1):
                for piece, c in overlapped(j >= 1, j < NJ):
                    if piece == "sample":
                        sample_attention(c)
                    elif piece != "chain":
                        prepare(piece, j)
                    else:
                        chain(j - 1, c)
                        if j == NJ and c == 0:
                            sample(8)
                if j < NJ:
                    for name, half in halves:
                        if name[0] == "Y":
                            u = slice(8 * half, 8 * half + 8)
                            dve.wait_ge(s("y_compact"), y_copies(j, int(name[1:]), half))
                            nc.vector.tensor_copy(AB[HD:P, u, HD:P], Yc[HD:P, u]).then_inc(s("y_second"), 1)
                        elif name not in ON_ACT:
                            evacuate(name, j, half)
                        if half == 0:
                            continue
                        if j + 1 < NJ:
                            for piece in EARLY.get(name, []):
                                prepare(piece, j + 1)
                        elif name in SAMPLE_AT:
                            sample(SAMPLE_AT.index(name))

            def centre(j):
                dve.wait_ge(s("gn_mean"), j + 1)
                nc.vector.scalar_tensor_tensor(slices(PT[:, j, PO:PW]), three(min(j, 1)), -1.0 / HD,
                                               slices(PT[:, 8 + j, PO:PW]), ALU.mult, ALU.add).then_inc(s("centred"), 1)

            def normalised(j):
                Y = PT[:, j, PO:PW]
                dve.wait_ge(s("gn_std"), j + 1)
                link(nc.vector.tensor_tensor(Y, Y, XG[j], ALU.mult))
                link(nc.vector.tensor_scalar(Y, Y, param("rwkv_ln_w", j), param("rwkv_ln_b", j), ALU.mult, ALU.add))
                link(nc.vector.tensor_tensor(Y, Y, PT[:, 4 + j, PO:PW], ALU.add))

            def gated(j, bank_set):
                Y = PT[:, j, PO:PW]
                dve.wait_ge(s("gn_gate"), j + 1)
                nc.vector.tensor_tensor(slices(Y), three(bank_set), slices(Y), ALU.mult).then_inc(s("gated"), 1)

            def mix_low(j):
                dve.wait_ge(s("mix_hi_r"), j + 1)
                nc.vector.tensor_tensor(XS[:, j, 1], PT[:, j, PO:PW], XS[:, j, 0].bitcast(F32), ALU.subtract
                                        ).then_inc(s("mix_lo_r"), 1)

            def low_out(n):
                dve.wait_ge(w_hi, PC + n + 1)
                w_low(n % 2, n % 4).then_inc(w_lo, 1)

            centre(0)
            centre(1)
            centre(2)
            normalised(0)
            centre(3)
            gated(0, 1)
            normalised(1)
            gated(1, 1)
            normalised(2)
            gated(2, 0)
            mix_low(0)
            normalised(3)
            low_out(0)
            gated(3, 1)
            for j in range(1, NJ):
                mix_low(j)
            low_out(1)
            link(nc.vector.tensor_tensor(gate[:, 0], mod[:, 16:24], params("norm_post_mix").unsqueeze(2).broadcast_to([P, KD, 9]), ALU.mult))
            link(nc.vector.tensor_tensor(gate[:, 1], mod[:, 40:48], params("norm_post_ffn").unsqueeze(2).broadcast_to([P, KD, 9]), ALU.mult))
            norm_scale(gs2, "norm_pre_ffn", 32)

            for n in range(2, KD):
                low_out(n)

            def over_rows(x):
                return x[:, T:N].unsqueeze(1).broadcast_to([P, KD, NS])

            dve.wait_ge(s("std2"), 1)
            dve.wait_ge(s("x2_in"), 16)
            dve.wait_ge(s("out_out"), KD)
            mo, x2 = MO[:, :, T:N], X2[:, :, T:N]
            link(nc.vector.tensor_tensor(mo, mo, over_rows(rsC), ALU.mult))
            link(nc.vector.tensor_tensor(mo, mo, gate[:, 0, :, 1:9], ALU.mult))
            link(nc.vector.tensor_tensor(x2, x2, mo, ALU.add))
            for k in range(KD):
                if k < POOL_FROM:
                    link(nc.vector.tensor_tensor(MO[:, k, 0:T], MO[:, k, 0:T], rsC[:, 0:T], ALU.mult))
                else:
                    dve.wait_ge(s("scaled"), k - POOL_FROM + 1)
                nc.vector.scalar_tensor_tensor(X2[:, k, 0:T], MO[:, k, 0:T], gate[:, 0, k, 0:1], X2[:, k, 0:T], ALU.mult,
                                               ALU.add).then_inc(s("x1_ready"), 1)
            def low3(slot, count):
                dve.wait_ge(s("w3_hi"), count)
                nc.vector.tensor_tensor(spl3[:, slot, 1], raw3[:, slot], spl3[:, slot, 0].bitcast(F32),
                                        ALU.subtract).then_inc(s("w3_lo"), 1)

            for m in range(3):
                low3(m, m + 1)
            dve.wait_ge(s("std2"), 2)
            dve.wait_ge(s("x1_ready"), KD)

            def low_h(k):
                dve.wait_ge(s("h2_hi"), k + 1)
                nc.vector.tensor_tensor(XS[:, k, 1], MO[:, k], XS[:, k, 0].bitcast(F32), ALU.subtract).then_inc(s("h2_lo"), 1)

            link(nc.vector.tensor_tensor(mo, x2, over_rows(rsC), ALU.mult))
            link(nc.vector.tensor_tensor(mo, mo, gs2[:, :, 1:9], ALU.mult))
            link(nc.vector.tensor_tensor(mo, mo, mod[:, 24:32, 1:9], ALU.add))
            for k in range(KD):
                if k < POOL_FROM:
                    link(nc.vector.tensor_tensor(MO[:, k, 0:T], X2[:, k, 0:T], rsC[:, 0:T], ALU.mult))
                else:
                    dve.wait_ge(s("scaled"), (KD - POOL_FROM) + k - POOL_FROM + 1)
                nc.vector.tensor_scalar(MO[:, k, 0:T], MO[:, k, 0:T], gs2[:, k, 0:1], mod[:, 24 + k, 0:1], ALU.mult,
                                        ALU.add).then_inc(s("h2_ready"), 1)
                if k >= 1:
                    low_h(k - 1)
            low_h(KD - 1)
            dve.wait_ge(s("x1_out"), 16 * KD)
            dve.wait_ge(s("h2_lo"), KD)
            dve.wait_ge(s("conv_in"), 16)

            def taps(n):
                a = PARAM_AT["ffn_conv_w"][0] + n * 2 * FC
                return par[:, a:a + 2 * FC].unsqueeze(2).broadcast_to([P, 2 * FC, NS])

            cu = ftail[:, :, 0:NS]
            link(nc.vector.tensor_tensor(conv_add[:], conv_st[:, 0], taps(0), ALU.mult))
            link(nc.vector.tensor_tensor(cu, conv_st[:, 1], taps(1), ALU.mult))
            nc.vector.tensor_tensor(conv_add[:], conv_add[:], cu, ALU.add).then_inc(s("g_done"), 1)
            dve.wait_ge(s("g_done"), 1)

            def conv(c, chunk, count):
                dve.wait_ge(s("up_out"), count)
                z, u = Z[:, c], U[:, c]
                for n in (1, 0):
                    d = CW - 1 - n
                    a = PARAM_AT["ffn_conv_w"][0] + n * 2 * FC
                    link(nc.vector.scalar_tensor_tensor(z[:, d:T], u[:, 0:T - d], col(a, chunk), z[:, d:T],
                                                        ALU.mult, ALU.add))
                link(nc.vector.tensor_copy(at_chunk(ftail, chunk), u[:, T - 2:N]))
                nc.vector.tensor_tensor(z[:, T:N], z[:, T:N], at_chunk(conv_add, chunk), ALU.add
                                        ).then_inc(s("conv_done"), 1)

            def form(pair, slot):
                dve.wait_ge(s("silu_done"), pair + 1)
                dve.wait_ge(s("conv_done"), pair * 2 + 2)
                nc.vector.tensor_tensor(G[:], Z[:, 0], Z[:, 1], ALU.mult).then_inc(s("g_done"), 1)
                dve.wait_ge(s("g_hi"), pair + 1)
                nc.vector.tensor_tensor(act2[:, slot, 1], G[:], act2[:, slot, 0].bitcast(F32), ALU.subtract
                                        ).then_inc(s("g_lo"), 1)
                dve.wait_ge(s("g_lo"), pair + 1)

            low3(0, 4)
            conv(0, 0, 1)
            conv(1, FC, 2)
            form(0, 0)
            low3(1, 5)
            conv(0, 1, 3)
            low3(2, 6)
            low3(0, 7)
            conv(1, FC + 1, 4)
            form(1, 1)

            dve.wait_ge(s("acc_zero"), 1)

            def add_down(i, last, first=0, end=KD):
                for k in range(first, end):
                    y = k + 1
                    dve.wait_ge(s("ffn_mm"), i * 12 - (8 if last else 7) + y)
                    bs = (y - 1) % 2 if last else y % 2
                    nc.vector.tensor_tensor(slices(acc[:, k]), slices(acc[:, k]), three(bs), ALU.add
                                            ).then_inc(s("down_out"), 1)

            def dve_body(i, last):
                add_down(i, False, 0, 1)
                low3(1, i * 6 + 2)
                add_down(i, False, 1, 3)
                conv(0, i * 2, i * 4 + 1)
                add_down(i, False, 3)
                low3(2, i * 6 + 3)
                low3(0, i * 6 + 4)
                conv(1, i * 2 + FC, i * 4 + 2)
                form(i * 2, 0)
                low3(1, i * 6 + 5)
                conv(0, i * 2 + 1, i * 4 + 3)
                low3(2, i * 6 + 6)
                if not last:
                    low3(0, i * 6 + 7)
                conv(1, i * 2 + (FC + 1), i * 4 + 4)
                form(i * 2 + 1, 1)

            rounds, links = FC // 2 - 2, 12
            with dve.Fori(1, 1 + rounds) as i:
                past[0] = i * links - links
                before = mark[0]
                dve_body(i, False)
                assert mark[0] - before == links
            mark[0] += (rounds - 1) * links
            past[0] = 0
            dve_body(FC // 2 - 1, True)
            add_down(FC // 2, True)
            dve.wait_ge(s("std2"), 3)
            dve.wait_ge(s("x1_in"), 16)
            dve.wait_ge(s("down_out"), KD * (FC // 2))
            out, x1 = acc[:, :, T:N], X1[:, :, T:N]
            link(nc.vector.tensor_tensor(out, out, over_rows(G), ALU.mult))
            link(nc.vector.tensor_tensor(out, out, gate[:, 1, :, 1:9], ALU.mult))
            link(nc.vector.tensor_tensor(out, out, x1, ALU.add))
            for k in range(KD):
                if k < POOL_FROM:
                    link(nc.vector.tensor_tensor(acc[:, k, 0:T], acc[:, k, 0:T], G[:, 0:T], ALU.mult))
                else:
                    dve.wait_ge(s("scaled"), 2 * (KD - POOL_FROM) + k - POOL_FROM + 1)
                nc.vector.scalar_tensor_tensor(acc[:, k, 0:T], acc[:, k, 0:T], gate[:, 1, k, 0:1], X1[:, k, 0:T], ALU.mult,
                                               ALU.add).then_inc(s("y_ready"), 1)


def _consts():
    i = np.arange(P)
    c = {}
    c["ident"] = np.eye(P)
    c["swap"] = (i[:, None] == (i[None, :] ^ 32))
    c["headsum"] = (i[:, None] // HD == i[None, :] // HD)
    c["ones"] = np.ones((P, P))
    same = i[:, None] // C == i[None, :] // C
    c["cumsum"] = np.concatenate([same & (i[:, None] <= i[None, :]), same & (i[:, None] < i[None, :])], 1)
    t = np.arange(C)
    c["after"] = (i % C)[:, None] < t[None, :]
    c["upto"] = (i % C)[:, None] <= t[None, :]
    c["eye"] = (i % C)[:, None] == t[None, :]
    k = np.arange(2 * P)[None, :]
    c["window"] = np.where((k <= i[:, None] + P) & (k > i[:, None]), 0.0, MASKED)
    out = np.concatenate([np.asarray(c[n], np.float32).reshape(P, w) for n, w in CONSTS], 1)
    lv = []
    for b in (1,) + LEVELS:
        r, q = (i % C)[:, None], t[None, :]
        m = (r // (2 * b) == q // (2 * b)) & (r // b > q // b)
        lv += [m, (r // (2 * b) == q // (2 * b)) & (r // b < q // b)]
    return out, np.stack(lv, 1).astype(np.uint32)


def _rope(past):
    pos = np.concatenate([np.arange(T), np.full(NS, past)]).astype(np.float32)
    half = HD // 2
    inv = (10000.0 ** (-np.arange(half) / half)).astype(np.float32)
    ang = (pos[:, None] * inv[None, :]).astype(np.float32)
    cos, sin = np.cos(ang.astype(np.float64)).T, np.sin(ang.astype(np.float64)).T
    d = np.arange(P)
    sign = np.where(d % HD < half, -1.0, 1.0)[:, None]
    return np.stack([cos[d % half], sin[d % half] * sign], 1).astype(np.float32)


def _features(a):
    a = np.asarray(a)
    return np.moveaxis(a.reshape(a.shape[:-1] + (-1, P)), -1, 0)


def _tiles(w):
    k, n = w.shape[0] // P, w.shape[1] // P
    return np.ascontiguousarray(w.reshape(k, P, n, P).transpose(2, 1, 0, 3)).reshape(n, P, k * P)


def host_arrays(v):
    v = {k: np.asarray(a) for k, a in v.items()}
    a = {}
    x = np.concatenate([v["x_prompt"][0], v["x_sample"][:, 0]], 0)
    a["xT"] = np.ascontiguousarray(_features(x).transpose(0, 2, 1))
    c = np.concatenate([v["c_prompt"], v["c_sample"]], 0)
    a["cT"] = np.ascontiguousarray(_features(c).transpose(0, 2, 1))
    a["ada"] = np.ascontiguousarray(v["w_ada"][0].reshape(4, 2, P, 12, 512).transpose(3, 0, 2, 1, 4)).reshape(48, P, D)
    pair = np.concatenate([np.r_[j * HD:(j + 1) * HD, (4 + j) * HD:(5 + j) * HD] for j in range(4)])
    q0 = RC * P
    cols = np.concatenate([np.arange(q0), q0 + pair, np.arange(q0 + RW, PC * P)])
    a["w_in"] = _tiles(v["w_in"][0][:, cols])
    rows = np.concatenate([np.arange(RW), RW + pair])
    a["w_out"] = _tiles(v["w_out"][0][rows])
    a["up"] = _tiles(v["ffn_w_up"][0])
    a["down"] = np.ascontiguousarray(v["ffn_w_down"][0].reshape(FC, P, D))
    a["consts"], a["levels"] = _consts()
    a["rope"] = _rope(8192)
    pars = []
    for name, width in PARAMS:
        if name == "sinks":
            p = np.broadcast_to(v["swa_sinks"][0][None, :], (P, 8))
        elif name == "sink_rows":
            p = np.tile(v["swa_sinks"][0], 16)[:, None]
        elif name == "rwkv_r_k":
            p = _features(v[name].reshape(-1))
        elif name == "b_ada":
            p = _features(v[name][0])
        else:
            p = _features(v[name].reshape(-1))
        pars.append(p.reshape(P, width))
    a["params"] = np.ascontiguousarray(np.concatenate(pars, 1))
    a["shift_st"] = np.ascontiguousarray(_features(v["state_rwkv_shift"][0]).transpose(0, 2, 1))
    a["conv_st"] = np.ascontiguousarray(_features(v["state_ffn_conv"][0]).transpose(0, 2, 3, 1))
    a["lora"] = np.concatenate([v["rwkv_w_up"][0], v["rwkv_a_up"][0]], 0)
    a["g_up"] = np.ascontiguousarray(v["rwkv_g_up"][0])
    w = v["state_rwkv_wkv"][0].reshape(NS, 8, 2, 32, HD)
    a["wkv"] = np.ascontiguousarray(w.transpose(2, 0, 1, 3, 4)).reshape(P, 32 * HD)
    a["cache_k"] = np.ascontiguousarray(v["cache_swa_k"][0]).reshape(NS, P, P)
    a["cache_v"] = np.ascontiguousarray(v["cache_swa_v"][0]).reshape(NS, P, P)
    return a


OUTPUTS = [("o_y", [P, KD, N]), ("o_shift", [P, RC, NS + 1]), ("o_ks", [NS, P, P]), ("o_vs", [NS, P, P]),
           ("o_kvp", [P, 2, P]), ("o_wkvs", [P, 32, HD]), ("o_wkvp", [P, NJ, HD]), ("o_tail", [P, 2 * FC, NS + 2]),
           ("o_prev", [P, 2 * FC, NS])]


def unpack(r):
    y = np.ascontiguousarray(r["o_y"].transpose(2, 1, 0)).reshape(N, D)
    shift = np.ascontiguousarray(r["o_shift"].transpose(2, 1, 0)).reshape(NS + 1, RC * P)
    kvp = r["o_kvp"].transpose(1, 2, 0).reshape(2, 1, 1, P, 2, HD)
    wkvp = r["o_wkvp"].reshape(2, HD, NJ, HD).transpose(2, 0, 3, 1).reshape(1, 1, 2 * NJ, HD, HD)
    wkvs = r["o_wkvs"].reshape(2, NS, 8, 32, HD).transpose(1, 2, 0, 3, 4).reshape(1, NS, 8, HD, HD)
    tail = np.ascontiguousarray(r["o_tail"].transpose(2, 1, 0)).reshape(NS + 2, 2 * FF)
    prev = np.ascontiguousarray(r["o_prev"].transpose(2, 1, 0)).reshape(NS, 2 * FF)
    convs = np.stack([prev, tail[2:]], 1)[None]
    got = (y[None, :T], y[T:, None], wkvp, shift[:1][None], kvp[0], kvp[1], tail[None, None, :2], wkvs,
           shift[1:][None], r["o_ks"].reshape(1, NS, P, 2, HD), r["o_vs"].reshape(1, NS, P, 2, HD), convs)
    return tuple(np.ascontiguousarray(a) for a in got)


def kernel(**inputs):
    import concourse.bacc as bacc
    from concourse.bass_utils import run_bass_kernel_spmd

    nc = bacc.Bacc("TRN2", target_bir_lowering=False, num_devices=1)
    arrays = host_arrays(inputs)
    io = {n: nc.dram_tensor(n, a.shape, mybir.dt.from_np(a.dtype), kind="ExternalInput").ap()
          for n, a in arrays.items()}
    for n, shape in OUTPUTS:
        io[n] = nc.dram_tensor(n, shape, F32, kind="ExternalOutput").ap()
    build_program(nc, io)
    r = run_bass_kernel_spmd(nc, [arrays], core_ids=[0])
    return unpack(r.results[0])
```
